# Optimizing a Trainium2 kernel written in Bass

```python
import jax
import jax.numpy as jnp
from jax import lax
import numpy as np

D_MODEL = 1024
BATCH = 1
SEQ = 256
DEPTH = 2

ML_HEADS = 4
ML_DIM = 128
ML_WIDTH = ML_HEADS * ML_DIM
ML_CHUNK = 64
CONV_W = 4
AT_HEADS = 8
AT_KV_HEADS = 2
AT_DIM = 64
AT_WIDTH = AT_HEADS * AT_DIM
KV_WIDTH = AT_KV_HEADS * AT_DIM
IDX_HEADS = 4
IDX_DIM = 64
TOPK_MAX = 256
Q_BLOCK = 128
ROPE_THETA = 500000.0
D_FF_DENSE = 2816
N_EXPERTS = 8
TOP_K_EXPERTS = 2
D_FF_EXPERT = 3584
ALPHA = (2 * DEPTH) ** 0.25
BETA = (8 * DEPTH) ** -0.25
LN_EPS = 1e-5
N_DENSE = (DEPTH + 1) // 2
N_MOE = DEPTH // 2
PROJ_SIZES = (ML_WIDTH, ML_WIDTH, ML_WIDTH, ML_WIDTH, ML_HEADS, ML_HEADS,
              AT_WIDTH, KV_WIDTH, KV_WIDTH, IDX_HEADS * IDX_DIM, IDX_DIM, IDX_HEADS)
D_IN_PROJ = sum(PROJ_SIZES)

kernel_name = "hybrid_mlstm_dsa_moe_deepnorm"

def layer_norm(x, g, b):
    xf = x.astype(jnp.float32)
    mu = jnp.mean(xf, -1, keepdims=True)
    var = jnp.mean(jnp.square(xf - mu), -1, keepdims=True)
    y = (xf - mu) * lax.rsqrt(var + LN_EPS) * g.astype(jnp.float32) + b.astype(jnp.float32)
    return y.astype(x.dtype)

def head_norm(h, g):
    mu = jnp.mean(h, -1, keepdims=True)
    var = jnp.mean(jnp.square(h - mu), -1, keepdims=True)
    return (h - mu) * lax.rsqrt(var + LN_EPS) * g.astype(jnp.float32)

def partial_rope(x, pos):
    rot = x.shape[-1] // 4
    half = rot // 2
    inv = ROPE_THETA ** (-jnp.arange(half, dtype=jnp.float32) / half)
    ang = pos.astype(jnp.float32)[:, None] * inv[None, :]
    cos = jnp.cos(ang)[:, None, :]
    sin = jnp.sin(ang)[:, None, :]
    xf = x.astype(jnp.float32)
    x1 = xf[..., :half]
    x2 = xf[..., half:rot]
    out = jnp.concatenate([x1 * cos - x2 * sin, x2 * cos + x1 * sin, xf[..., rot:]], -1)
    return out.astype(x.dtype)

def causal_conv(x, w, b):
    s = x.shape[1]
    xp = jnp.pad(x, ((0, 0), (CONV_W - 1, 0), (0, 0)))
    y = xp[:, 0:s] * w[0]
    for j in range(1, CONV_W):
        y = y + xp[:, j:j + s] * w[j]
    return y + b

def mlstm_chunkwise(q, k, v, i_pre, f_pre):
    bsz, s, nh, d = q.shape
    nc = s // ML_CHUNK

    def chunks(a):
        a = a.astype(jnp.float32).reshape((bsz, nc, ML_CHUNK) + a.shape[2:])
        return jnp.moveaxis(jnp.moveaxis(a, 1, 0), 3, 2)

    qc = chunks(q) * (d ** -0.5)
    kc = chunks(k)
    vc = chunks(v)
    lf = jax.nn.log_sigmoid(chunks(f_pre))
    li = chunks(i_pre)
    bcum = jnp.cumsum(lf, axis=-1)
    causal = jnp.tril(jnp.ones((ML_CHUNK, ML_CHUNK), dtype=bool))

    def step(carry, inp):
        c_st, n_st, m_st = carry
        qj, kj, vj, bj, lij = inp
        dmat = bj[..., :, None] - bj[..., None, :] + lij[..., None, :]
        dmat = jnp.where(causal, dmat, -jnp.inf)
        g_inter = bj + m_st[..., None]
        m_t = jnp.maximum(g_inter, jnp.max(dmat, -1))
        w_inter = jnp.exp(g_inter - m_t)
        sc = jnp.einsum("bhtd,bhsd->bhts", qj, kj) * jnp.exp(dmat - m_t[..., None])
        num = w_inter[..., None] * jnp.einsum("bhtd,bhde->bhte", qj, c_st) + jnp.einsum("bhts,bhse->bhte", sc, vj)
        den = w_inter * jnp.einsum("bhtd,bhd->bht", qj, n_st) + jnp.sum(sc, -1)
        h = num / jnp.maximum(jnp.abs(den), jnp.exp(-m_t))[..., None]
        b_last = bj[..., -1]
        g_state = b_last + m_st
        ls = b_last[..., None] - bj + lij
        m_new = jnp.maximum(g_state, jnp.max(ls, -1))
        ws = jnp.exp(ls - m_new[..., None])
        decay = jnp.exp(g_state - m_new)
        c_new = decay[..., None, None] * c_st + jnp.einsum("bhs,bhsd,bhse->bhde", ws, kj, vj)
        n_new = decay[..., None] * n_st + jnp.einsum("bhs,bhsd->bhd", ws, kj)
        return (c_new, n_new, m_new), h

    init = (jnp.zeros((bsz, nh, d, d), jnp.float32),
            jnp.zeros((bsz, nh, d), jnp.float32),
            jnp.zeros((bsz, nh), jnp.float32))
    _, h = lax.scan(step, init, (qc, kc, vc, bcum, li))
    return jnp.transpose(h, (1, 0, 3, 2, 4)).reshape(bsz, s, nh, d)

def dsa_attention(q, k, v, qi, ki, wi):
    bsz, s = q.shape[0], q.shape[1]
    topk = min(TOPK_MAX, s // 4)
    nb = s // Q_BLOCK
    rep = AT_HEADS // AT_KV_HEADS
    key_pos = jnp.arange(s)
    kif = ki.astype(jnp.float32)

    def block(j):
        t0 = j * Q_BLOCK
        qb = lax.dynamic_slice_in_dim(q, t0, Q_BLOCK, axis=1)
        qib = lax.dynamic_slice_in_dim(qi, t0, Q_BLOCK, axis=1).astype(jnp.float32)
        wib = lax.dynamic_slice_in_dim(wi, t0, Q_BLOCK, axis=1).astype(jnp.float32) * (IDX_HEADS ** -0.5)
        tpos = t0 + jnp.arange(Q_BLOCK)
        sc = jax.nn.relu(jnp.einsum("bthd,bsd->bths", qib, kif) * (IDX_DIM ** -0.5))
        iscore = jnp.einsum("bth,bths->bts", wib, sc)
        allowed = key_pos[None, :] <= tpos[:, None]
        iscore = jnp.where(allowed[None], iscore, -jnp.inf)
        _, idx = lax.top_k(iscore, topk)
        valid = idx <= tpos[None, :, None]
        kg = jax.vmap(lambda kb, ib: kb[ib])(k, idx).astype(jnp.float32)
        vg = jax.vmap(lambda vb, ib: vb[ib])(v, idx).astype(jnp.float32)
        qg = qb.astype(jnp.float32).reshape(bsz, Q_BLOCK, AT_KV_HEADS, rep, AT_DIM)
        logits = jnp.einsum("btgrd,btkgd->btgrk", qg, kg) * (AT_DIM ** -0.5)
        logits = jnp.where(valid[:, :, None, None, :], logits, -jnp.inf)
        p = jax.nn.softmax(logits, axis=-1)
        o = jnp.einsum("btgrk,btkgd->btgrd", p, vg)
        return o.reshape(bsz, Q_BLOCK, AT_WIDTH).astype(q.dtype)

    out = lax.map(block, jnp.arange(nb))
    return jnp.transpose(out, (1, 0, 2, 3)).reshape(bsz, s, AT_WIDTH)

def swiglu(x, wg, wu, wd):
    return (jax.nn.silu(x @ wg) * (x @ wu)) @ wd

def moe_ffn(x, w_router, b_router, w_gate, w_up, w_down):
    bsz, s, dm = x.shape
    xt = x.reshape(-1, dm)
    logits = xt.astype(jnp.float32) @ w_router.astype(jnp.float32) + b_router.astype(jnp.float32)
    top_val, top_idx = lax.top_k(logits, TOP_K_EXPERTS)
    gates = jax.nn.softmax(top_val, axis=-1)
    combine = jnp.sum(jax.nn.one_hot(top_idx, N_EXPERTS, dtype=jnp.float32) * gates[..., None], axis=1)
    y = jnp.zeros((xt.shape[0], dm), jnp.float32)
    for e in range(N_EXPERTS):
        y = y + combine[:, e:e + 1] * swiglu(xt, w_gate[e], w_up[e], w_down[e]).astype(jnp.float32)
    return y.reshape(bsz, s, dm).astype(x.dtype)

def setup_inputs(seed: int = 0) -> dict:
    key = jax.random.key(seed)
    ks = jax.random.split(key, 24)

    def nrm(k, shape, scale):
        return jax.random.normal(k, shape, jnp.float32) * scale

    return {
        "x": nrm(ks[0], (BATCH, SEQ, D_MODEL), 1.0),
        "w_in": nrm(ks[1], (DEPTH, D_MODEL, D_IN_PROJ), D_MODEL ** -0.5),
        "ml_conv_w": nrm(ks[2], (DEPTH, CONV_W, 2 * ML_WIDTH), CONV_W ** -0.5),
        "ml_conv_b": nrm(ks[3], (DEPTH, 2 * ML_WIDTH), 0.02),
        "ml_i_b": nrm(ks[4], (DEPTH, ML_HEADS), 0.1),
        "ml_f_b": 3.0 + jnp.linspace(0.0, 3.0, ML_HEADS, dtype=jnp.float32)[None, :] + nrm(ks[5], (DEPTH, ML_HEADS), 0.1),
        "ml_norm_g": 1.0 + nrm(ks[6], (DEPTH, ML_WIDTH), 0.02),
        "idx_k_norm_g": 1.0 + nrm(ks[7], (DEPTH, IDX_DIM), 0.02),
        "idx_k_norm_b": nrm(ks[8], (DEPTH, IDX_DIM), 0.02),
        "w_out": nrm(ks[9], (DEPTH, D_MODEL, D_MODEL), BETA * D_MODEL ** -0.5),
        "ln1_g": 1.0 + nrm(ks[10], (DEPTH, D_MODEL), 0.02),
        "ln1_b": nrm(ks[11], (DEPTH, D_MODEL), 0.02),
        "ln2_g": 1.0 + nrm(ks[12], (DEPTH, D_MODEL), 0.02),
        "ln2_b": nrm(ks[13], (DEPTH, D_MODEL), 0.02),
        "ffn_w_gate": nrm(ks[14], (N_DENSE, D_MODEL, D_FF_DENSE), D_MODEL ** -0.5),
        "ffn_w_up": nrm(ks[15], (N_DENSE, D_MODEL, D_FF_DENSE), D_MODEL ** -0.5),
        "ffn_w_down": nrm(ks[16], (N_DENSE, D_FF_DENSE, D_MODEL), BETA * D_FF_DENSE ** -0.5),
        "moe_w_router": nrm(ks[17], (N_MOE, D_MODEL, N_EXPERTS), D_MODEL ** -0.5),
        "moe_b_router": nrm(ks[18], (N_MOE, N_EXPERTS), 0.01),
        "moe_w_gate": nrm(ks[19], (N_MOE, N_EXPERTS, D_MODEL, D_FF_EXPERT), D_MODEL ** -0.5),
        "moe_w_up": nrm(ks[20], (N_MOE, N_EXPERTS, D_MODEL, D_FF_EXPERT), D_MODEL ** -0.5),
        "moe_w_down": nrm(ks[21], (N_MOE, N_EXPERTS, D_FF_EXPERT, D_MODEL), BETA * D_FF_EXPERT ** -0.5),
    }

def reference(x, w_in, ml_conv_w, ml_conv_b, ml_i_b, ml_f_b, ml_norm_g, idx_k_norm_g, idx_k_norm_b,
              w_out, ln1_g, ln1_b, ln2_g, ln2_b, ffn_w_gate, ffn_w_up, ffn_w_down,
              moe_w_router, moe_b_router, moe_w_gate, moe_w_up, moe_w_down):
    bsz, s, _ = x.shape
    pos = jnp.arange(s)
    split_at = np.cumsum(np.array(PROJ_SIZES))[:-1].tolist()
    for l in range(DEPTH):
        proj = x @ w_in[l]
        mq, mk, mv, mo, mi, mf, aq, ak, av, iq, ik, iw = jnp.split(proj, split_at, axis=-1)

        qk = jax.nn.silu(causal_conv(jnp.concatenate([mq, mk], -1), ml_conv_w[l], ml_conv_b[l]))
        mq_c, mk_c = jnp.split(qk, 2, axis=-1)
        hm = mlstm_chunkwise(mq_c.reshape(bsz, s, ML_HEADS, ML_DIM),
                             mk_c.reshape(bsz, s, ML_HEADS, ML_DIM),
                             mv.reshape(bsz, s, ML_HEADS, ML_DIM),
                             mi + ml_i_b[l], mf + ml_f_b[l])
        hm = head_norm(hm, ml_norm_g[l].reshape(ML_HEADS, ML_DIM)).reshape(bsz, s, ML_WIDTH)
        ml_out = (jax.nn.sigmoid(mo.astype(jnp.float32)) * hm).astype(x.dtype)

        aq_r = partial_rope(aq.reshape(bsz, s, AT_HEADS, AT_DIM), pos)
        ak_r = partial_rope(ak.reshape(bsz, s, AT_KV_HEADS, AT_DIM), pos)
        av_h = av.reshape(bsz, s, AT_KV_HEADS, AT_DIM)
        iq_r = partial_rope(iq.reshape(bsz, s, IDX_HEADS, IDX_DIM), pos)
        ik_r = partial_rope(layer_norm(ik, idx_k_norm_g[l], idx_k_norm_b[l])[:, :, None, :], pos)[:, :, 0, :]
        at_out = dsa_attention(aq_r, ak_r, av_h, iq_r, ik_r, iw)

        mix = jnp.concatenate([ml_out, at_out], -1) @ w_out[l]
        x = layer_norm(ALPHA * x + mix, ln1_g[l], ln1_b[l])

        if l % 2 == 0:
            j = l // 2
            ffn = swiglu(x, ffn_w_gate[j], ffn_w_up[j], ffn_w_down[j])
        else:
            j = l // 2
            ffn = moe_ffn(x, moe_w_router[j], moe_b_router[j], moe_w_gate[j], moe_w_up[j], moe_w_down[j])
        x = layer_norm(ALPHA * x + ffn, ln2_g[l], ln2_b[l])
    return x


_drawn_inputs = setup_inputs


def setup_inputs(seed=0):
    import zlib

    import numpy as np

    out = dict(_drawn_inputs(seed))
    spreads = {}
    factors = {'ml_conv_b': 7.637,
     'ml_i_b': 49.613,
     'ml_norm_g': 6.923,
     'idx_k_norm_g': 28.959,
     'idx_k_norm_b': 51.626,
     'moe_b_router': 13.079}
    for name, (base, spread) in spreads.items():
        noise = np.random.default_rng([zlib.crc32(name.encode()), seed]).standard_normal(out[name].shape)
        drawn = base * np.exp(spread * noise) if base else spread * noise
        out[name] = jnp.asarray(drawn.astype(out[name].dtype))
    for name, factor in factors.items():
        out[name] = (out[name] * factor).astype(out[name].dtype)
    return out
```

```python
from contextlib import ExitStack

import numpy as np

import concourse.bass as bass
from concourse import mybir

F32 = mybir.dt.float32
I32 = mybir.dt.int32
U32 = mybir.dt.uint32
ALU = mybir.AluOpType
ACT = mybir.ActivationFunctionType
AX = mybir.AxisListType

P = 128
SEQ, D = 256, 1024
T = SEQ // P
KT = D // P
DEPTH = 2
ML_H, ML_D = 4, 128
ML_W = ML_H * ML_D
CONV = 4
AT_H, AT_KV, AT_D = 8, 2, 64
IDX_H = 4
TOPK = min(256, SEQ // 4)
FF_DENSE, FF_EXPERT, NEXP = 2816, 3584, 8
ALPHA = (2 * DEPTH) ** 0.25
LN_EPS = 1e-5
ROPE_THETA = 500000.0
ROT = AT_D // 4 // 2

C_MQ, C_MK, C_MV, C_MO = 0, ML_W, 2 * ML_W, 3 * ML_W
C_GATE = 4 * ML_W
C_END = C_GATE + 2 * ML_H + AT_H * AT_D + 2 * AT_KV * AT_D + (IDX_H + 1) * AT_D + IDX_H
AW = C_END - C_GATE
A_Q = 2 * ML_H
A_K = A_Q + AT_H * AT_D
A_V = A_K + AT_KV * AT_D
A_IQ = A_V + AT_KV * AT_D
A_IK = A_IQ + IDX_H * AT_D
A_IW = A_IK + AT_D

NSLOT = 6
SLOT = 4096
CH = 512
NEG = -1.0e30
TAKEN = -3.0e38

K_ID, K_CAUSAL, K_CAUSALT, K_IOTA, K_TRIU, K_ONES = 0, 128, 512, 896, 1024, 1152
K_SEL, K_COS, K_SIN, K_EPS = 1408, 1920, 1936, 1952
K_END = 1953


def shape_constants():
    t = np.zeros((P, K_END), np.float32)
    p = np.arange(P)[:, None]
    f = np.arange(P)[None, :]
    t[:, K_ID:K_ID + P] = p == f
    diag = np.where(f <= p, 0.0, NEG)
    t[:, K_CAUSAL:K_CAUSAL + P] = diag
    t[:, K_CAUSAL + 2 * P:K_CAUSAL + 3 * P] = diag
    t[:, K_CAUSALT:K_CAUSALT + P] = diag.T
    t[:, K_CAUSALT + 2 * P:K_CAUSALT + 3 * P] = diag.T
    t[:, K_IOTA:K_IOTA + P] = f
    t[:, K_TRIU:K_TRIU + P] = p < f
    t[:, K_ONES:K_ONES + SEQ] = 1.0
    for h in range(ML_H):
        t[h, K_SEL + h * P:K_SEL + (h + 1) * P] = 1.0
    inv = np.float32(ROPE_THETA) ** (-np.arange(ROT, dtype=np.float32) / np.float32(ROT))
    ang = np.arange(SEQ, dtype=np.float32)[:, None] * inv[None, :]
    t[:, K_COS:K_COS + T * ROT] = np.cos(ang).reshape(T, P, ROT).transpose(1, 0, 2).reshape(P, T * ROT)
    t[:, K_SIN:K_SIN + T * ROT] = np.sin(ang).reshape(T, P, ROT).transpose(1, 0, 2).reshape(P, T * ROT)
    t[:, K_EPS] = LN_EPS
    return t


PC_W, PC_B, PC_I, PC_F, PC_END = 0, 2 * ML_H * CONV, 2 * ML_H * CONV + 2 * ML_H, 2 * ML_H * CONV + 2 * ML_H + 1, 42
AR_NG, AR_IG, AR_IB, AR_END = 0, ML_W, ML_W + AT_D, ML_W + 2 * AT_D


def build_program(nc, x, w_in, w_out, ffn_gate, ffn_up, ffn_down, w_router, b_router, moe_gate, moe_up, moe_down,
                  feat_params, row_params, ln_params, consts, out):
    with ExitStack() as ctx:
        def sb(name, shape, dt=F32):
            return ctx.enter_context(nc.sbuf_tensor(name, shape, dt))

        def sem(name):
            return ctx.enter_context(nc.semaphore(name))

        def layer_sem(name):
            return [sem(f"{name}_{l}") for l in range(DEPTH)]

        x_tok = sb("x_tok", [P, T, D])
        xT = sb("xT", [P, KT, SEQ])
        cst = sb("cst", [P, K_END])
        feat = sb("feat", [P, DEPTH, PC_END])
        rows = sb("rows", [P, DEPTH, AR_END])
        ln = sb("ln", [P, 4, D])
        ring = sb("ring", [P, NSLOT, SLOT])
        WORK = 16000
        work = sb("work", [P, WORK])
        used = [0, 0]

        def carve(phase, size):
            a = used[phase]
            used[phase] += size
            assert used[phase] <= WORK, (phase, used[phase])
            return work[:, a:a + size]

        pre_mem = carve(0, 2 * ML_H * (SEQ + CONV - 1))
        pre = pre_mem.rearrange("p (f s) -> p f s", f=2 * ML_H)
        mixT = pre_mem[:, 0:KT * SEQ].rearrange("p (k s) -> p k s", k=KT)
        og = pre_mem[:, 0:T * ML_W].rearrange("p (t n) -> p t n", t=T)
        qk_mem = carve(0, 2 * ML_H * SEQ)
        qk = qk_mem.rearrange("p (f s) -> p f s", f=2 * ML_H)
        mix = qk_mem.rearrange("p (t n) -> p t n", t=T)
        v_aug = carve(0, T * ML_H * (ML_D + 1)).rearrange("p (t h n) -> p t h n", t=T, h=ML_H)
        att = carve(0, T * AW).rearrange("p (t n) -> p t n", t=T)
        iqT = carve(0, 2 * SEQ).rearrange("p (f s) -> p f s", f=2)
        ikT = carve(0, SEQ)
        aqT = carve(0, 4 * SEQ).rearrange("p (f s) -> p f s", f=4)
        akT = carve(0, AT_KV * SEQ).rearrange("p (g s) -> p g s", g=AT_KV)
        shared = carve(0, 4 * 384 + 4 * SEQ)
        relu = shared[:, 0:IDX_H * 384].rearrange("p (h s) -> p h s", h=IDX_H)
        gate = shared[:, 4 * 384:].rearrange("p (r s) -> p r s", r=4)
        probs = shared[:, 0:3 * 384].rearrange("p (b s) -> p b s", b=3)
        probsT = shared[:, 3 * 384:6 * 384].rearrange("p (b s) -> p b s", b=3)
        iscore = carve(0, 384)
        left = carve(0, 384)
        choice = carve(0, 384)
        mld_mem = carve(0, ML_H * 384)
        mld = mld_mem.rearrange("p (h s) -> p h s", h=ML_H)
        kdup = carve(0, T * 2 * AT_KV * AT_D).rearrange("p (t g c n) -> p t g c n", t=T, g=AT_KV, c=2)
        ikdup = carve(0, T * 2 * AT_D).rearrange("p (t c n) -> p t c n", t=T, c=2)
        rope = [mld_mem[:, i * T * 10 * ROT:(i + 1) * T * 10 * ROT].rearrange("p (t h r) -> p t h r", t=T, h=10)
                for i in range(4)]
        top8 = carve(0, T * 8).rearrange("p (t n) -> p t n", t=T)
        gT = carve(0, T * ML_H).rearrange("p (t h) -> p t h", t=T)
        emT = carve(0, T * ML_H).rearrange("p (t h) -> p t h", t=T)
        rden = carve(0, T * ML_H).rearrange("p (t h) -> p t h", t=T)
        rden2 = carve(0, T * ML_H).rearrange("p (t h) -> p t h", t=T)
        rsum = carve(0, T * AT_H).rearrange("p (t h) -> p t h", t=T)
        rmax = carve(0, 3 * T).rearrange("p (b t) -> p b t", b=3)
        nmax = carve(0, 3 * T).rearrange("p (b t) -> p b t", b=3)
        y = carve(1, T * D).rearrange("p (t n) -> p t n", t=T)
        silu = carve(1, 2 * CH).rearrange("p (b n) -> p b n", b=2)
        hid = carve(1, 2 * CH).rearrange("p (b n) -> p b n", b=2)
        hidT = carve(1, 2 * CH).rearrange("p (b j n) -> p b j n", b=2, j=CH // P)
        xg = carve(1, KT * P).rearrange("p (k n) -> p k n", k=KT)
        sel = carve(1, T * P).rearrange("p (t n) -> p t n", t=T)
        selc = carve(1, T * P).rearrange("p (t n) -> p t n", t=T)
        selT = carve(1, T * P).rearrange("p (t n) -> p t n", t=T)
        eo = carve(1, D)
        stats = sb("stats", [P, 8, 2, 6])
        mv = sb("mv", [P, 8, 2])
        var = sb("var", [P, 8])
        rs = sb("rs", [P, 8])
        nt = sb("nt", [P, 2, 8])
        wr = sb("wr", [P, KT, NEXP])
        br = sb("br", [P, NEXP])
        lg = sb("lg", [P, T, NEXP])
        m8 = sb("m8", [P, T, 8])
        i8 = sb("i8", [P, T, 8], U32)
        i8f = sb("i8f", [P, T, 2])
        oh = sb("oh", [P, T, 2, NEXP])
        g2 = sb("g2", [P, T, 3])
        comb = sb("comb", [P, T, NEXP])
        routed = sb("routed", [P, T, NEXP])
        rank = sb("rank", [P, T, NEXP])
        cnt = sb("cnt", [P, NEXP])
        cmax = sb("cmax", [P, 1])
        more = sb("more", [P, 1], I32)

        bank = [ctx.enter_context(nc.psum_tensor(f"bank{i}", [P, CH], F32)) for i in range(8)]

        ident = cst[:, K_ID:K_ID + P]
        causal = cst[:, K_CAUSAL:K_CAUSAL + 384]
        causalT = cst[:, K_CAUSALT:K_CAUSALT + 384]
        iota = cst[:, K_IOTA:K_IOTA + P]
        triu = cst[:, K_TRIU:K_TRIU + P]
        ones = cst[:, K_ONES:K_ONES + SEQ]
        eps = cst[:, K_EPS:K_EPS + 1]
        one = cst[:, K_ONES:K_ONES + 1]

        in_x, in_const, in_rows, in_ln = sem("in_x"), sem("in_const"), sem("in_rows"), sem("in_ln")
        stored = sem("stored")
        slot_full = [sem(f"slot_full{i}") for i in range(NSLOT)]
        dstep = sem("dstep")
        xt_mm, xt_ready = sem("xt_mm"), sem("xt_ready")
        x_ready = sem("x_ready")
        proj_mm, proj_ev = layer_sem("proj_mm"), layer_sem("proj_ev")
        gate_mm, gate_ev = layer_sem("gate_mm"), layer_sem("gate_ev")
        qk_mm, qk_ev = layer_sem("qk_mm"), layer_sem("qk_ev")
        conv_y, conv_ok = layer_sem("conv_y"), layer_sem("conv_ok")
        var_ok, ln_v, rs_ok = layer_sem("var_ok"), layer_sem("ln_v"), layer_sem("rs_ok")
        roped, dup_ok = layer_sem("roped"), layer_sem("dup_ok")
        itr_mm, itr_ev = layer_sem("itr_mm"), layer_sem("itr_ev")
        idx_mm, idx_ev = layer_sem("idx_mm"), layer_sem("idx_ev")
        atr_mm, atr_ev = layer_sem("atr_mm"), layer_sem("atr_ev")
        gate_row, gtr_mm, gtr_ev = layer_sem("gate_row"), layer_sem("gtr_mm"), layer_sem("gtr_ev")
        vo_mm, v_ev, o_ev = layer_sem("vo_mm"), layer_sem("v_ev"), layer_sem("o_ev")
        mrow_mm, mls_mm, ml_e, ml_d, ml_p, num_mm, mix_ml = (
            layer_sem(n) for n in ("mrow_mm", "mls_mm", "ml_e", "ml_d", "ml_p", "num_mm", "mix_ml"))
        sc_mm, sc_max, sc_exp, ptr_mm, pt_ok, pv_mm, mix_at = (
            layer_sem(n) for n in ("sc_mm", "sc_max", "sc_exp", "ptr_mm", "pt_ok", "pv_mm", "mix_at"))
        mtr_mm, mtr_ev, op_mm = layer_sem("mtr_mm"), layer_sem("mtr_ev"), layer_sem("op_mm")
        op_half = layer_sem("op_half")
        g_mm, g_silu, u_mm, h_ok, ht_mm, ht_ev, dn_mm = (
            sem(n) for n in ("g_mm", "g_silu", "u_mm", "h_ok", "ht_mm", "ht_ev", "dn_mm"))
        rt_mm, rt_diff, rt_exp, rt_mask, rk_mm, more_ok = (
            sem(n) for n in ("rt_mm", "rt_diff", "rt_exp", "rt_mask", "rk_mm", "more_ok"))
        rank_ok = sem("rank_ok")
        Y0, GA0, ST0 = T, 1, 1
        sel_ok, ga_mm, ga_ev, st_mm, st_ev, eo_lo, eo_hi, back_mm, y_add = (
            sem(n) for n in ("sel_ok", "ga_mm", "ga_ev", "st_mm", "st_ev", "eo_lo", "eo_hi", "back_mm", "y_add"))

        PROJ = [(C_GATE, C_GATE + CH), (C_GATE + CH, C_GATE + 2 * CH), (C_GATE + 2 * CH, C_END),
                (C_MQ, C_MK), (C_MK, C_MV), (C_MV, C_MO), (C_MO, C_GATE)]
        DENSE = [(c, min(CH, FF_DENSE - c)) for c in range(0, FF_DENSE, CH)]
        UNITS = FF_EXPERT // CH
        DENSE_UNITS = T * len(DENSE)
        stream, FIRST_IN, FIRST_OUT = [], [], []
        for l in range(DEPTH):
            FIRST_IN.append(len(stream))
            reads = [(gate_mm[l], 2), (proj_mm[l], 4), (proj_mm[l], 6), (qk_mm[l], 2), (qk_mm[l], 4),
                     (vo_mm[l], 2), (vo_mm[l], 4)]
            for (a, b), read in zip(PROJ, reads):
                stream.append((w_in[l, :, a:b].rearrange("(k p) n -> p k n", p=P), KT, b - a, read))
            FIRST_OUT.append(len(stream))
            for h, read in enumerate([(op_half[l], 1), (op_mm[l], 4)]):
                stream.append((w_out[l, h * CH:(h + 1) * CH, :].rearrange("(k p) n -> p k n", p=P), CH // P, D, read))
            if l == 0:
                FIRST_DENSE = len(stream)
                for c, (a, w) in enumerate(DENSE):
                    for m, done in ((ffn_gate, g_mm), (ffn_up, u_mm)):
                        stream.append((m[0, :, a:a + w].rearrange("(k p) n -> p k n", p=P), KT, w, (done, T * (c + 1))))
                    stream.append((ffn_down[0, a:a + w, :].rearrange("(p j) n -> p j n", p=P), w // P, D,
                                   (dn_mm, T * (c + 1))))
        N_STREAM = len(stream)
        assert N_STREAM % NSLOT == 0

        def slot_view(s, k, n):
            return ring[:, s, 0:k * n].rearrange("p (k n) -> p k n", k=k)

        def chunk_view(n):
            return slot_view(n % NSLOT, stream[n][1], stream[n][2])

        def wait_chunk(eng, n):
            eng.wait_ge(slot_full[n % NSLOT], 16 * (n // NSLOT + 1))

        TURN = 2
        TURNS = NEXP // TURN
        FILLS0 = N_STREAM // NSLOT
        FILLS = TURN * UNITS * 3 // NSLOT
        assert FILLS * NSLOT == TURN * UNITS * 3
        wg_v = moe_gate.rearrange("a e (k p) f -> p (a e) k f", p=P)
        wu_v = moe_up.rearrange("a e (k p) f -> p (a e) k f", p=P)
        wd_v = moe_down.rearrange("a e (c p j) n -> p (a e) c j n", p=P, j=CH // P)

        block = ctx.enter_context(nc.Block())

        @block.sync
        def _(sp):
            sp.dma_start(x_tok[:], x[0].rearrange("(t p) n -> p t n", p=P)).then_inc(in_x, 16)
            for n, (src, _, _, _) in enumerate(stream):
                if n >= NSLOT:
                    sp.wait_ge(*stream[n - NSLOT][3])
                sp.dma_start(chunk_view(n), src).then_inc(slot_full[n % NSLOT], 16)

            def turn(it, pair):
                for u in range(TURN * UNITS):
                    j, c = divmod(u, UNITS)
                    e = bass.ds(pair * TURN + j, 1)
                    for m, read in enumerate((g_mm, u_mm, dn_mm)):
                        s = (3 * u + m) % NSLOT
                        if isinstance(it, int) and it == 0 and u < 2:
                            sp.wait_ge(*stream[N_STREAM - NSLOT + s][3])
                        else:
                            sp.wait_ge(read, it * (TURN * UNITS) + (DENSE_UNITS + u - 1))
                        if m < 2:
                            src = (wg_v, wu_v)[m][:, e, :, c * CH:(c + 1) * CH]
                            dst = slot_view(s, KT, CH)
                        else:
                            src = wd_v[:, e, c]
                            dst = slot_view(s, CH // P, D)
                        sp.dma_start(dst, src.rearrange("p a k n -> p (a k) n")).then_inc(slot_full[s], 16)

            turn(0, 0)
            with sp.Fori(1, TURNS) as i:
                turn(i, i)
            sp.wait_ge(more_ok, 1)
            again = sp.value_load(more[0:1, 0:1], min_val=0, max_val=1)
            with sp.If(again > 0):
                with sp.Fori(0, TURNS) as i:
                    turn(i + TURNS, i)
            for t in range(T):
                sp.wait_ge(x_ready, 3 * T + t + 1)
                sp.dma_start(out[0, t * P:(t + 1) * P, :], x_tok[:, t, :]).then_inc(stored, 16)
            sp.wait_ge(stored, 16 * T)

        @block.gpsimd
        def _(pool):
            pool.dma_start(cst[:], consts).then_inc(in_const, 16)
            pool.dma_start(feat[:], feat_params.rearrange("l p n -> p l n")).then_inc(in_const, 16)
            pool.dma_start(rows[:], row_params.partition_broadcast(P)).then_inc(in_rows, 16)
            pool.dma_start(br[:], b_router.rearrange("a n -> (a n)").partition_broadcast(P)).then_inc(in_rows, 16)
            pool.dma_start(wr[:], w_router[0].rearrange("(k p) n -> p k n", p=P)).then_inc(in_rows, 16)
            for l in range(DEPTH):
                if l:
                    pool.wait_ge(x_ready, 2 * T)
                pool.dma_start(ln[:], ln_params[l].partition_broadcast(P)).then_inc(in_ln, 16)
                pool.wait_ge(roped[l], 1)
                for t in range(T):
                    pool.tensor_copy(ikdup[:, t], att[:, t, A_IK:A_IW].unsqueeze(1).to_broadcast([P, 2, AT_D])
                                     ).then_inc(dup_ok[l], 1)
                pool.wait_ge(roped[l], 2)
                for t in range(T):
                    k = att[:, t, A_K:A_V].rearrange("p (g n) -> p g n", g=AT_KV)
                    pool.tensor_copy(kdup[:, t], k.unsqueeze(2).to_broadcast([P, AT_KV, 2, AT_D])
                                     ).then_inc(dup_ok[l], 1)

        @block.tensor
        def _(pe):
            mm = nc.tensor.matmul
            tr = nc.tensor.transpose

            def x_transposes(stage):
                for t in range(T):
                    if stage:
                        pe.wait_ge(x_ready, (stage - 1) * T + t + 1)
                    elif t == 0:
                        pe.wait_ge(in_x, 16)
                        pe.wait_ge(in_const, 32)
                    for h in range(2):
                        for j in range(4):
                            k = 4 * h + j
                            i = tr(bank[4 + 2 * t + h][:, j * P:(j + 1) * P], x_tok[:, t, k * P:(k + 1) * P], ident)
                        i.then_inc(xt_mm, 1)

            def token_group(n, t, b):
                w = chunk_view(n)
                for k in range(KT):
                    i = mm(b[:, 0:w.shape[2]], xT[:, k, t * P:(t + 1) * P], w[:, k, :], start=k == 0, stop=k == KT - 1)
                return i

            def feature_pairs(l, n, first):
                wait_chunk(pe, n)
                w = chunk_view(n)
                for pair in range(2):
                    j = first + pair
                    if j >= 2:
                        pe.wait_ge(qk_ev[l], j - 1)
                    for f in range(2):
                        c = (2 * pair + f) * P
                        for k in range(KT):
                            i = mm(bank[5 + j % 2][:, f * SEQ:(f + 1) * SEQ], w[:, k, c:c + P], xT[:, k, :],
                                   start=k == 0, stop=k == KT - 1)
                    i.then_inc(qk_mm[l], 1)

            def attention(l):
                c0 = FIRST_IN[l]
                pe.wait_ge(xt_ready, 8 * l + 4)
                for c in range(3):
                    wait_chunk(pe, c0 + c)
                    for t in range(T):
                        g = 2 * c + t
                        if g >= 4:
                            pe.wait_ge(proj_ev[l], g - 3)
                        token_group(c0 + c, t, bank[g % 4]).then_inc(proj_mm[l], 1)
                    if c == 0:
                        for m in range(2):
                            for k in range(KT):
                                i = mm(bank[4][0:ML_H, m * SEQ:(m + 1) * SEQ],
                                       chunk_view(c0)[:, k, m * ML_H:(m + 1) * ML_H], xT[:, k, :],
                                       start=k == 0, stop=k == KT - 1)
                            i.then_inc(gate_mm[l], 1)
                feature_pairs(l, c0 + 3, 0)
                pe.wait_ge(proj_ev[l], 6)
                pe.wait_ge(roped[l], 1)
                for f in range(2):
                    for t in range(T):
                        i = tr(bank[0][:, f * SEQ + t * P:f * SEQ + (t + 1) * P],
                               att[:, t, A_IQ + f * P:A_IQ + (f + 1) * P], ident)
                i.then_inc(itr_mm[l], 1)
                pe.wait_ge(dup_ok[l], T)
                for t in range(T):
                    i = tr(bank[1][:, t * P:(t + 1) * P], ikdup[:, t].rearrange("p c n -> p (c n)"), ident)
                i.then_inc(itr_mm[l], 1)
                feature_pairs(l, c0 + 4, 2)
                pe.wait_ge(itr_ev[l], 2)
                for h in range(IDX_H):
                    a = AT_D * (h % 2)
                    for t in range(T):
                        o = (0, P)[t]
                        i = mm(bank[h][:, o:o + (t + 1) * P], iqT[a:a + AT_D, h // 2, t * P:(t + 1) * P],
                               ikT[a:a + AT_D, 0:(t + 1) * P], start=True, stop=True)
                    i.then_inc(idx_mm[l], 1)
                pe.wait_ge(dup_ok[l], 2 * T)
                pe.wait_ge(gate_ev[l], 2)
                pe.wait_ge(qk_ev[l], 4)
                for f in range(4):
                    for t in range(T):
                        i = tr(bank[4 + f // 2][:, (f % 2) * SEQ + t * P:(f % 2) * SEQ + (t + 1) * P],
                               att[:, t, A_Q + f * P:A_Q + (f + 1) * P], ident)
                    if f % 2:
                        i.then_inc(atr_mm[l], 1)
                for g in range(AT_KV):
                    for t in range(T):
                        i = tr(bank[6][:, g * SEQ + t * P:g * SEQ + (t + 1) * P],
                               kdup[:, t, g].rearrange("p c n -> p (c n)"), ident)
                i.then_inc(atr_mm[l], 1)
                pe.wait_ge(gate_row[l], 1)
                for m, r in enumerate((0, 2)):
                    for t in range(T):
                        i = tr(bank[7][:, (2 * m + t) * ML_H:(2 * m + t + 1) * ML_H],
                               gate[0:ML_H, r, t * P:(t + 1) * P], cst[0:ML_H, K_ID:K_ID + ML_H])
                i.then_inc(gtr_mm[l], 1)
                pe.wait_ge(idx_ev[l], IDX_H)
                for c in range(2):
                    wait_chunk(pe, c0 + 5 + c)
                    for t in range(T):
                        token_group(c0 + 5 + c, t, bank[2 * c + t]).then_inc(vo_mm[l], 1)
                pe.wait_ge(atr_ev[l], 3)
                for h in range(ML_H):
                    i = mm(bank[4 + h // 2][:, (h % 2) * SEQ:(h % 2 + 1) * SEQ],
                           cst[0:ML_H, K_SEL + h * P:K_SEL + (h + 1) * P], gate[0:ML_H, 1, :], start=True, stop=True)
                    if h % 2:
                        i.then_inc(mrow_mm[l], 1)
                pe.wait_ge(conv_ok[l], 2)
                pe.wait_ge(gtr_ev[l], 2)
                for h in range(ML_H):
                    if h >= 2:
                        pe.wait_ge(ml_p[l], h - 1)
                    mm(bank[6 + h % 2][:, 0:SEQ], qk[:, ML_H + h, 0:P], qk[:, h, :], start=True, stop=True)
                    mm(bank[6 + h % 2][:, SEQ:SEQ + P], qk[:, ML_H + h, P:SEQ], qk[:, h, P:SEQ],
                       start=True, stop=True).then_inc(mls_mm[l], 1)
                pe.wait_ge(v_ev[l], T)
                pe.wait_ge(o_ev[l], T)
                for h in range(ML_H):
                    pe.wait_ge(ml_p[l], h + 1)
                    a = (h % 2) * (ML_D + 1)
                    mm(bank[h // 2][:, a:a + ML_D + 1], mld[:, h, 0:P], v_aug[:, 0, h, :], start=True, stop=True)
                    o = bank[2 + h // 2][:, a:a + ML_D + 1]
                    mm(o, mld[:, h, P:2 * P], v_aug[:, 0, h, :], start=True, stop=False)
                    mm(o, mld[:, h, 2 * P:3 * P], v_aug[:, 1, h, :], start=False, stop=True).then_inc(num_mm[l], 1)

                def scores(h):
                    a = AT_D * (h % 2)
                    if h >= 4:
                        pe.wait_ge(sc_max[l], h - 3)
                    for t in range(T):
                        o = (0, P)[t]
                        i = mm(bank[4 + h % 4][:, o:o + (t + 1) * P], aqT[a:a + AT_D, h // 2, t * P:(t + 1) * P],
                               akT[a:a + AT_D, h // (AT_H // AT_KV), 0:(t + 1) * P], start=True, stop=True)
                    i.then_inc(sc_mm[l], 1)

                def prob_transposes(h):
                    pe.wait_ge(sc_exp[l], h + 1)
                    if h >= 2:
                        pe.wait_ge(pt_ok[l], h - 1)
                    for j in range(3):
                        i = tr(bank[2 + h % 2][:, j * P:(j + 1) * P], probs[:, h % 3, j * P:(j + 1) * P], ident)
                    i.then_inc(ptr_mm[l], 1)

                def values(h):
                    pe.wait_ge(pt_ok[l], h + 1)
                    v = A_V + AT_D * (h // (AT_H // AT_KV))
                    o = slice(h * AT_D, (h + 1) * AT_D)
                    pT = probsT[:, h % 3]
                    mm(bank[0][:, o], pT[:, 0:P], att[:, 0, v:v + AT_D], start=True, stop=True)
                    mm(bank[1][:, o], pT[:, P:2 * P], att[:, 0, v:v + AT_D], start=True, stop=False)
                    mm(bank[1][:, o], pT[:, 2 * P:3 * P], att[:, 1, v:v + AT_D], start=False, stop=True
                       ).then_inc(pv_mm[l], 1)

                pe.wait_ge(ml_p[l], ML_H)
                for h in range(AT_H + 2):
                    if h < AT_H:
                        scores(h)
                    if h == 1:
                        pe.wait_ge(mix_ml[l], 1)
                    if 1 <= h <= AT_H:
                        prob_transposes(h - 1)
                    if h >= 2:
                        values(h - 2)
                pe.wait_ge(mix_at[l], 1)
                for t in range(T):
                    for h in range(2):
                        for j in range(4):
                            k = 4 * h + j
                            i = tr(bank[4 + 2 * t + h][:, j * P:(j + 1) * P], mix[:, t, k * P:(k + 1) * P], ident)
                        i.then_inc(mtr_mm[l], 1)
                pe.wait_ge(mtr_ev[l], 4)
                for half in range(2):
                    n = FIRST_OUT[l] + half
                    wait_chunk(pe, n)
                    for g in range(4):
                        t, c = divmod(g, 2)
                        for j in range(4):
                            k = 4 * half + j
                            i = mm(bank[g][:, :], mixT[:, k, t * P:(t + 1) * P],
                                   chunk_view(n)[:, j, c * CH:(c + 1) * CH], start=k == 0, stop=k == KT - 1)
                        if half:
                            i.then_inc(op_mm[l], 1)
                    if not half:
                        i.then_inc(op_half[l], 1)
                x_transposes(2 * l + 1)

            def hidden_transposes(u, w):
                k, base = u
                b = bank[2 + k % 2]
                pe.wait_ge(h_ok, base + (k + 1))
                h = hid[:, k % 2, 0:w].rearrange("p (f j) -> p j f", j=w // P)
                for j in range(w // P):
                    i = tr(b[:, j * P:(j + 1) * P], h[:, j, :], ident)
                i.then_inc(ht_mm, 1)

            def dense():
                units = [(c, t) for c in range(len(DENSE)) for t in range(T)]
                pe.wait_ge(xt_ready, 8)

                def down(k):
                    c, t = units[k]
                    w = DENSE[c][1] // P
                    n = FIRST_DENSE + 3 * c + 2
                    pe.wait_ge(ht_ev, k + 1)
                    if t == 0:
                        wait_chunk(pe, n)
                    for half in range(2):
                        for j in range(w):
                            i = mm(bank[4 + 2 * t + half][:, :], hidT[:, k % 2, j, :],
                                   chunk_view(n)[:, j, half * CH:(half + 1) * CH],
                                   start=c == 0 and j == 0, stop=c == len(DENSE) - 1 and j == w - 1)
                    i.then_inc(dn_mm, 1)

                for k, (c, t) in enumerate(units):
                    n = FIRST_DENSE + 3 * c
                    if t == 0:
                        wait_chunk(pe, n)
                        wait_chunk(pe, n + 1)
                    if k:
                        pe.wait_ge(g_silu, k)
                    token_group(n, t, bank[0]).then_inc(g_mm, 1)
                    if k:
                        if k > 2:
                            pe.wait_ge(ht_ev, k - 2)
                        hidden_transposes((k - 1, 0), DENSE[units[k - 1][0]][1])
                        pe.wait_ge(h_ok, k)
                    token_group(n + 1, t, bank[1]).then_inc(u_mm, 1)
                    if k:
                        down(k - 1)
                k = len(units)
                hidden_transposes((k - 1, 0), DENSE[-1][1])
                down(k - 1)
                x_transposes(2)

            def router():
                pe.wait_ge(xt_ready, 16)
                pe.wait_ge(in_rows, 48)
                for t in range(T):
                    for k in range(KT):
                        i = mm(bank[0][:, t * NEXP:(t + 1) * NEXP], xT[:, k, t * P:(t + 1) * P], wr[:, k, :],
                               start=k == 0, stop=k == KT - 1)
                i.then_inc(rt_mm, 1)
                pe.wait_ge(rt_mask, 1)
                mm(bank[1][:, 0:8], triu, routed[:, 0, :], start=True, stop=True).then_inc(ga_mm, GA0)
                mm(bank[1][:, 8:16], ones[:, 0:P], routed[:, 0, :], start=True, stop=False)
                mm(bank[1][:, 8:16], triu, routed[:, 1, :], start=False, stop=True).then_inc(st_mm, ST0)
                mm(bank[1][:, 16:24], ones[:, 0:P], routed[:, 0, :], start=True, stop=False)
                mm(bank[1][:, 16:24], ones[:, 0:P], routed[:, 1, :], start=False, stop=True).then_inc(rk_mm, 1)

            def experts(it):
                U = it * (TURN * UNITS) + DENSE_UNITS
                for j in range(TURN):
                    E = it * TURN + j
                    pe.wait_ge(sel_ok, E * 2 + 2)
                    for h in range(2):
                        for kk in range(4):
                            k = 4 * h + kk
                            for t in range(T):
                                i = mm(bank[2 + h][:, kk * P:(kk + 1) * P], x_tok[:, t, k * P:(k + 1) * P],
                                       sel[:, t, :], start=t == 0, stop=t == T - 1)
                        i.then_inc(ga_mm, 1)
                    pe.wait_ge(y_add, E * 4 + Y0)
                    for t in range(T):
                        i = tr(bank[6][:, t * P:(t + 1) * P], selc[:, t, :], ident)
                    i.then_inc(st_mm, 1)
                    pe.wait_ge(ga_ev, E * 2 + 2)

                    def down(c):
                        k = j * UNITS + c
                        s = (3 * k + 2) % NSLOT
                        pe.wait_ge(ht_ev, U + (k + 1))
                        pe.wait_ge(slot_full[s], (it * FILLS + (FILLS0 + (3 * k + 2) // NSLOT + 1)) * 16)
                        for half in range(2):
                            for jj in range(CH // P):
                                i = mm(bank[4 + half][:, :], hidT[:, k % 2, jj, :],
                                       slot_view(s, CH // P, D)[:, jj, half * CH:(half + 1) * CH],
                                       start=c == 0 and jj == 0, stop=c == UNITS - 1 and jj == CH // P - 1)
                        i.then_inc(dn_mm, 1)

                    def up(c, m, b):
                        k = j * UNITS + c
                        s = (3 * k + m) % NSLOT
                        pe.wait_ge(slot_full[s], (it * FILLS + (FILLS0 + (3 * k + m) // NSLOT + 1)) * 16)
                        for kk in range(KT):
                            i = mm(b[:, :], xg[:, kk, :], slot_view(s, KT, CH)[:, kk, :], start=kk == 0, stop=kk == KT - 1)
                        return i

                    for c in range(UNITS):
                        k = j * UNITS + c
                        pe.wait_ge(g_silu, U + k)
                        up(c, 0, bank[0]).then_inc(g_mm, 1)
                        if c:
                            pe.wait_ge(ht_ev, U + max(k - 2, 0))
                            hidden_transposes((k - 1, U), CH)
                        pe.wait_ge(h_ok, U + k)
                        up(c, 1, bank[1]).then_inc(u_mm, 1)
                        if c:
                            down(c - 1)
                    pe.wait_ge(ht_ev, U + ((j + 1) * UNITS - 2))
                    hidden_transposes(((j + 1) * UNITS - 1, U), CH)
                    down(UNITS - 1)
                    pe.wait_ge(st_ev, E + 1)
                    for half in range(2):
                        pe.wait_ge((eo_lo, eo_hi)[half], E + 1)
                        for t in range(T):
                            b = bank[(6, 7, 4, 5)[2 * half + t]]
                            mm(b[:, :], selT[:, t, :], eo[:, half * CH:(half + 1) * CH], start=True, stop=True
                               ).then_inc(back_mm, 1)

            def again():
                pe.wait_ge(more_ok, 1)
                return pe.value_load(more[0:1, 0:1], min_val=0, max_val=1)

            x_transposes(0)
            attention(0)
            dense()
            attention(1)
            router()
            with pe.Fori(0, TURNS) as i:
                experts(i)
            with pe.If(again() > 0):
                with pe.Fori(0, TURNS) as i:
                    experts(i + TURNS)

        @block.scalar
        def _(act):
            copy = nc.scalar.copy

            def fn(out_, in_, f, **kw):
                return nc.scalar.activation(out_, in_, f, **kw)

            def x_evacuate(stage):
                for t in range(T):
                    for h in range(2):
                        act.wait_ge(xt_mm, 4 * stage + 2 * t + h + 1)
                        copy(xT[:, 4 * h:4 * h + 4, t * P:(t + 1) * P],
                             bank[4 + 2 * t + h][:, :].rearrange("p (k n) -> p k n", k=4)).then_inc(xt_ready, 1)

            def rsqrt_start(l, step, n):
                act.wait_ge(var_ok[l], step + 1)
                fn(rs[:, 0:n], var[:, 0:n], ACT.Ln, bias=eps).then_inc(ln_v[l], 1)
                act.wait_ge(ln_v[l], step + 1)
                fn(rs[:, 0:n], rs[:, 0:n], ACT.Exp, scale=-0.5).then_inc(rs_ok[l], 1)

            def q_or_k(l, first):
                for j in range(first, first + 2):
                    act.wait_ge(qk_mm[l], j + 1)
                    copy(pre[:, 2 * j:2 * j + 2, CONV - 1:], bank[5 + j % 2][:, :].rearrange("p (f s) -> p f s", f=2)
                         ).then_inc(qk_ev[l], 1)

            def attention(l):
                for g in range(6):
                    c, t = divmod(g, 2)
                    w = PROJ[c][1] - PROJ[c][0]
                    act.wait_ge(proj_mm[l], g + 1)
                    copy(att[:, t, c * CH:c * CH + w], bank[g % 4][:, 0:w]).then_inc(proj_ev[l], 1)
                    if g == 1:
                        act.wait_ge(gate_mm[l], 2)
                        act.wait_ge(in_const, 32)
                        fn(gate[0:ML_H, 0, :], bank[4][0:ML_H, 0:SEQ], ACT.Identity,
                           bias=feat[0:ML_H, l, PC_I:PC_I + 1]).then_inc(gate_ev[l], 1)
                        fn(gate[0:ML_H, 1, :], bank[4][0:ML_H, SEQ:2 * SEQ], ACT.Identity,
                           bias=feat[0:ML_H, l, PC_F:PC_F + 1]).then_inc(gate_ev[l], 1)
                        act.wait_ge(gate_ev[l], 2)
                        fn(gate[0:ML_H, 2, :], gate[0:ML_H, 1, :], ACT.Abs).then_inc(gate_ev[l], 1)
                        act.wait_ge(gate_ev[l], 3)
                        fn(gate[0:ML_H, 2, :], gate[0:ML_H, 2, :], ACT.Exp, scale=-1.0).then_inc(gate_ev[l], 1)
                        act.wait_ge(gate_ev[l], 4)
                        fn(gate[0:ML_H, 2, :], gate[0:ML_H, 2, :], ACT.Ln, bias=cst[0:ML_H, K_ONES:K_ONES + 1]
                           ).then_inc(gate_ev[l], 1)
                rsqrt_start(l, 0, T)
                q_or_k(l, 0)
                act.wait_ge(itr_mm[l], 1)
                copy(iqT, bank[0][:, :].rearrange("p (f s) -> p f s", f=2)).then_inc(itr_ev[l], 1)
                act.wait_ge(itr_mm[l], 2)
                copy(ikT, bank[1][:, 0:SEQ]).then_inc(itr_ev[l], 1)
                q_or_k(l, 2)
                for h in range(IDX_H):
                    act.wait_ge(idx_mm[l], h + 1)
                    fn(relu[:, h, :], bank[h][:, 0:384], ACT.Relu, scale=AT_D ** -0.5 * IDX_H ** -0.5
                       ).then_inc(idx_ev[l], 1)
                for b in range(3):
                    act.wait_ge(atr_mm[l], b + 1)
                    dst = aqT[:, 2 * b:2 * b + 2] if b < 2 else akT
                    copy(dst, bank[4 + b][:, :].rearrange("p (f s) -> p f s", f=2)).then_inc(atr_ev[l], 1)
                act.wait_ge(gtr_mm[l], 1)
                copy(gT, bank[7][:, 0:T * ML_H].rearrange("p (t h) -> p t h", t=T)).then_inc(gtr_ev[l], 1)
                fn(emT, bank[7][:, T * ML_H:2 * T * ML_H].rearrange("p (t h) -> p t h", t=T), ACT.Exp, scale=-1.0
                   ).then_inc(gtr_ev[l], 1)
                for half in range(2):
                    act.wait_ge(conv_y[l], half + 1)
                    fn(qk[:, half * ML_H:(half + 1) * ML_H, :], qk[:, half * ML_H:(half + 1) * ML_H, :], ACT.Silu
                       ).then_inc(conv_ok[l], 1)
                for t in range(T):
                    act.wait_ge(vo_mm[l], t + 1)
                    copy(v_aug[:, t, :, 0:ML_D], bank[t][:, :].rearrange("p (h n) -> p h n", h=ML_H)
                         ).then_inc(v_ev[l], 1)
                for t in range(T):
                    act.wait_ge(vo_mm[l], T + t + 1)
                    fn(og[:, t, :], bank[2 + t][:, :], ACT.Exp, scale=-1.0).then_inc(o_ev[l], 1)
                for h in range(ML_H):
                    act.wait_ge(ml_e[l], h + 1)
                    fn(mld[:, h, :], mld[:, h, :], ACT.Exp).then_inc(ml_d[l], 1)
                rsqrt_start(l, 1, T * ML_H)
                for h in range(AT_H):
                    act.wait_ge(sc_max[l], h + 1)
                    for t in range(T):
                        o = slice(0, P) if t == 0 else slice(P, 3 * P)
                        i = fn(probs[:, h % 3, o], probs[:, h % 3, o], ACT.Exp, scale=AT_D ** -0.5,
                               bias=nmax[:, h % 3, t:t + 1], accum_out=rsum[:, t, h:h + 1])
                    i.then_inc(sc_exp[l], 1)
                for t in range(T):
                    for h in range(2):
                        g = 2 * t + h
                        act.wait_ge(mtr_mm[l], g + 1)
                        copy(mixT[:, 4 * h:4 * h + 4, t * P:(t + 1) * P],
                             bank[4 + g][:, :].rearrange("p (k n) -> p k n", k=4)).then_inc(mtr_ev[l], 1)
                rsqrt_start(l, 2, T)
                x_evacuate(2 * l + 1)

            def unit(k, base, w):
                act.wait_ge(g_mm, base + (k + 1))
                if k > 1 or not isinstance(base, int):
                    act.wait_ge(h_ok, base + max(k - 1, 0))
                fn(silu[:, k % 2, 0:w], bank[0][:, 0:w], ACT.Silu).then_inc(g_silu, 1)

            def hidden_out(k, base, w):
                act.wait_ge(ht_mm, base + (k + 1))
                if k > 1 or not isinstance(base, int):
                    act.wait_ge(dn_mm, base + max(k - 1, 0))
                copy(hidT[:, k % 2, 0:w // P, :], bank[2 + k % 2][:, 0:w].rearrange("p (j n) -> p j n", j=w // P)
                     ).then_inc(ht_ev, 1)

            def dense():
                ws = [w for _, w in DENSE for _ in range(T)]
                for k in range(len(ws) + 1):
                    if k < len(ws):
                        unit(k, 0, ws[k])
                    if k:
                        hidden_out(k - 1, 0, ws[k - 1])
                rsqrt_start(0, 3, T)
                x_evacuate(2)

            def experts(it):
                U = it * (TURN * UNITS) + DENSE_UNITS
                for j in range(TURN):
                    E = it * TURN + j
                    for h in range(2):
                        act.wait_ge(ga_mm, E * 2 + (GA0 + h + 1))
                        copy(xg[:, 4 * h:4 * h + 4, :], bank[2 + h][:, :].rearrange("p (k n) -> p k n", k=4)
                             ).then_inc(ga_ev, 1)
                    act.wait_ge(st_mm, E + (ST0 + 1))
                    copy(selT, bank[6][:, 0:SEQ].rearrange("p (t n) -> p t n", t=T)).then_inc(st_ev, 1)
                    for c in range(UNITS + 1):
                        k = j * UNITS + c
                        if c < UNITS:
                            unit(k, U, CH)
                        if c:
                            hidden_out(k - 1, U, CH)
                    act.wait_ge(dn_mm, U + (j + 1) * UNITS)
                    copy(eo[:, 0:CH], bank[4][:, :]).then_inc(eo_lo, 1)

            x_evacuate(0)
            attention(0)
            dense()
            attention(1)
            act.wait_ge(rt_diff, 1)
            fn(g2[:, :, 0:1], g2[:, :, 0:1], ACT.Exp).then_inc(rt_exp, 1)
            with act.Fori(0, TURNS) as i:
                experts(i)
            act.wait_ge(more_ok, 1)
            again = act.value_load(more[0:1, 0:1], min_val=0, max_val=1)
            with act.If(again > 0):
                with act.Fori(0, TURNS) as i:
                    experts(i + TURNS)
            rsqrt_start(1, 3, T)

        @block.vector
        def _(dve):
            ts, tt, stt = nc.vector.tensor_scalar, nc.vector.tensor_tensor, nc.vector.scalar_tensor_tensor
            steps = [0]

            def step(i):
                i.then_inc(dstep, 1)
                steps[0] += 1
                return steps[0]

            def after(n):
                dve.wait_ge(dstep, n)

            def link(i):
                after(step(i))

            def rsqrt_finish(l, n_step, n):
                dve.wait_ge(rs_ok[l], n_step + 1)
                v, r, a, b = var[:, 0:n], rs[:, 0:n], nt[:, 0, 0:n], nt[:, 1, 0:n]
                link(stt(a, v, eps, r, ALU.add, ALU.mult))
                link(stt(b, a, -0.5, r, ALU.mult, ALU.mult))
                link(stt(r, b, 1.5, r, ALU.add, ALU.mult))

            def layer_norm(l, which, src):
                for t in range(T):
                    for h in range(2):
                        s = step(nc.vector.bn_stats(stats[:, t, h, :], src[:, t, h * CH:(h + 1) * CH]))
                after(s)
                for t in range(T):
                    s = step(nc.vector.bn_aggr(mv[:, t, :], stats[:, t]))
                after(s)
                nc.vector.tensor_copy(var[:, 0:T], mv[:, 0:T, 1]).then_inc(var_ok[l], 1)
                dve.wait_ge(var_ok[l], 3 + which)
                rsqrt_finish(l, 2 + which, T)
                dve.wait_ge(in_ln, 16 * (l + 1))
                for t in range(T):
                    link(ts(x_tok[:, t], src[:, t], mv[:, t, 0:1], rs[:, t:t + 1], ALU.subtract, ALU.mult))
                    link(tt(x_tok[:, t], x_tok[:, t], ln[:, 2 * which], ALU.mult))
                    tt(x_tok[:, t], x_tok[:, t], ln[:, 2 * which + 1], ALU.add).then_inc(x_ready, 1)
                dve.wait_ge(x_ready, (2 * l + which + 1) * T)

            def rotate(l, h0, n):
                heads = att[:, :, A_Q:A_IW].rearrange("p t (h n) -> p t h n", n=AT_D)[:, :, h0:h0 + n]
                x1, x2 = heads[:, :, :, 0:ROT], heads[:, :, :, ROT:2 * ROT]
                table = [cst[:, a:a + T * ROT].rearrange("p (t r) -> p t r", t=T).unsqueeze(2)
                         .to_broadcast([P, T, n, ROT]) for a in (K_COS, K_SIN)]
                r = [b[:, :, 0:n, :] for b in rope]
                for i, (a, b) in enumerate(((x1, 0), (x2, 1), (x2, 0), (x1, 1))):
                    s = step(tt(r[i], a, table[b], ALU.mult))
                after(s)
                step(tt(x1, r[0], r[1], ALU.subtract))
                after(steps[0])
                tt(x2, r[2], r[3], ALU.add).then_inc(roped[l], 1)
                dve.wait_ge(roped[l], 1 if h0 else 2)

            def conv(l, half):
                dve.wait_ge(qk_ev[l], 2 * half + 2)
                f0 = half * ML_H
                for j in range(CONV):
                    for f in range(f0, f0 + ML_H):
                        w = feat[:, l, PC_W + f * CONV + j:PC_W + f * CONV + j + 1]
                        if j == 0:
                            s = step(ts(qk[:, f], pre[:, f, 0:SEQ], w, feat[:, l, PC_B + f:PC_B + f + 1],
                                        ALU.mult, ALU.add))
                        elif j < CONV - 1 or f < f0 + ML_H - 1:
                            after(s - ML_H + 1)
                            s = step(stt(qk[:, f], pre[:, f, j:j + SEQ], w, qk[:, f], ALU.mult, ALU.add))
                        else:
                            after(s)
                            stt(qk[:, f], pre[:, f, j:j + SEQ], w, qk[:, f], ALU.mult, ALU.add
                                ).then_inc(conv_y[l], 1)

            def index_norm(l):
                ik = [att[:, t, A_IK:A_IW] for t in range(T)]
                for t in range(T):
                    s = step(nc.vector.bn_stats(stats[:, t, 0, :], ik[t]))
                after(s)
                for t in range(T):
                    s = step(nc.vector.bn_aggr(mv[:, t, :], stats[:, t, 0]))
                after(s)
                nc.vector.tensor_copy(var[:, 0:T], mv[:, 0:T, 1]).then_inc(var_ok[l], 1)
                dve.wait_ge(var_ok[l], 1)
                rsqrt_finish(l, 0, T)
                dve.wait_ge(in_rows, 48)
                for t in range(T):
                    link(ts(ik[t], ik[t], mv[:, t, 0:1], rs[:, t:t + 1], ALU.subtract, ALU.mult))
                    link(tt(ik[t], ik[t], rows[:, l, AR_IG:AR_IB], ALU.mult))
                    link(tt(ik[t], ik[t], rows[:, l, AR_IB:AR_END], ALU.add))

            def gates(l):
                r = [gate[0:ML_H, i, :] for i in range(4)]
                dve.wait_ge(gate_ev[l], 5)
                link(stt(r[2], r[1], 0.0, r[2], ALU.min, ALU.subtract))
                scan = nc.vector.tensor_tensor_scan
                link(scan(r[3], ones[0:ML_H], r[2], 0.0, ALU.mult, ALU.add))
                link(tt(r[0], r[0], r[3], ALU.subtract))
                link(scan(r[1], ones[0:ML_H], r[0], 0.0, ALU.mult, ALU.max))
                tt(r[2], r[3], r[1], ALU.add).then_inc(gate_row[l], 1)

            def choose(l):
                part = [slice(0, P), slice(P, 3 * P)]
                for h in range(IDX_H):
                    dve.wait_ge(idx_ev[l], h + 1)
                    for t in range(T):
                        w = att[:, t, A_IW + h:A_IW + h + 1]
                        if h == 0:
                            s = step(ts(iscore[:, part[t]], relu[:, h, part[t]], w, None, ALU.mult))
                        else:
                            after(s - 1)
                            s = step(stt(iscore[:, part[t]], relu[:, h, part[t]], w, iscore[:, part[t]],
                                         ALU.mult, ALU.add))
                after(s)
                link(tt(iscore, iscore, causal, ALU.add))
                for r in range(TOPK // 8):
                    src = iscore if r == 0 else left
                    for t in range(T):
                        if r:
                            after(steps[0] - 1)
                        step(nc.vector.max(top8[:, t], src[:, part[t]]))
                    for t in range(T):
                        after(steps[0] - 1)
                        step(nc.vector.match_replace(left[:, part[t]], top8[:, t], src[:, part[t]], TAKEN))
                after(steps[0])
                link(ts(choice, left, TAKEN, NEG, ALU.not_equal, ALU.mult))
                link(tt(choice, choice, causal, ALU.add))

            def mlstm(l):
                dve.wait_ge(gtr_ev[l], 2)
                for h in range(ML_H):
                    if h % 2 == 0:
                        dve.wait_ge(mrow_mm[l], h // 2 + 1)
                    m = bank[4 + h // 2][:, (h % 2) * SEQ:(h % 2 + 1) * SEQ]
                    stt(mld[:, h, 0:SEQ], causalT[:, 0:SEQ], gT[:, 0, h:h + 1], m, ALU.add, ALU.subtract)
                    stt(mld[:, h, SEQ:SEQ + P], causalT[:, SEQ:SEQ + P], gT[:, 1, h:h + 1], m[:, P:SEQ],
                        ALU.add, ALU.subtract).then_inc(ml_e[l], 1)
                dve.wait_ge(o_ev[l], T)
                link(ts(og, og, 1.0, None, ALU.add))
                link(nc.vector.reciprocal(og, og))
                for t in range(T):
                    step(tt(og[:, t], og[:, t], rows[:, l, AR_NG:AR_IG], ALU.mult))
                for h in range(ML_H):
                    dve.wait_ge(mls_mm[l], h + 1)
                    dve.wait_ge(ml_d[l], h + 1)
                    stt(mld[:, h], bank[6 + h % 2][:, 0:384], float(ML_D) ** -0.5, mld[:, h], ALU.mult, ALU.mult
                        ).then_inc(ml_p[l], 1)
                dve.wait_ge(num_mm[l], ML_H)
                num = [[bank[2 * t + h // 2][:, (h % 2) * (ML_D + 1):(h % 2) * (ML_D + 1) + ML_D]
                        for h in range(ML_H)] for t in range(T)]
                for t in range(T):
                    for pair in range(2):
                        den = bank[2 * t + pair][:, 0:2 * (ML_D + 1)].rearrange("p (h n) -> p h n", h=2)[:, :, ML_D]
                        d = slice(2 * pair, 2 * pair + 2)
                        link(ts(rden2[:, t, d], den, -1.0, None, ALU.mult))
                        step(tt(rden[:, t, d], den, rden2[:, t, d], ALU.max))
                    for h in range(ML_H):
                        step(nc.vector.bn_stats(stats[:, t * ML_H + h, 0, :], num[t][h]))
                after(steps[0])
                link(tt(rden, rden, emT, ALU.max))
                step(nc.vector.reciprocal(rden, rden))
                for i in range(T * ML_H):
                    step(nc.vector.bn_aggr(mv[:, i, :], stats[:, i, 0]))
                after(steps[0])
                link(tt(rden2, rden, rden, ALU.mult))
                tt(var[:, 0:T * ML_H], mv[:, :, 1], rden2.rearrange("p t h -> p (t h)"), ALU.mult
                   ).then_inc(var_ok[l], 1)
                dve.wait_ge(var_ok[l], 2)
                rsqrt_finish(l, 1, T * ML_H)
                link(tt(rs[:, :], rs[:, :], rden.rearrange("p t h -> p (t h)"), ALU.mult))
                for t in range(T):
                    for h in range(ML_H):
                        i = t * ML_H + h
                        step(ts(mix[:, t, h * ML_D:(h + 1) * ML_D], num[t][h], mv[:, i, 0:1], rs[:, i:i + 1],
                                ALU.subtract, ALU.mult))
                after(steps[0])
                step(tt(mix[:, 0, 0:ML_W], mix[:, 0, 0:ML_W], og[:, 0], ALU.mult))
                tt(mix[:, 1, 0:ML_W], mix[:, 1, 0:ML_W], og[:, 1], ALU.mult).then_inc(mix_ml[l], 1)

            def attention(l):
                step(nc.vector.memset(pre[:, :, 0:CONV - 1], 0.0))
                link(nc.vector.memset(v_aug[:, :, :, ML_D:ML_D + 1], 1.0))
                dve.wait_ge(proj_ev[l], 6)
                index_norm(l)
                rotate(l, (A_IQ - A_Q) // AT_D, IDX_H + 1)
                gates(l)
                rotate(l, 0, AT_H + AT_KV)
                conv(l, 0)
                choose(l)
                conv(l, 1)
                mlstm(l)

                def masked(h):
                    b = h % 3
                    dve.wait_ge(sc_mm[l], h + 1)
                    if h >= 3:
                        dve.wait_ge(ptr_mm[l], h - 2)
                    for t in range(T):
                        o = slice(0, P) if t == 0 else slice(P, 3 * P)
                        s = step(nc.vector.tensor_tensor_reduce(
                            out=probs[:, b, o], in0=bank[4 + h % 4][:, o], in1=choice[:, o], scale=1.0, scalar=TAKEN,
                            op0=ALU.add, op1=ALU.max, accum_out=rmax[:, b, t:t + 1]))
                    after(s)
                    ts(nmax[:, b], rmax[:, b], -(AT_D ** -0.5), None, ALU.mult).then_inc(sc_max[l], 1)

                def transposed(h):
                    dve.wait_ge(ptr_mm[l], h + 1)
                    if h >= 3:
                        dve.wait_ge(pv_mm[l], h - 2)
                    nc.vector.tensor_copy(probsT[:, h % 3], bank[2 + h % 2][:, 0:384]).then_inc(pt_ok[l], 1)

                for h in range(AT_H + 1):
                    if h < AT_H:
                        masked(h)
                    if h:
                        transposed(h - 1)
                dve.wait_ge(pv_mm[l], AT_H)
                dve.wait_ge(sc_exp[l], AT_H)
                link(nc.vector.reciprocal(rsum, rsum))
                for t in range(T):
                    i = tt(mix[:, t, ML_W:].rearrange("p (h n) -> p h n", h=AT_H),
                           bank[t][:, :].rearrange("p (h n) -> p h n", h=AT_H),
                           rsum[:, t].unsqueeze(2).to_broadcast([P, AT_H, AT_D]), ALU.mult)
                    if t == 0:
                        step(i)
                i.then_inc(mix_at[l], 1)
                for g in range(4):
                    t, c = divmod(g, 2)
                    dve.wait_ge(op_mm[l], g + 1)
                    half = x_tok[:, t, c * CH:(c + 1) * CH]
                    s = step(stt(half, half, ALPHA, bank[g][:, :], ALU.mult, ALU.add))
                after(s)
                layer_norm(l, 0, x_tok)

            def hidden(k, base, w):
                dve.wait_ge(g_silu, base + (k + 1))
                dve.wait_ge(u_mm, base + (k + 1))
                if k > 1 or not isinstance(base, int):
                    dve.wait_ge(ht_mm, base + max(k - 1, 0))
                tt(hid[:, k % 2, 0:w], silu[:, k % 2, 0:w], bank[1][:, 0:w], ALU.mult).then_inc(h_ok, 1)

            def dense():
                n = T * len(DENSE)
                for k in range(n):
                    hidden(k, 0, DENSE[k // T][1])
                dve.wait_ge(dn_mm, n)
                for g in range(4):
                    t, c = divmod(g, 2)
                    half = x_tok[:, t, c * CH:(c + 1) * CH]
                    s = step(stt(half, half, ALPHA, bank[4 + g][:, :], ALU.mult, ALU.add))
                after(s)
                layer_norm(0, 1, x_tok)

            def route():
                dve.wait_ge(rt_mm, 1)
                for t in range(T):
                    s = step(tt(lg[:, t], bank[0][:, t * NEXP:(t + 1) * NEXP], br[:], ALU.add))
                after(s)
                for t in range(T):
                    s = step(nc.vector.max(m8[:, t], lg[:, t]))
                after(s)
                tt(g2[:, :, 0:1], m8[:, :, 1:2], m8[:, :, 0:1], ALU.subtract).then_inc(rt_diff, 1)
                for t in range(T):
                    s = step(nc.vector.max_index(i8[:, t], m8[:, t], lg[:, t]))
                after(s)
                link(nc.vector.tensor_copy(i8f[:, :, :], i8[:, :, 0:2]))
                for t in range(T):
                    for j in range(2):
                        s = step(ts(oh[:, t, j], iota[:, 0:NEXP], i8f[:, t, j:j + 1], None, ALU.is_equal))
                after(s)
                tt(routed[:, :, :], oh[:, :, 0], oh[:, :, 1], ALU.add).then_inc(rt_mask, 1)
                dve.wait_ge(rt_exp, 1)
                link(ts(g2[:, :, 1:2], g2[:, :, 0:1], 1.0, None, ALU.add))
                link(nc.vector.reciprocal(g2[:, :, 1:2], g2[:, :, 1:2]))
                link(tt(g2[:, :, 2:3], g2[:, :, 0:1], g2[:, :, 1:2], ALU.mult))
                for t in range(T):
                    s = step(ts(comb[:, t], oh[:, t, 0], g2[:, t, 1:2], None, ALU.mult))
                after(s)
                for t in range(T):
                    s = step(stt(comb[:, t], oh[:, t, 1], g2[:, t, 2:3], comb[:, t], ALU.mult, ALU.add))
                dve.wait_ge(rk_mm, 1)
                after(s)
                r = rank[:, :, :]
                link(stt(r, bank[1][:, 0:16].rearrange("p (t e) -> p t e", t=T), 1.0, routed[:, :, :],
                         ALU.add, ALU.mult))
                link(ts(r, r, -1.0, None, ALU.add))
                link(nc.vector.reduce_max(cmax[:], bank[1][:, 16:24], axis=AX.X))
                ts(more[:], cmax[:], float(P), None, ALU.is_gt).then_inc(more_ok, 1)
                for t in range(T):
                    ts(y[:, t], x_tok[:, t], ALPHA, None, ALU.mult).then_inc(y_add, 1)
                dve.wait_ge(y_add, Y0)

            def experts(it, pair):
                U = it * (TURN * UNITS) + DENSE_UNITS
                for j in range(TURN):
                    E = it * TURN + j
                    e = bass.ds(pair * TURN + j, 1)
                    dve.wait_ge(ga_mm, E * 2 + GA0)
                    for t in range(T):
                        i = ts(sel[:, t], iota, rank[:, t, e], None, ALU.is_equal)
                    i.then_inc(sel_ok, 1)
                    dve.wait_ge(st_mm, E + ST0)
                    for t in range(T):
                        i = ts(selc[:, t], iota, rank[:, t, e], comb[:, t, e], ALU.is_equal, ALU.mult)
                    i.then_inc(sel_ok, 1)
                    for c in range(UNITS):
                        hidden(j * UNITS + c, U, CH)
                    dve.wait_ge(dn_mm, U + (j + 1) * UNITS)
                    nc.vector.tensor_copy(eo[:, CH:D], bank[5][:, :]).then_inc(eo_hi, 1)
                    dve.wait_ge(y_add, E * 4 + Y0)
                    for half in range(2):
                        for t in range(T):
                            g = 2 * half + t
                            dve.wait_ge(back_mm, E * 4 + (g + 1))
                            part = y[:, t, half * CH:(half + 1) * CH]
                            tt(part, part, bank[(6, 7, 4, 5)[g]][:, :], ALU.add).then_inc(y_add, 1)

            attention(0)
            dense()
            attention(1)
            route()
            with dve.Fori(0, TURNS) as i:
                experts(i, i)
            dve.wait_ge(y_add, 4 * NEXP + Y0)
            again = dve.value_load(more[0:1, 0:1], min_val=0, max_val=1)
            with dve.If(again > 0):
                ts(rank[:, :, :], rank[:, :, :], -float(P), None, ALU.add).then_inc(rank_ok, 1)
                dve.wait_ge(rank_ok, 1)
                with dve.Fori(0, TURNS) as i:
                    experts(i + TURNS, i)
                dve.wait_ge(y_add, 8 * NEXP + Y0)
            layer_norm(1, 1, y)


_OUTS = [((1, SEQ, D), "float32")]


def kernel(x, w_in, ml_conv_w, ml_conv_b, ml_i_b, ml_f_b, ml_norm_g, idx_k_norm_g, idx_k_norm_b, w_out,
           ln1_g, ln1_b, ln2_g, ln2_b, ffn_w_gate, ffn_w_up, ffn_w_down,
           moe_w_router, moe_b_router, moe_w_gate, moe_w_up, moe_w_down):
    import concourse.bacc as bacc
    from concourse.bass_utils import run_bass_kernel_spmd

    a = {k: np.asarray(v) for k, v in locals().items() if hasattr(v, "shape")}
    feat = np.zeros((DEPTH, P, PC_END), np.float32)
    feat[:, :, PC_W:PC_B] = a["ml_conv_w"].reshape(DEPTH, CONV, 2 * ML_H, P).transpose(0, 3, 2, 1).reshape(DEPTH, P, -1)
    feat[:, :, PC_B:PC_I] = a["ml_conv_b"].reshape(DEPTH, 2 * ML_H, P).transpose(0, 2, 1)
    feat[:, 0:ML_H, PC_I] = a["ml_i_b"]
    feat[:, 0:ML_H, PC_F] = a["ml_f_b"]
    arrays = {
        "x": a["x"], "w_in": a["w_in"], "w_out": a["w_out"],
        "ffn_gate": a["ffn_w_gate"], "ffn_up": a["ffn_w_up"], "ffn_down": a["ffn_w_down"],
        "w_router": a["moe_w_router"], "b_router": a["moe_b_router"],
        "moe_gate": a["moe_w_gate"], "moe_up": a["moe_w_up"], "moe_down": a["moe_w_down"],
        "feat_params": feat,
        "row_params": np.concatenate([a["ml_norm_g"], a["idx_k_norm_g"], a["idx_k_norm_b"]], axis=1),
        "ln_params": np.stack([a["ln1_g"], a["ln1_b"], a["ln2_g"], a["ln2_b"]], axis=1),
        "consts": shape_constants(),
    }
    arrays = {k: np.ascontiguousarray(v) for k, v in arrays.items()}
    nc = bacc.Bacc("TRN2", target_bir_lowering=False, num_devices=1)
    aps = {k: nc.dram_tensor(k, v.shape, mybir.dt.from_np(v.dtype), kind="ExternalInput").ap()
           for k, v in arrays.items()}
    shape, dtype = _OUTS[0]
    out = nc.dram_tensor("out", shape, mybir.dt.from_np(np.dtype(dtype)), kind="ExternalOutput").ap()
    build_program(nc, **aps, out=out)
    r = run_bass_kernel_spmd(nc, [arrays], core_ids=[0])
    return r.results[0]["out"]
```

```python
from contextlib import ExitStack

import numpy as np

import concourse.bass as bass
from concourse import mybir

F32 = mybir.dt.float32
F32R = mybir.dt.float32r
I32 = mybir.dt.int32
U32 = mybir.dt.uint32
ALU = mybir.AluOpType
ACT = mybir.ActivationFunctionType
AX = mybir.AxisListType

P = 128
SEQ, D = 256, 1024
T = SEQ // P
KT = D // P
DEPTH = 2
ML_H, ML_D = 4, 128
ML_W = ML_H * ML_D
CONV = 4
AT_H, AT_KV, AT_D = 8, 2, 64
IDX_H = 4
TOPK = min(256, SEQ // 4)
FF_DENSE, FF_EXPERT, NEXP = 2816, 3584, 8
ALPHA = (2 * DEPTH) ** 0.25
LN_EPS = 1e-5
ROPE_THETA = 500000.0
ROT = AT_D // 4 // 2

C_MQ, C_MK, C_MV, C_MO = 0, ML_W, 2 * ML_W, 3 * ML_W
C_GATE = 4 * ML_W
C_END = C_GATE + 2 * ML_H + AT_H * AT_D + 2 * AT_KV * AT_D + (IDX_H + 1) * AT_D + IDX_H
AW = C_END - C_GATE
A_Q = 2 * ML_H
A_K = A_Q + AT_H * AT_D
A_V = A_K + AT_KV * AT_D
A_IQ = A_V + AT_KV * AT_D
A_IK = A_IQ + IDX_H * AT_D
A_IW = A_IK + AT_D

NSLOT = 6
SLOT = 2048
NSPLIT = 3
CH = 512
NEG = -1.0e30
TAKEN = -3.0e38

K_ID, K_CAUSAL, K_CAUSALT, K_IOTA, K_TRIU, K_ONES = 0, 128, 512, 896, 1024, 1152
K_SEL, K_COS, K_SIN, K_EPS = 1408, 1920, 1936, 1952
K_END = 1953


def shape_constants():
    t = np.zeros((P, K_END), np.float32)
    p = np.arange(P)[:, None]
    f = np.arange(P)[None, :]
    t[:, K_ID:K_ID + P] = p == f
    diag = np.where(f <= p, 0.0, NEG)
    t[:, K_CAUSAL:K_CAUSAL + P] = diag
    t[:, K_CAUSAL + 2 * P:K_CAUSAL + 3 * P] = diag
    t[:, K_CAUSALT:K_CAUSALT + P] = diag.T
    t[:, K_CAUSALT + 2 * P:K_CAUSALT + 3 * P] = diag.T
    t[:, K_IOTA:K_IOTA + P] = f
    t[:, K_TRIU:K_TRIU + P] = p < f
    t[:, K_ONES:K_ONES + SEQ] = 1.0
    for h in range(ML_H):
        t[h, K_SEL + h * P:K_SEL + (h + 1) * P] = 1.0
    inv = np.float32(ROPE_THETA) ** (-np.arange(ROT, dtype=np.float32) / np.float32(ROT))
    ang = np.arange(SEQ, dtype=np.float32)[:, None] * inv[None, :]
    t[:, K_COS:K_COS + T * ROT] = np.cos(ang).reshape(T, P, ROT).transpose(1, 0, 2).reshape(P, T * ROT)
    t[:, K_SIN:K_SIN + T * ROT] = np.sin(ang).reshape(T, P, ROT).transpose(1, 0, 2).reshape(P, T * ROT)
    t[:, K_EPS] = LN_EPS
    return t


PC_W, PC_B, PC_I, PC_F, PC_END = 0, 2 * ML_H * CONV, 2 * ML_H * CONV + 2 * ML_H, 2 * ML_H * CONV + 2 * ML_H + 1, 42
AR_NG, AR_IG, AR_IB, AR_END = 0, ML_W, ML_W + AT_D, ML_W + 2 * AT_D


def build_program(nc, x, w_in, w_out, ffn_gate, ffn_up, ffn_down, w_router, b_router, moe_gate, moe_up, moe_down,
                  feat_params, row_params, ln_params, consts, out):
    with ExitStack() as ctx:
        def sb(name, shape, dt=F32):
            return ctx.enter_context(nc.sbuf_tensor(name, shape, dt))

        def sem(name):
            return ctx.enter_context(nc.semaphore(name))

        def layer_sem(name):
            return [sem(f"{name}_{l}") for l in range(DEPTH)]

        x_tok = sb("x_tok", [P, T, D])
        xT = sb("xT", [P, KT, SEQ])
        cst = sb("cst", [P, K_END])
        feat = sb("feat", [P, DEPTH, PC_END])
        rows = sb("rows", [P, DEPTH, AR_END])
        ln = sb("ln", [P, 2, D])
        ring = sb("ring", [P, NSLOT, SLOT])
        split = sb("split", [P, NSPLIT, 2, SLOT], F32R)
        xs = sb("xs", [P, 2, KT, SEQ], F32R)
        hs = sb("hs", [P, T, 2, CH // P, P], F32R)
        WORK = 12352
        work = sb("work", [P, WORK])
        used = [0, 0]

        def carve(phase, size):
            a = used[phase]
            used[phase] += size
            assert used[phase] <= WORK, (phase, used[phase])
            return work[:, a:a + size]

        pre_mem = carve(0, 2 * ML_H * (SEQ + CONV - 1))
        pre = pre_mem.rearrange("p (f s) -> p f s", f=2 * ML_H)
        og = pre_mem[:, 0:T * ML_W].rearrange("p (t n) -> p t n", t=T)
        v_aug = pre_mem[:, T * ML_W:T * ML_W + T * ML_H * (ML_D + 1)].rearrange(
            "p (t h n) -> p t h n", t=T, h=ML_H)
        mixT = xT
        qk_mem = carve(0, 2 * ML_H * SEQ)
        qk = qk_mem.rearrange("p (f s) -> p f s", f=2 * ML_H)
        mix = qk_mem.rearrange("p (t n) -> p t n", t=T)
        iscore = qk_mem[:, ML_H * SEQ:ML_H * SEQ + 384]
        left = qk_mem[:, ML_H * SEQ + 384:ML_H * SEQ + 768]
        att = carve(0, T * AW).rearrange("p (t n) -> p t n", t=T)
        aqT = carve(0, 4 * SEQ).rearrange("p (f s) -> p f s", f=4)
        akT = carve(0, AT_KV * SEQ).rearrange("p (g s) -> p g s", g=AT_KV)
        idx_mem = carve(0, 2 * SEQ + SEQ + 2 * 384)
        iqT = idx_mem[:, 0:2 * SEQ].rearrange("p (f s) -> p f s", f=2)
        ikT = idx_mem[:, 2 * SEQ:3 * SEQ]
        relu = idx_mem[:, 3 * SEQ:].rearrange("p (b s) -> p b s", b=2)
        mld = idx_mem[:, 0:ML_H * 384].rearrange("p (h s) -> p h s", h=ML_H)
        shared = carve(0, 6 * 384)
        rope = [shared[:, i * T * 10 * ROT:(i + 1) * T * 10 * ROT].rearrange("p (t h r) -> p t h r", t=T, h=10)
                for i in range(4)]
        kdup = shared[:, 0:T * 2 * AT_KV * AT_D].rearrange("p (t g c n) -> p t g c n", t=T, g=AT_KV, c=2)
        ikdup = shared[:, 640:640 + T * 2 * AT_D].rearrange("p (t c n) -> p t c n", t=T, c=2)
        gate = shared[:, 3 * 384:3 * 384 + 4 * SEQ].rearrange("p (r s) -> p r s", r=4)
        probs = shared[:, 0:3 * 384].rearrange("p (b s) -> p b s", b=3)
        probsT = shared[:, 3 * 384:6 * 384].rearrange("p (b s) -> p b s", b=3)
        choice = carve(0, 384)
        top8 = carve(0, T * 8).rearrange("p (t n) -> p t n", t=T)
        gT = carve(0, T * ML_H).rearrange("p (t h) -> p t h", t=T)
        emT = carve(0, T * ML_H).rearrange("p (t h) -> p t h", t=T)
        rden = carve(0, T * ML_H).rearrange("p (t h) -> p t h", t=T)
        rden2 = carve(0, T * ML_H).rearrange("p (t h) -> p t h", t=T)
        rsum = carve(0, T * AT_H).rearrange("p (t h) -> p t h", t=T)
        rmax = carve(0, 3 * T).rearrange("p (b t) -> p b t", b=3)
        nmax = carve(0, 3 * T).rearrange("p (b t) -> p b t", b=3)
        y = carve(1, T * D).rearrange("p (t n) -> p t n", t=T)
        silu = carve(1, T * CH).rearrange("p (t n) -> p t n", t=T)
        hid = carve(1, T * CH).rearrange("p (t n) -> p t n", t=T)
        sel = carve(1, T * P).rearrange("p (t n) -> p t n", t=T)
        selc = carve(1, T * P).rearrange("p (t n) -> p t n", t=T)
        selT = carve(1, T * P).rearrange("p (t n) -> p t n", t=T)
        eo = carve(1, D)
        stats = sb("stats", [P, 8, 2, 6])
        mv = sb("mv", [P, 8, 2])
        var = sb("var", [P, 8])
        rs = sb("rs", [P, 8])
        nt = sb("nt", [P, 2, 8])
        wr = sb("wr", [P, KT, NEXP])
        br = sb("br", [P, NEXP])
        lg = sb("lg", [P, T, NEXP])
        m8 = sb("m8", [P, T, 8])
        i8 = sb("i8", [P, T, 8], U32)
        i8f = sb("i8f", [P, T, 2])
        oh = sb("oh", [P, T, 2, NEXP])
        g2 = sb("g2", [P, T, 3])
        comb = sb("comb", [P, T, NEXP])
        routed = sb("routed", [P, T, NEXP])
        rank = sb("rank", [P, T, NEXP])
        cnt = sb("cnt", [P, NEXP])
        cmax = sb("cmax", [P, 1])
        more = sb("more", [P, 1], I32)

        bank = [ctx.enter_context(nc.psum_tensor(f"bank{i}", [P, CH], F32)) for i in range(2)]
        hid_ps = ctx.enter_context(nc.psum_tensor("bank23", [P, T, CH], F32))
        bank += [hid_ps[:, t, :] for t in range(T)]
        bank += [ctx.enter_context(nc.psum_tensor(f"bank{i}", [P, CH], F32)) for i in range(4, 8)]

        ident = cst[:, K_ID:K_ID + P]
        causal = cst[:, K_CAUSAL:K_CAUSAL + 384]
        causalT = cst[:, K_CAUSALT:K_CAUSALT + 384]
        iota = cst[:, K_IOTA:K_IOTA + P]
        triu = cst[:, K_TRIU:K_TRIU + P]
        ones = cst[:, K_ONES:K_ONES + SEQ]
        eps = cst[:, K_EPS:K_EPS + 1]
        one = cst[:, K_ONES:K_ONES + 1]

        in_x, in_const, in_rows, in_ln = sem("in_x"), sem("in_const"), sem("in_rows"), sem("in_ln")
        stored = sem("stored")
        xs_hi, xs_lo = sem("xs_hi"), sem("xs_lo")
        slot_full = [sem(f"slot_full{i}") for i in range(NSLOT)]
        dstep = sem("dstep")
        xt_mm, xt_ready = sem("xt_mm"), sem("xt_ready")
        x_ready = sem("x_ready")
        proj_mm, proj_ev = layer_sem("proj_mm"), layer_sem("proj_ev")
        gate_mm, gate_ev = layer_sem("gate_mm"), layer_sem("gate_ev")
        qk_mm, qk_ev = layer_sem("qk_mm"), layer_sem("qk_ev")
        conv_y, conv_ok = layer_sem("conv_y"), layer_sem("conv_ok")
        var_ok, ln_v, rs_ok = layer_sem("var_ok"), layer_sem("ln_v"), layer_sem("rs_ok")
        roped, dup_ok = layer_sem("roped"), layer_sem("dup_ok")
        itr_mm, itr_ev = layer_sem("itr_mm"), layer_sem("itr_ev")
        idx_mm, idx_ev, idx_used = layer_sem("idx_mm"), layer_sem("idx_ev"), layer_sem("idx_used")
        atr_mm, atr_ev = layer_sem("atr_mm"), layer_sem("atr_ev")
        gate_row, gtr_mm, gtr_ev = layer_sem("gate_row"), layer_sem("gtr_mm"), layer_sem("gtr_ev")
        vo_mm, v_ev, o_ev = layer_sem("vo_mm"), layer_sem("v_ev"), layer_sem("o_ev")
        mrow_mm, mls_mm, ml_e, ml_d, ml_p, num_mm, mix_ml = (
            layer_sem(n) for n in ("mrow_mm", "mls_mm", "ml_e", "ml_d", "ml_p", "num_mm", "mix_ml"))
        sc_mm, sc_max, sc_exp, ptr_mm, pt_ok, pv_mm, mix_at = (
            layer_sem(n) for n in ("sc_mm", "sc_max", "sc_exp", "ptr_mm", "pt_ok", "pv_mm", "mix_at"))
        mtr_mm, mtr_ev, op_mm = layer_sem("mtr_mm"), layer_sem("mtr_ev"), layer_sem("op_mm")
        half_read = layer_sem("half_read")
        hi_ok, lo_ok, w_read = sem("hi_ok"), sem("lo_ok"), sem("w_read")
        g_silu, h_ok, ht_mm, ht_hi, ht_lo = (sem(n) for n in ("g_silu", "h_ok", "ht_mm", "ht_hi", "ht_lo"))
        rt_mm, rt_diff, rt_exp, rt_mask, rk_mm, more_ok = (
            sem(n) for n in ("rt_mm", "rt_diff", "rt_exp", "rt_mask", "rk_mm", "more_ok"))
        rank_ok = sem("rank_ok")
        Y0, GA0, ST0 = T, 1, 1
        BACK = (6, 7, 1, 3)
        sel_ok, ga_mm, ga_hi, ga_lo, st_mm, st_ev, eo_lo, eo_hi, back_mm, y_add = (
            sem(n) for n in ("sel_ok", "ga_mm", "ga_hi", "ga_lo", "st_mm", "st_ev", "eo_lo", "eo_hi", "back_mm", "y_add"))

        def by_k(m, r0, c0, c1, k):
            return m[r0:r0 + k * P, c0:c1].rearrange("(k p) n -> p k n", p=P), k, c1 - c0

        DENSE = [(c, min(CH, FF_DENSE - c)) for c in range(0, FF_DENSE, CH)]
        UNITS = FF_EXPERT // CH
        stream, FIRST_IN, FIRST_OUT = [], [], []

        def add(chunk, read):
            stream.append((*chunk, read))

        n_dense = 0
        for l in range(DEPTH):
            m = w_in[l]
            FIRST_IN.append(len(stream))
            for c in range(2):
                c0 = C_GATE + c * CH
                add(by_k(m, 0, c0, c0 + CH, 4), (half_read[l], c + 1))
                add(by_k(m, CH, c0, c0 + CH, 4), (proj_mm[l], 2 * (c + 1)))
            add(by_k(m, 0, C_GATE + 2 * CH, C_END, KT), (proj_mm[l], 6))
            for i in range(4):
                add(by_k(m, 0, C_MQ + i * SEQ, C_MQ + (i + 1) * SEQ, KT), (qk_mm[l], i + 1))
            for c in range(2):
                c0 = C_MV + c * CH
                add(by_k(m, 0, c0, c0 + CH, 4), (half_read[l], c + 3))
                add(by_k(m, CH, c0, c0 + CH, 4), (vo_mm[l], 2 * (c + 1)))
            FIRST_OUT.append(len(stream))
            for i in range(4):
                add(by_k(w_out[l], i * 2 * P, 0, D, 2), (half_read[l], 5 + i) if i < 3 else (op_mm[l], 4))
            if l == 0:
                FIRST_DENSE = len(stream)
                downs = []
                for c, w in DENSE:
                    for m in (ffn_gate[0], ffn_up[0]):
                        parts = [(0, 4), (CH, 4)] if w == CH else [(0, KT)]
                        for r0, k in parts:
                            n_dense += 1
                            add(by_k(m, r0, c, c + w, k), (lo_ok, n_dense))
                    for d in downs:
                        n_dense += 1
                        add(d, (lo_ok, n_dense))
                    v = ffn_down[0, c:c + w, :].rearrange("(p j) n -> p j n", p=P)
                    downs = [(v[:, j:j + 2, :], 2, D) for j in range(0, w // P, 2)]
                for d in downs:
                    n_dense += 1
                    add(d, (lo_ok, n_dense))
        N_STREAM, N_DENSE = len(stream), n_dense

        def slot_view(s, k, n):
            return ring[:, s, 0:k * n].rearrange("p (k n) -> p k n", k=k)

        def chunk_view(n):
            return slot_view(n % NSLOT, stream[n][1], stream[n][2])

        def wait_chunk(eng, n):
            eng.wait_ge(slot_full[n % NSLOT], 16 * (n // NSLOT + 1))

        TURN = 2
        TURNS = NEXP // TURN
        ORDER = []
        for j in range(TURN):
            for c in range(UNITS + 1):
                for part in ("gate", "up") if c < UNITS else ():
                    ORDER += [(j, c, part, 0), (j, c, part, 1)]
                if c:
                    ORDER += [(j, c - 1, "down", 0), (j, c - 1, "down", 1)]
        PER_TURN = len(ORDER)
        assert PER_TURN % NSLOT == 0 and PER_TURN % NSPLIT == 0
        FILLS = PER_TURN // NSLOT
        wg_v = moe_gate.rearrange("a e (k p) f -> p (a e) k f", p=P)
        wu_v = moe_up.rearrange("a e (k p) f -> p (a e) k f", p=P)
        wd_v = moe_down.rearrange("a e (c p j) n -> p (a e) c j n", p=P, j=CH // P)

        class Run:

            def __init__(self, first, split0, shapes, it=0):
                self.first, self.split0, self.shapes, self.it = first, split0, shapes, it

            def raw(self, i):
                return ring[:, (self.first + i) % NSLOT, :]

            def parts(self, i):
                k, n = self.shapes[i]
                return [split[:, (self.split0 + i) % NSPLIT, h, 0:k * n].rearrange("p (k n) -> p k n", k=k)
                        for h in range(2)]

            def wait_full(self, eng, i):
                n = self.first + i
                eng.wait_ge(slot_full[n % NSLOT], self.it * (16 * FILLS) + 16 * (n // NSLOT + 1))

            def count(self, i):
                return self.it * PER_TURN + (self.split0 + i)

        def dense_run():
            return Run(FIRST_DENSE, 0, [stream[FIRST_DENSE + i][1:3] for i in range(N_DENSE)])

        def turn_run(it):
            return Run(N_STREAM, N_DENSE, [(2, D) if o[2] == "down" else (4, CH) for o in ORDER], it)

        def dense_stops():
            i, stops = 0, []
            for c in range(len(DENSE) + 1):
                for part in ("gate", "up") if c < len(DENSE) else ():
                    n = 2 if DENSE[c][1] == CH else 1
                    stops.append((part, c, list(range(i, i + n))))
                    i += n
                if c:
                    n = 2 if DENSE[c - 1][1] == CH else 1
                    stops.append(("down", c - 1, list(range(i, i + n))))
                    i += n
            return stops

        def turn_stops(j):
            i, stops = j * PER_TURN // TURN, []
            for c in range(UNITS + 1):
                for part in ("gate", "up") if c < UNITS else ():
                    stops.append((part, c, [i, i + 1]))
                    i += 2
                if c:
                    stops.append(("down", c - 1, [i, i + 1]))
                    i += 2
            return stops

        block = ctx.enter_context(nc.Block())

        def hidden_banks(tiles, w):
            return hid_ps[:, 0:tiles, 0:w * P].rearrange("p t (j n) -> p t j n", j=w)

        @block.sync
        def _(sp):
            sp.dma_start(x_tok[:], x[0].rearrange("(t p) n -> p t n", p=P)).then_inc(in_x, 16)
            for n, (src, _, _, _) in enumerate(stream):
                if n >= NSLOT:
                    sp.wait_ge(*stream[n - NSLOT][3])
                sp.dma_start(chunk_view(n), src).then_inc(slot_full[n % NSLOT], 16)

            def turn(it, pair):
                for i, (j, c, part, half) in enumerate(ORDER):
                    e = bass.ds(pair * TURN + j, 1)
                    n = N_STREAM + i
                    if isinstance(it, int) and i < NSLOT:
                        sp.wait_ge(*stream[n - NSLOT][3])
                    else:
                        sp.wait_ge(lo_ok, it * PER_TURN + (N_DENSE + i - NSLOT + 1))
                    if part == "down":
                        src, k, w = wd_v[:, e, c, 2 * half:2 * half + 2], 2, D
                    else:
                        m = wg_v if part == "gate" else wu_v
                        src, k, w = m[:, e, 4 * half:4 * half + 4, c * CH:(c + 1) * CH], 4, CH
                    sp.dma_start(slot_view(n % NSLOT, k, w), src.rearrange("p a k n -> p (a k) n")
                                 ).then_inc(slot_full[n % NSLOT], 16)

            turn(0, 0)
            with sp.Fori(1, TURNS) as i:
                turn(i, i)
            sp.wait_ge(more_ok, 1)
            again = sp.value_load(more[0:1, 0:1], min_val=0, max_val=1)
            with sp.If(again > 0):
                with sp.Fori(0, TURNS) as i:
                    turn(i + TURNS, i)
            for t in range(T):
                sp.wait_ge(x_ready, 3 * T + t + 1)
                sp.dma_start(out[0, t * P:(t + 1) * P, :], x_tok[:, t, :]).then_inc(stored, 16)
            sp.wait_ge(stored, 16 * T)

        @block.gpsimd
        def _(pool):
            pool.dma_start(cst[:], consts).then_inc(in_const, 16)
            pool.dma_start(feat[:], feat_params.rearrange("l p n -> p l n")).then_inc(in_const, 16)
            pool.dma_start(rows[:], row_params.partition_broadcast(P)).then_inc(in_rows, 16)
            pool.dma_start(br[:], b_router.rearrange("a n -> (a n)").partition_broadcast(P)).then_inc(in_rows, 16)
            pool.dma_start(wr[:], w_router[0].rearrange("(k p) n -> p k n", p=P)).then_inc(in_rows, 16)
            for l in range(DEPTH):
                if l:
                    pool.wait_ge(x_ready, 2 * l * T)
                pool.dma_start(ln[:], ln_params[l, 0:2].partition_broadcast(P)).then_inc(in_ln, 16)
                pool.wait_ge(roped[l], 1)
                for t in range(T):
                    pool.tensor_copy(ikdup[:, t], att[:, t, A_IK:A_IW].unsqueeze(1).to_broadcast([P, 2, AT_D])
                                     ).then_inc(dup_ok[l], 1)
                pool.wait_ge(roped[l], 2)
                for t in range(T):
                    k = att[:, t, A_K:A_V].rearrange("p (g n) -> p g n", g=AT_KV)
                    pool.tensor_copy(kdup[:, t], k.unsqueeze(2).to_broadcast([P, AT_KV, 2, AT_D])
                                     ).then_inc(dup_ok[l], 1)
                pool.wait_ge(x_ready, (2 * l + 1) * T)
                pool.dma_start(ln[:], ln_params[l, 2:4].partition_broadcast(P)).then_inc(in_ln, 16)

        @block.tensor
        def _(pe):
            mm = nc.tensor.matmul
            tr = nc.tensor.transpose

            def x_transposes(stage):
                for t in range(T):
                    if stage:
                        pe.wait_ge(x_ready, (stage - 1) * T + t + 1)
                    elif t == 0:
                        pe.wait_ge(in_x, 16)
                        pe.wait_ge(in_const, 32)
                    for h in range(2):
                        for j in range(4):
                            k = 4 * h + j
                            i = tr(bank[4 + 2 * t + h][:, j * P:(j + 1) * P], x_tok[:, t, k * P:(k + 1) * P], ident)
                        i.then_inc(xt_mm, 1)

            def token_halves(l, n, banks, done, waits=()):
                for half in range(2):
                    wait_chunk(pe, n + half)
                    w = chunk_view(n + half)
                    for t in range(T):
                        if half == 0 and waits:
                            pe.wait_ge(*waits[t])
                        for j in range(4):
                            i = mm(banks[t][:, :], xT[:, 4 * half + j, t * P:(t + 1) * P], w[:, j, :],
                                   start=half == 0 and j == 0, stop=half == 1 and j == 3)
                        if half:
                            i.then_inc(done, 1)
                    if not half:
                        i.then_inc(half_read[l], 1)

            def feature_pairs(l, n, first):
                for pair in range(2):
                    wait_chunk(pe, n + pair)
                    w = chunk_view(n + pair)
                    j = first + pair
                    if j >= 2:
                        pe.wait_ge(qk_ev[l], j - 1)
                    for f in range(2):
                        for k in range(KT):
                            i = mm(bank[5 + j % 2][:, f * SEQ:(f + 1) * SEQ], w[:, k, f * P:(f + 1) * P],
                                   xT[:, k, :], start=k == 0, stop=k == KT - 1)
                    i.then_inc(qk_mm[l], 1)

            def attention(l):
                c0 = FIRST_IN[l]
                pe.wait_ge(xt_ready, 4 * (l + 1))
                for c in range(2):
                    token_halves(l, c0 + 2 * c, bank[2 * c:2 * c + 2], proj_mm[l])
                pe.wait_ge(proj_ev[l], T)
                for m in range(2):
                    for t in range(T):
                        i = tr(bank[4][0:ML_H, m * SEQ + t * P:m * SEQ + (t + 1) * P],
                               att[:, t, m * ML_H:(m + 1) * ML_H], ident)
                i.then_inc(gate_mm[l], 1)
                wait_chunk(pe, c0 + 4)
                for t in range(T):
                    w = chunk_view(c0 + 4)
                    for k in range(KT):
                        i = mm(bank[t][:, 0:w.shape[2]], xT[:, k, t * P:(t + 1) * P], w[:, k, :],
                               start=k == 0, stop=k == KT - 1)
                    i.then_inc(proj_mm[l], 1)
                feature_pairs(l, c0 + 5, 0)
                pe.wait_ge(proj_ev[l], 6)
                pe.wait_ge(roped[l], 1)
                for f in range(2):
                    for t in range(T):
                        i = tr(bank[0][:, f * SEQ + t * P:f * SEQ + (t + 1) * P],
                               att[:, t, A_IQ + f * P:A_IQ + (f + 1) * P], ident)
                i.then_inc(itr_mm[l], 1)
                pe.wait_ge(dup_ok[l], T)
                for t in range(T):
                    i = tr(bank[1][:, t * P:(t + 1) * P], ikdup[:, t].rearrange("p c n -> p (c n)"), ident)
                i.then_inc(itr_mm[l], 1)
                feature_pairs(l, c0 + 7, 2)
                pe.wait_ge(itr_ev[l], 2)
                for h in range(IDX_H):
                    a = AT_D * (h % 2)
                    for t in range(T):
                        o = (0, P)[t]
                        i = mm(bank[h][:, o:o + (t + 1) * P], iqT[a:a + AT_D, h // 2, t * P:(t + 1) * P],
                               ikT[a:a + AT_D, 0:(t + 1) * P], start=True, stop=True)
                    i.then_inc(idx_mm[l], 1)
                pe.wait_ge(dup_ok[l], 2 * T)
                pe.wait_ge(gate_ev[l], 2)
                pe.wait_ge(qk_ev[l], 4)
                for f in range(4):
                    for t in range(T):
                        i = tr(bank[4 + f // 2][:, (f % 2) * SEQ + t * P:(f % 2) * SEQ + (t + 1) * P],
                               att[:, t, A_Q + f * P:A_Q + (f + 1) * P], ident)
                    if f % 2:
                        i.then_inc(atr_mm[l], 1)
                for g in range(AT_KV):
                    for t in range(T):
                        i = tr(bank[6][:, g * SEQ + t * P:g * SEQ + (t + 1) * P],
                               kdup[:, t, g].rearrange("p c n -> p (c n)"), ident)
                i.then_inc(atr_mm[l], 1)
                pe.wait_ge(gate_row[l], 1)
                for m, r in enumerate((0, 2)):
                    for t in range(T):
                        i = tr(bank[7][:, (2 * m + t) * ML_H:(2 * m + t + 1) * ML_H],
                               gate[0:ML_H, r, t * P:(t + 1) * P], cst[0:ML_H, K_ID:K_ID + ML_H])
                i.then_inc(gtr_mm[l], 1)
                pe.wait_ge(idx_ev[l], IDX_H)
                for c in range(2):
                    token_halves(l, c0 + 9 + 2 * c, bank[2 * c:2 * c + 2], vo_mm[l])
                pe.wait_ge(atr_ev[l], 3)
                for h in range(ML_H):
                    i = mm(bank[4 + h // 2][:, (h % 2) * SEQ:(h % 2 + 1) * SEQ],
                           cst[0:ML_H, K_SEL + h * P:K_SEL + (h + 1) * P], gate[0:ML_H, 1, :], start=True, stop=True)
                    if h % 2:
                        i.then_inc(mrow_mm[l], 1)
                pe.wait_ge(conv_ok[l], 2)
                pe.wait_ge(gtr_ev[l], 2)
                for h in range(ML_H):
                    if h >= 2:
                        pe.wait_ge(ml_p[l], h - 1)
                    mm(bank[6 + h % 2][:, 0:SEQ], qk[:, ML_H + h, 0:P], qk[:, h, :], start=True, stop=True)
                    mm(bank[6 + h % 2][:, SEQ:SEQ + P], qk[:, ML_H + h, P:SEQ], qk[:, h, P:SEQ],
                       start=True, stop=True).then_inc(mls_mm[l], 1)
                pe.wait_ge(v_ev[l], T)
                pe.wait_ge(o_ev[l], T)
                for h in range(ML_H):
                    pe.wait_ge(ml_p[l], h + 1)
                    a = (h % 2) * (ML_D + 1)
                    mm(bank[h // 2][:, a:a + ML_D + 1], mld[:, h, 0:P], v_aug[:, 0, h, :], start=True, stop=True)
                    o = bank[2 + h // 2][:, a:a + ML_D + 1]
                    mm(o, mld[:, h, P:2 * P], v_aug[:, 0, h, :], start=True, stop=False)
                    mm(o, mld[:, h, 2 * P:3 * P], v_aug[:, 1, h, :], start=False, stop=True).then_inc(num_mm[l], 1)

                def scores(h):
                    a = AT_D * (h % 2)
                    if h >= 4:
                        pe.wait_ge(sc_max[l], h - 3)
                    for t in range(T):
                        o = (0, P)[t]
                        i = mm(bank[4 + h % 4][:, o:o + (t + 1) * P], aqT[a:a + AT_D, h // 2, t * P:(t + 1) * P],
                               akT[a:a + AT_D, h // (AT_H // AT_KV), 0:(t + 1) * P], start=True, stop=True)
                    i.then_inc(sc_mm[l], 1)

                def prob_transposes(h):
                    pe.wait_ge(sc_exp[l], h + 1)
                    if h >= 2:
                        pe.wait_ge(pt_ok[l], h - 1)
                    for j in range(3):
                        i = tr(bank[2 + h % 2][:, j * P:(j + 1) * P], probs[:, h % 3, j * P:(j + 1) * P], ident)
                    i.then_inc(ptr_mm[l], 1)

                def values(h):
                    pe.wait_ge(pt_ok[l], h + 1)
                    v = A_V + AT_D * (h // (AT_H // AT_KV))
                    o = slice(h * AT_D, (h + 1) * AT_D)
                    pT = probsT[:, h % 3]
                    mm(bank[0][:, o], pT[:, 0:P], att[:, 0, v:v + AT_D], start=True, stop=True)
                    mm(bank[1][:, o], pT[:, P:2 * P], att[:, 0, v:v + AT_D], start=True, stop=False)
                    mm(bank[1][:, o], pT[:, 2 * P:3 * P], att[:, 1, v:v + AT_D], start=False, stop=True
                       ).then_inc(pv_mm[l], 1)

                pe.wait_ge(ml_p[l], ML_H)
                for h in range(AT_H + 2):
                    if h < AT_H:
                        scores(h)
                    if h == 1:
                        pe.wait_ge(mix_ml[l], 1)
                    if 1 <= h <= AT_H:
                        prob_transposes(h - 1)
                    if h >= 2:
                        values(h - 2)
                pe.wait_ge(mix_at[l], 1)
                for t in range(T):
                    for h in range(2):
                        for j in range(4):
                            k = 4 * h + j
                            i = tr(bank[4 + 2 * t + h][:, j * P:(j + 1) * P], mix[:, t, k * P:(k + 1) * P], ident)
                        i.then_inc(mtr_mm[l], 1)
                pe.wait_ge(mtr_ev[l], 4)
                for q in range(4):
                    n = FIRST_OUT[l] + q
                    wait_chunk(pe, n)
                    for g in range(4):
                        t, c = divmod(g, 2)
                        for j in range(2):
                            k = 2 * q + j
                            i = mm(bank[g][:, :], mixT[:, k, t * P:(t + 1) * P],
                                   chunk_view(n)[:, j, c * CH:(c + 1) * CH], start=k == 0, stop=k == KT - 1)
                        if q == 3:
                            i.then_inc(op_mm[l], 1)
                    if q < 3:
                        i.then_inc(half_read[l], 1)
                x_transposes(2 * l + 1)

            def product(o, run, i, a, k, cols, first, last):
                hi, lo = run.parts(i)
                for kk in range(k):
                    ah, al = a(kk)
                    mm(o, ah, hi[:, kk, cols], start=first and kk == 0, stop=False)
                    mm(o, ah, lo[:, kk, cols], start=False, stop=False)
                    r = mm(o, al, hi[:, kk, cols], start=False, stop=last and kk == k - 1)
                return r

            def units(run, stops, base, n_units, tiles, x_of, width):
                def transposes(u):
                    pe.wait_ge(h_ok, base + (u + 1))
                    w = width(u)
                    for t in range(tiles):
                        h = hid[:, t, 0:w].rearrange("p (f j) -> p j f", j=w // P)
                        for j in range(w // P):
                            i = tr(bank[2 + t][:, j * P:(j + 1) * P], h[:, j, :], ident)
                    i.then_inc(ht_mm, 1)

                for part, u, chunks in stops:
                    w = width(u)
                    if part == "down" and u == n_units - 1:
                        transposes(u)
                    if part == "gate":
                        pe.wait_ge(g_silu, base + u)
                    elif part == "up":
                        if u:
                            pe.wait_ge(ht_lo, base + u)
                        else:
                            pe.wait_ge(h_ok, base + u)
                    else:
                        pe.wait_ge(ht_lo, base + (u + 1))
                    for n, i in enumerate(chunks):
                        pe.wait_ge(lo_ok, run.count(i + 1))
                        k = run.shapes[i][0]
                        for t in range(tiles):
                            if part == "down":
                                for half in range(2):
                                    r = product(bank[4 + 2 * t + half][:, :], run, i,
                                                lambda kk: [hs[:, t, m, 2 * n + kk, :] for m in range(2)], k,
                                                slice(half * CH, (half + 1) * CH), u == 0 and n == 0,
                                                u == n_units - 1 and n == len(chunks) - 1)
                            else:
                                r = product(bank[(0 if part == "gate" else 2) + t][:, 0:w], run, i,
                                            lambda kk: x_of(t, 4 * n + kk), k, slice(0, w), n == 0,
                                            n == len(chunks) - 1)
                        r.then_inc(w_read, 1)
                        if part == "gate" and n == 0 and u:
                            transposes(u - 1)

            def dense():
                pe.wait_ge(xs_lo, 4)
                units(dense_run(), dense_stops(), 0, len(DENSE), T,
                      lambda t, k: [xs[:, m, k, t * P:(t + 1) * P] for m in range(2)], lambda u: DENSE[u][1])
                x_transposes(2)

            def router():
                pe.wait_ge(xt_ready, 12)
                pe.wait_ge(in_rows, 48)
                for t in range(T):
                    for k in range(KT):
                        i = mm(bank[0][:, t * NEXP:(t + 1) * NEXP], xT[:, k, t * P:(t + 1) * P], wr[:, k, :],
                               start=k == 0, stop=k == KT - 1)
                i.then_inc(rt_mm, 1)
                pe.wait_ge(rt_mask, 1)
                mm(bank[1][:, 0:8], triu, routed[:, 0, :], start=True, stop=True).then_inc(ga_mm, GA0)
                mm(bank[1][:, 8:16], ones[:, 0:P], routed[:, 0, :], start=True, stop=False)
                mm(bank[1][:, 8:16], triu, routed[:, 1, :], start=False, stop=True).then_inc(st_mm, ST0)
                mm(bank[1][:, 16:24], ones[:, 0:P], routed[:, 0, :], start=True, stop=False)
                mm(bank[1][:, 16:24], ones[:, 0:P], routed[:, 1, :], start=False, stop=True).then_inc(rk_mm, 1)

            def experts(it):
                for j in range(TURN):
                    E = it * TURN + j
                    pe.wait_ge(sel_ok, E * 2 + 2)
                    pe.wait_ge(y_add, E * 4 + Y0)
                    for h in range(2):
                        for kk in range(4):
                            k = 4 * h + kk
                            for t in range(T):
                                i = mm(bank[6 + h][:, kk * P:(kk + 1) * P], x_tok[:, t, k * P:(k + 1) * P],
                                       sel[:, t, :], start=t == 0, stop=t == T - 1)
                        i.then_inc(ga_mm, 1)
                    for t in range(T):
                        i = tr(bank[1][:, t * P:(t + 1) * P], selc[:, t, :], ident)
                    i.then_inc(st_mm, 1)
                    pe.wait_ge(ga_lo, E * 2 + 2)
                    units(turn_run(it), turn_stops(j), it * (TURN * UNITS) + (len(DENSE) + j * UNITS), UNITS, 1,
                          lambda t, k: [xs[:, m, k, 0:P] for m in range(2)], lambda u: CH)
                    pe.wait_ge(st_ev, E + 1)
                    for half in range(2):
                        pe.wait_ge((eo_lo, eo_hi)[half], E + 1)
                        for t in range(T):
                            mm(bank[BACK[2 * half + t]][:, :], selT[:, t, :], eo[:, half * CH:(half + 1) * CH],
                               start=True, stop=True).then_inc(back_mm, 1)

            def again():
                pe.wait_ge(more_ok, 1)
                return pe.value_load(more[0:1, 0:1], min_val=0, max_val=1)

            x_transposes(0)
            attention(0)
            dense()
            attention(1)
            router()
            with pe.Fori(0, TURNS) as i:
                experts(i)
            with pe.If(again() > 0):
                with pe.Fori(0, TURNS) as i:
                    experts(i + TURNS)

        @block.scalar
        def _(act):
            copy = nc.scalar.copy

            def fn(out_, in_, f, **kw):
                return nc.scalar.activation(out_, in_, f, **kw)

            def x_evacuate(stage):
                for t in range(T):
                    for h in range(2):
                        act.wait_ge(xt_mm, 4 * stage + 2 * t + h + 1)
                        src = bank[4 + 2 * t + h][:, :].rearrange("p (k n) -> p k n", k=4)
                        k = slice(4 * h, 4 * h + 4)
                        if stage == 1:
                            copy(xs[:, 0, k, t * P:(t + 1) * P], src).then_inc(xs_hi, 1)
                        else:
                            copy(xT[:, k, t * P:(t + 1) * P], src).then_inc(xt_ready, 1)

            def rsqrt_start(l, step, n):
                act.wait_ge(var_ok[l], step + 1)
                fn(rs[:, 0:n], var[:, 0:n], ACT.Ln, bias=eps).then_inc(ln_v[l], 1)
                act.wait_ge(ln_v[l], step + 1)
                fn(rs[:, 0:n], rs[:, 0:n], ACT.Exp, scale=-0.5).then_inc(rs_ok[l], 1)

            def q_or_k(l, first):
                for j in range(first, first + 2):
                    act.wait_ge(qk_mm[l], j + 1)
                    copy(pre[:, 2 * j:2 * j + 2, CONV - 1:], bank[5 + j % 2][:, :].rearrange("p (f s) -> p f s", f=2)
                         ).then_inc(qk_ev[l], 1)

            def attention(l):
                for g in range(6):
                    c, t = divmod(g, 2)
                    w = min(CH, AW - c * CH)
                    act.wait_ge(proj_mm[l], g + 1)
                    copy(att[:, t, c * CH:c * CH + w], bank[g % 4][:, 0:w]).then_inc(proj_ev[l], 1)
                    if g == 3:
                        act.wait_ge(gate_mm[l], 1)
                        act.wait_ge(in_const, 32)
                        fn(gate[0:ML_H, 0, :], bank[4][0:ML_H, 0:SEQ], ACT.Identity,
                           bias=feat[0:ML_H, l, PC_I:PC_I + 1]).then_inc(gate_ev[l], 1)
                        fn(gate[0:ML_H, 1, :], bank[4][0:ML_H, SEQ:2 * SEQ], ACT.Identity,
                           bias=feat[0:ML_H, l, PC_F:PC_F + 1]).then_inc(gate_ev[l], 1)
                        act.wait_ge(gate_ev[l], 2)
                        fn(gate[0:ML_H, 2, :], gate[0:ML_H, 1, :], ACT.Abs).then_inc(gate_ev[l], 1)
                        act.wait_ge(gate_ev[l], 3)
                        fn(gate[0:ML_H, 2, :], gate[0:ML_H, 2, :], ACT.Exp, scale=-1.0).then_inc(gate_ev[l], 1)
                        act.wait_ge(gate_ev[l], 4)
                        fn(gate[0:ML_H, 2, :], gate[0:ML_H, 2, :], ACT.Ln, bias=cst[0:ML_H, K_ONES:K_ONES + 1]
                           ).then_inc(gate_ev[l], 1)
                rsqrt_start(l, 0, T)
                q_or_k(l, 0)
                act.wait_ge(itr_mm[l], 1)
                copy(iqT, bank[0][:, :].rearrange("p (f s) -> p f s", f=2)).then_inc(itr_ev[l], 1)
                act.wait_ge(itr_mm[l], 2)
                copy(ikT, bank[1][:, 0:SEQ]).then_inc(itr_ev[l], 1)
                q_or_k(l, 2)
                for h in range(IDX_H):
                    act.wait_ge(idx_mm[l], h + 1)
                    if h >= 2:
                        act.wait_ge(idx_used[l], h - 1)
                    fn(relu[:, h % 2, :], bank[h][:, 0:384], ACT.Relu, scale=AT_D ** -0.5 * IDX_H ** -0.5
                       ).then_inc(idx_ev[l], 1)
                for b in range(3):
                    act.wait_ge(atr_mm[l], b + 1)
                    dst = aqT[:, 2 * b:2 * b + 2] if b < 2 else akT
                    copy(dst, bank[4 + b][:, :].rearrange("p (f s) -> p f s", f=2)).then_inc(atr_ev[l], 1)
                act.wait_ge(gtr_mm[l], 1)
                copy(gT, bank[7][:, 0:T * ML_H].rearrange("p (t h) -> p t h", t=T)).then_inc(gtr_ev[l], 1)
                fn(emT, bank[7][:, T * ML_H:2 * T * ML_H].rearrange("p (t h) -> p t h", t=T), ACT.Exp, scale=-1.0
                   ).then_inc(gtr_ev[l], 1)
                for half in range(2):
                    act.wait_ge(conv_y[l], half + 1)
                    fn(qk[:, half * ML_H:(half + 1) * ML_H, :], qk[:, half * ML_H:(half + 1) * ML_H, :], ACT.Silu
                       ).then_inc(conv_ok[l], 1)
                for t in range(T):
                    act.wait_ge(vo_mm[l], t + 1)
                    copy(v_aug[:, t, :, 0:ML_D], bank[t][:, :].rearrange("p (h n) -> p h n", h=ML_H)
                         ).then_inc(v_ev[l], 1)
                for t in range(T):
                    act.wait_ge(vo_mm[l], T + t + 1)
                    fn(og[:, t, :], bank[2 + t][:, :], ACT.Exp, scale=-1.0).then_inc(o_ev[l], 1)
                for h in range(ML_H):
                    act.wait_ge(ml_e[l], h + 1)
                    fn(mld[:, h, :], mld[:, h, :], ACT.Exp).then_inc(ml_d[l], 1)
                rsqrt_start(l, 1, T * ML_H)
                for h in range(AT_H):
                    act.wait_ge(sc_max[l], h + 1)
                    for t in range(T):
                        o = slice(0, P) if t == 0 else slice(P, 3 * P)
                        i = fn(probs[:, h % 3, o], probs[:, h % 3, o], ACT.Exp, scale=AT_D ** -0.5,
                               bias=nmax[:, h % 3, t:t + 1], accum_out=rsum[:, t, h:h + 1])
                    i.then_inc(sc_exp[l], 1)
                for t in range(T):
                    for h in range(2):
                        g = 2 * t + h
                        act.wait_ge(mtr_mm[l], g + 1)
                        copy(mixT[:, 4 * h:4 * h + 4, t * P:(t + 1) * P],
                             bank[4 + g][:, :].rearrange("p (k n) -> p k n", k=4)).then_inc(mtr_ev[l], 1)
                rsqrt_start(l, 2, T)
                x_evacuate(2 * l + 1)

            def split_hi(run, i):
                run.wait_full(act, i)
                if run.split0 + i >= NSPLIT:
                    act.wait_ge(w_read, run.count(i - NSPLIT + 1))
                k, n = run.shapes[i]
                copy(run.parts(i)[0], run.raw(i)[:, 0:k * n].rearrange("p (k n) -> p k n", k=k)).then_inc(hi_ok, 1)

            def units(run, stops, base, n_units, tiles, width, last):
                def hidden(u):
                    act.wait_ge(ht_mm, base + (u + 1))
                    w = width(u) // P
                    copy(hs[:, 0:tiles, 0, 0:w, :], hidden_banks(tiles, w)).then_inc(ht_hi, 1)

                for part, u, chunks in stops:
                    if part == "down" and u == n_units - 1:
                        hidden(u)
                    for n, i in enumerate(chunks):
                        if i + 2 < last:
                            split_hi(run, i + 2)
                        if part == "gate" and n == 0 and u:
                            hidden(u - 1)
                    if part == "gate":
                        act.wait_ge(w_read, run.count(chunks[-1] + 1))
                        w = width(u)
                        for t in range(tiles):
                            f = fn(silu[:, t, 0:w], bank[t][:, 0:w], ACT.Silu)
                        f.then_inc(g_silu, 1)

            def dense():
                run = dense_run()
                units(run, dense_stops(), 0, len(DENSE), T, lambda u: DENSE[u][1], N_DENSE)
                rsqrt_start(0, 3, T)
                x_evacuate(2)

            def experts(it):
                run = turn_run(it)
                for i in range(2):
                    split_hi(run, i)
                for j in range(TURN):
                    E = it * TURN + j
                    for h in range(2):
                        act.wait_ge(ga_mm, E * 2 + (GA0 + h + 1))
                        copy(xs[:, 0, 4 * h:4 * h + 4, 0:P], bank[6 + h][:, :].rearrange("p (k n) -> p k n", k=4)
                             ).then_inc(ga_hi, 1)
                    act.wait_ge(st_mm, E + (ST0 + 1))
                    copy(selT, bank[1][:, 0:SEQ].rearrange("p (t n) -> p t n", t=T)).then_inc(st_ev, 1)
                    units(run, turn_stops(j), it * (TURN * UNITS) + (len(DENSE) + j * UNITS), UNITS, 1,
                          lambda u: CH, PER_TURN)
                    act.wait_ge(w_read, run.count((j + 1) * PER_TURN // TURN))
                    copy(eo[:, 0:CH], bank[4][:, :]).then_inc(eo_lo, 1)

            x_evacuate(0)
            attention(0)
            for i in range(2):
                split_hi(dense_run(), i)
            dense()
            attention(1)
            act.wait_ge(rt_diff, 1)
            fn(g2[:, :, 0:1], g2[:, :, 0:1], ACT.Exp).then_inc(rt_exp, 1)
            with act.Fori(0, TURNS) as i:
                experts(i)
            act.wait_ge(more_ok, 1)
            again = act.value_load(more[0:1, 0:1], min_val=0, max_val=1)
            with act.If(again > 0):
                with act.Fori(0, TURNS) as i:
                    experts(i + TURNS)
            rsqrt_start(1, 3, T)

        @block.vector
        def _(dve):
            ts, tt, stt = nc.vector.tensor_scalar, nc.vector.tensor_tensor, nc.vector.scalar_tensor_tensor
            steps = [0]

            def step(i):
                i.then_inc(dstep, 1)
                steps[0] += 1
                return steps[0]

            def after(n):
                dve.wait_ge(dstep, n)

            def link(i):
                after(step(i))

            def rsqrt_finish(l, n_step, n):
                dve.wait_ge(rs_ok[l], n_step + 1)
                v, r, a, b = var[:, 0:n], rs[:, 0:n], nt[:, 0, 0:n], nt[:, 1, 0:n]
                link(stt(a, v, eps, r, ALU.add, ALU.mult))
                link(stt(b, a, -0.5, r, ALU.mult, ALU.mult))
                link(stt(r, b, 1.5, r, ALU.add, ALU.mult))

            def layer_norm(l, which, src):
                for t in range(T):
                    for h in range(2):
                        s = step(nc.vector.bn_stats(stats[:, t, h, :], src[:, t, h * CH:(h + 1) * CH]))
                after(s)
                for t in range(T):
                    s = step(nc.vector.bn_aggr(mv[:, t, :], stats[:, t]))
                after(s)
                nc.vector.tensor_copy(var[:, 0:T], mv[:, 0:T, 1]).then_inc(var_ok[l], 1)
                dve.wait_ge(var_ok[l], 3 + which)
                rsqrt_finish(l, 2 + which, T)
                dve.wait_ge(in_ln, 16 * (2 * l + which + 1))
                for t in range(T):
                    link(ts(x_tok[:, t], src[:, t], mv[:, t, 0:1], rs[:, t:t + 1], ALU.subtract, ALU.mult))
                    link(tt(x_tok[:, t], x_tok[:, t], ln[:, 0], ALU.mult))
                    tt(x_tok[:, t], x_tok[:, t], ln[:, 1], ALU.add).then_inc(x_ready, 1)
                dve.wait_ge(x_ready, (2 * l + which + 1) * T)

            def rotate(l, h0, n):
                heads = att[:, :, A_Q:A_IW].rearrange("p t (h n) -> p t h n", n=AT_D)[:, :, h0:h0 + n]
                x1, x2 = heads[:, :, :, 0:ROT], heads[:, :, :, ROT:2 * ROT]
                table = [cst[:, a:a + T * ROT].rearrange("p (t r) -> p t r", t=T).unsqueeze(2)
                         .to_broadcast([P, T, n, ROT]) for a in (K_COS, K_SIN)]
                r = [b[:, :, 0:n, :] for b in rope]
                for i, (a, b) in enumerate(((x1, 0), (x2, 1), (x2, 0), (x1, 1))):
                    s = step(tt(r[i], a, table[b], ALU.mult))
                after(s)
                step(tt(x1, r[0], r[1], ALU.subtract))
                after(steps[0])
                tt(x2, r[2], r[3], ALU.add).then_inc(roped[l], 1)
                dve.wait_ge(roped[l], 1 if h0 else 2)

            def conv(l, half):
                dve.wait_ge(qk_ev[l], 2 * half + 2)
                f0 = half * ML_H
                for j in range(CONV):
                    for f in range(f0, f0 + ML_H):
                        w = feat[:, l, PC_W + f * CONV + j:PC_W + f * CONV + j + 1]
                        if j == 0:
                            s = step(ts(qk[:, f], pre[:, f, 0:SEQ], w, feat[:, l, PC_B + f:PC_B + f + 1],
                                        ALU.mult, ALU.add))
                        elif j < CONV - 1 or f < f0 + ML_H - 1:
                            after(s - ML_H + 1)
                            s = step(stt(qk[:, f], pre[:, f, j:j + SEQ], w, qk[:, f], ALU.mult, ALU.add))
                        else:
                            after(s)
                            stt(qk[:, f], pre[:, f, j:j + SEQ], w, qk[:, f], ALU.mult, ALU.add
                                ).then_inc(conv_y[l], 1)

            def index_norm(l):
                ik = [att[:, t, A_IK:A_IW] for t in range(T)]
                for t in range(T):
                    s = step(nc.vector.bn_stats(stats[:, t, 0, :], ik[t]))
                after(s)
                for t in range(T):
                    s = step(nc.vector.bn_aggr(mv[:, t, :], stats[:, t, 0]))
                after(s)
                nc.vector.tensor_copy(var[:, 0:T], mv[:, 0:T, 1]).then_inc(var_ok[l], 1)
                dve.wait_ge(var_ok[l], 1)
                rsqrt_finish(l, 0, T)
                dve.wait_ge(in_rows, 48)
                for t in range(T):
                    link(ts(ik[t], ik[t], mv[:, t, 0:1], rs[:, t:t + 1], ALU.subtract, ALU.mult))
                    link(tt(ik[t], ik[t], rows[:, l, AR_IG:AR_IB], ALU.mult))
                    link(tt(ik[t], ik[t], rows[:, l, AR_IB:AR_END], ALU.add))

            def gates(l):
                r = [gate[0:ML_H, i, :] for i in range(4)]
                dve.wait_ge(gate_ev[l], 5)
                link(stt(r[2], r[1], 0.0, r[2], ALU.min, ALU.subtract))
                scan = nc.vector.tensor_tensor_scan
                link(scan(r[3], ones[0:ML_H], r[2], 0.0, ALU.mult, ALU.add))
                link(tt(r[0], r[0], r[3], ALU.subtract))
                link(scan(r[1], ones[0:ML_H], r[0], 0.0, ALU.mult, ALU.max))
                tt(r[2], r[3], r[1], ALU.add).then_inc(gate_row[l], 1)

            def choose(l):
                part = [slice(0, P), slice(P, 3 * P)]
                for h in range(IDX_H):
                    dve.wait_ge(idx_ev[l], h + 1)
                    for t in range(T):
                        w = att[:, t, A_IW + h:A_IW + h + 1]
                        o, r = iscore[:, part[t]], relu[:, h % 2, part[t]]
                        if h:
                            dve.wait_ge(idx_used[l], h)
                            i = stt(o, r, w, o, ALU.mult, ALU.add)
                        else:
                            i = ts(o, r, w, None, ALU.mult)
                    i.then_inc(idx_used[l], 1)
                dve.wait_ge(idx_used[l], IDX_H)
                link(tt(iscore, iscore, causal, ALU.add))
                for r in range(TOPK // 8):
                    src = iscore if r == 0 else left
                    for t in range(T):
                        if r:
                            after(steps[0] - 1)
                        step(nc.vector.max(top8[:, t], src[:, part[t]]))
                    for t in range(T):
                        after(steps[0] - 1)
                        step(nc.vector.match_replace(left[:, part[t]], top8[:, t], src[:, part[t]], TAKEN))
                after(steps[0])
                link(ts(choice, left, TAKEN, NEG, ALU.not_equal, ALU.mult))
                link(tt(choice, choice, causal, ALU.add))

            def mlstm(l):
                dve.wait_ge(gtr_ev[l], 2)
                for h in range(ML_H):
                    if h % 2 == 0:
                        dve.wait_ge(mrow_mm[l], h // 2 + 1)
                    m = bank[4 + h // 2][:, (h % 2) * SEQ:(h % 2 + 1) * SEQ]
                    stt(mld[:, h, 0:SEQ], causalT[:, 0:SEQ], gT[:, 0, h:h + 1], m, ALU.add, ALU.subtract)
                    stt(mld[:, h, SEQ:SEQ + P], causalT[:, SEQ:SEQ + P], gT[:, 1, h:h + 1], m[:, P:SEQ],
                        ALU.add, ALU.subtract).then_inc(ml_e[l], 1)
                dve.wait_ge(o_ev[l], T)
                link(ts(og, og, 1.0, None, ALU.add))
                link(nc.vector.reciprocal(og, og))
                for t in range(T):
                    step(tt(og[:, t], og[:, t], rows[:, l, AR_NG:AR_IG], ALU.mult))
                for h in range(ML_H):
                    dve.wait_ge(mls_mm[l], h + 1)
                    dve.wait_ge(ml_d[l], h + 1)
                    stt(mld[:, h], bank[6 + h % 2][:, 0:384], float(ML_D) ** -0.5, mld[:, h], ALU.mult, ALU.mult
                        ).then_inc(ml_p[l], 1)
                dve.wait_ge(num_mm[l], ML_H)
                num = [[bank[2 * t + h // 2][:, (h % 2) * (ML_D + 1):(h % 2) * (ML_D + 1) + ML_D]
                        for h in range(ML_H)] for t in range(T)]
                for t in range(T):
                    for pair in range(2):
                        den = bank[2 * t + pair][:, 0:2 * (ML_D + 1)].rearrange("p (h n) -> p h n", h=2)[:, :, ML_D]
                        d = slice(2 * pair, 2 * pair + 2)
                        link(ts(rden2[:, t, d], den, -1.0, None, ALU.mult))
                        step(tt(rden[:, t, d], den, rden2[:, t, d], ALU.max))
                    for h in range(ML_H):
                        step(nc.vector.bn_stats(stats[:, t * ML_H + h, 0, :], num[t][h]))
                after(steps[0])
                link(tt(rden, rden, emT, ALU.max))
                step(nc.vector.reciprocal(rden, rden))
                for i in range(T * ML_H):
                    step(nc.vector.bn_aggr(mv[:, i, :], stats[:, i, 0]))
                after(steps[0])
                link(tt(rden2, rden, rden, ALU.mult))
                tt(var[:, 0:T * ML_H], mv[:, :, 1], rden2.rearrange("p t h -> p (t h)"), ALU.mult
                   ).then_inc(var_ok[l], 1)
                dve.wait_ge(var_ok[l], 2)
                rsqrt_finish(l, 1, T * ML_H)
                link(tt(rs[:, :], rs[:, :], rden.rearrange("p t h -> p (t h)"), ALU.mult))
                for t in range(T):
                    for h in range(ML_H):
                        i = t * ML_H + h
                        step(ts(mix[:, t, h * ML_D:(h + 1) * ML_D], num[t][h], mv[:, i, 0:1], rs[:, i:i + 1],
                                ALU.subtract, ALU.mult))
                after(steps[0])
                step(tt(mix[:, 0, 0:ML_W], mix[:, 0, 0:ML_W], og[:, 0], ALU.mult))
                tt(mix[:, 1, 0:ML_W], mix[:, 1, 0:ML_W], og[:, 1], ALU.mult).then_inc(mix_ml[l], 1)

            def attention(l):
                link(nc.vector.memset(pre[:, :, 0:CONV - 1], 0.0))
                dve.wait_ge(proj_ev[l], 6)
                index_norm(l)
                rotate(l, (A_IQ - A_Q) // AT_D, IDX_H + 1)
                gates(l)
                rotate(l, 0, AT_H + AT_KV)
                conv(l, 0)
                choose(l)
                conv(l, 1)
                dve.wait_ge(conv_y[l], 2)
                link(nc.vector.memset(v_aug[:, :, :, ML_D:ML_D + 1], 1.0))
                mlstm(l)

                def masked(h):
                    b = h % 3
                    dve.wait_ge(sc_mm[l], h + 1)
                    if h >= 3:
                        dve.wait_ge(ptr_mm[l], h - 2)
                    for t in range(T):
                        o = slice(0, P) if t == 0 else slice(P, 3 * P)
                        s = step(nc.vector.tensor_tensor_reduce(
                            out=probs[:, b, o], in0=bank[4 + h % 4][:, o], in1=choice[:, o], scale=1.0, scalar=TAKEN,
                            op0=ALU.add, op1=ALU.max, accum_out=rmax[:, b, t:t + 1]))
                    after(s)
                    ts(nmax[:, b], rmax[:, b], -(AT_D ** -0.5), None, ALU.mult).then_inc(sc_max[l], 1)

                def transposed(h):
                    dve.wait_ge(ptr_mm[l], h + 1)
                    if h >= 3:
                        dve.wait_ge(pv_mm[l], h - 2)
                    nc.vector.tensor_copy(probsT[:, h % 3], bank[2 + h % 2][:, 0:384]).then_inc(pt_ok[l], 1)

                for h in range(AT_H + 1):
                    if h < AT_H:
                        masked(h)
                    if h:
                        transposed(h - 1)
                dve.wait_ge(pv_mm[l], AT_H)
                dve.wait_ge(sc_exp[l], AT_H)
                link(nc.vector.reciprocal(rsum, rsum))
                for t in range(T):
                    i = tt(mix[:, t, ML_W:].rearrange("p (h n) -> p h n", h=AT_H),
                           bank[t][:, :].rearrange("p (h n) -> p h n", h=AT_H),
                           rsum[:, t].unsqueeze(2).to_broadcast([P, AT_H, AT_D]), ALU.mult)
                    if t == 0:
                        step(i)
                i.then_inc(mix_at[l], 1)
                for g in range(4):
                    t, c = divmod(g, 2)
                    dve.wait_ge(op_mm[l], g + 1)
                    half = x_tok[:, t, c * CH:(c + 1) * CH]
                    s = step(stt(half, half, ALPHA, bank[g][:, :], ALU.mult, ALU.add))
                after(s)
                layer_norm(l, 0, x_tok)

            def split_lo(run, i):
                dve.wait_ge(hi_ok, run.count(i + 1))
                k, n = run.shapes[i]
                hi, lo = run.parts(i)
                tt(lo, run.raw(i)[:, 0:k * n].rearrange("p (k n) -> p k n", k=k), hi.bitcast(F32), ALU.subtract
                   ).then_inc(lo_ok, 1)

            def units(run, stops, base, n_units, tiles, width, last):
                def hidden(u):
                    dve.wait_ge(ht_hi, base + (u + 1))
                    w = width(u) // P
                    tt(hs[:, 0:tiles, 1, 0:w, :], hidden_banks(tiles, w), hs[:, 0:tiles, 0, 0:w, :].bitcast(F32),
                       ALU.subtract).then_inc(ht_lo, 1)

                for part, u, chunks in stops:
                    if part == "down" and u == n_units - 1:
                        hidden(u)
                    for n, i in enumerate(chunks):
                        if i + 2 < last:
                            split_lo(run, i + 2)
                        if part == "gate" and n == 0 and u:
                            hidden(u - 1)
                    if part == "up":
                        dve.wait_ge(g_silu, base + (u + 1))
                        dve.wait_ge(w_read, run.count(chunks[-1] + 1))
                        w = width(u)
                        for t in range(tiles):
                            i = tt(hid[:, t, 0:w], silu[:, t, 0:w], bank[2 + t][:, 0:w], ALU.mult)
                        i.then_inc(h_ok, 1)

            def dense():
                for g in range(4):
                    t, h = divmod(g, 2)
                    dve.wait_ge(xs_hi, g + 1)
                    k, n = slice(4 * h, 4 * h + 4), slice(t * P, (t + 1) * P)
                    tt(xs[:, 1, k, n], bank[4 + g][:, :].rearrange("p (k n) -> p k n", k=4),
                       xs[:, 0, k, n].bitcast(F32), ALU.subtract).then_inc(xs_lo, 1)
                run = dense_run()
                for i in range(2):
                    split_lo(run, i)
                units(run, dense_stops(), 0, len(DENSE), T, lambda u: DENSE[u][1], N_DENSE)
                dve.wait_ge(w_read, N_DENSE)
                for g in range(4):
                    t, c = divmod(g, 2)
                    half = x_tok[:, t, c * CH:(c + 1) * CH]
                    s = step(stt(half, half, ALPHA, bank[4 + g][:, :], ALU.mult, ALU.add))
                after(s)
                layer_norm(0, 1, x_tok)

            def route():
                dve.wait_ge(rt_mm, 1)
                for t in range(T):
                    s = step(tt(lg[:, t], bank[0][:, t * NEXP:(t + 1) * NEXP], br[:], ALU.add))
                after(s)
                for t in range(T):
                    s = step(nc.vector.max(m8[:, t], lg[:, t]))
                after(s)
                tt(g2[:, :, 0:1], m8[:, :, 1:2], m8[:, :, 0:1], ALU.subtract).then_inc(rt_diff, 1)
                for t in range(T):
                    s = step(nc.vector.max_index(i8[:, t], m8[:, t], lg[:, t]))
                after(s)
                link(nc.vector.tensor_copy(i8f[:, :, :], i8[:, :, 0:2]))
                for t in range(T):
                    for j in range(2):
                        s = step(ts(oh[:, t, j], iota[:, 0:NEXP], i8f[:, t, j:j + 1], None, ALU.is_equal))
                after(s)
                tt(routed[:, :, :], oh[:, :, 0], oh[:, :, 1], ALU.add).then_inc(rt_mask, 1)
                dve.wait_ge(rt_exp, 1)
                link(ts(g2[:, :, 1:2], g2[:, :, 0:1], 1.0, None, ALU.add))
                link(nc.vector.reciprocal(g2[:, :, 1:2], g2[:, :, 1:2]))
                link(tt(g2[:, :, 2:3], g2[:, :, 0:1], g2[:, :, 1:2], ALU.mult))
                for t in range(T):
                    s = step(ts(comb[:, t], oh[:, t, 0], g2[:, t, 1:2], None, ALU.mult))
                after(s)
                for t in range(T):
                    s = step(stt(comb[:, t], oh[:, t, 1], g2[:, t, 2:3], comb[:, t], ALU.mult, ALU.add))
                dve.wait_ge(rk_mm, 1)
                after(s)
                r = rank[:, :, :]
                link(stt(r, bank[1][:, 0:16].rearrange("p (t e) -> p t e", t=T), 1.0, routed[:, :, :],
                         ALU.add, ALU.mult))
                link(ts(r, r, -1.0, None, ALU.add))
                link(nc.vector.reduce_max(cmax[:], bank[1][:, 16:24], axis=AX.X))
                ts(more[:], cmax[:], float(P), None, ALU.is_gt).then_inc(more_ok, 1)
                for t in range(T):
                    ts(y[:, t], x_tok[:, t], ALPHA, None, ALU.mult).then_inc(y_add, 1)
                dve.wait_ge(y_add, Y0)

            def experts(it, pair):
                run = turn_run(it)
                for j in range(TURN):
                    E = it * TURN + j
                    e = bass.ds(pair * TURN + j, 1)
                    dve.wait_ge(ga_mm, E * 2 + GA0)
                    for t in range(T):
                        i = ts(sel[:, t], iota, rank[:, t, e], None, ALU.is_equal)
                    i.then_inc(sel_ok, 1)
                    dve.wait_ge(st_mm, E + ST0)
                    for t in range(T):
                        i = ts(selc[:, t], iota, rank[:, t, e], comb[:, t, e], ALU.is_equal, ALU.mult)
                    i.then_inc(sel_ok, 1)
                    if j == 0:
                        for i in range(2):
                            split_lo(run, i)
                    for h in range(2):
                        dve.wait_ge(ga_hi, E * 2 + (h + 1))
                        k = slice(4 * h, 4 * h + 4)
                        tt(xs[:, 1, k, 0:P], bank[6 + h][:, :].rearrange("p (k n) -> p k n", k=4),
                           xs[:, 0, k, 0:P].bitcast(F32), ALU.subtract).then_inc(ga_lo, 1)
                    units(run, turn_stops(j), it * (TURN * UNITS) + (len(DENSE) + j * UNITS), UNITS, 1,
                          lambda u: CH, PER_TURN)
                    dve.wait_ge(w_read, run.count((j + 1) * PER_TURN // TURN))
                    nc.vector.tensor_copy(eo[:, CH:D], bank[5][:, :]).then_inc(eo_hi, 1)
                    dve.wait_ge(y_add, E * 4 + Y0)
                    for half in range(2):
                        for t in range(T):
                            g = 2 * half + t
                            dve.wait_ge(back_mm, E * 4 + (g + 1))
                            part = y[:, t, half * CH:(half + 1) * CH]
                            tt(part, part, bank[BACK[g]][:, :], ALU.add).then_inc(y_add, 1)

            attention(0)
            dense()
            attention(1)
            route()
            with dve.Fori(0, TURNS) as i:
                experts(i, i)
            dve.wait_ge(y_add, 4 * NEXP + Y0)
            again = dve.value_load(more[0:1, 0:1], min_val=0, max_val=1)
            with dve.If(again > 0):
                ts(rank[:, :, :], rank[:, :, :], -float(P), None, ALU.add).then_inc(rank_ok, 1)
                dve.wait_ge(rank_ok, 1)
                with dve.Fori(0, TURNS) as i:
                    experts(i + TURNS, i)
                dve.wait_ge(y_add, 8 * NEXP + Y0)
            layer_norm(1, 1, y)


_OUTS = [((1, SEQ, D), "float32")]


def kernel(x, w_in, ml_conv_w, ml_conv_b, ml_i_b, ml_f_b, ml_norm_g, idx_k_norm_g, idx_k_norm_b, w_out,
           ln1_g, ln1_b, ln2_g, ln2_b, ffn_w_gate, ffn_w_up, ffn_w_down,
           moe_w_router, moe_b_router, moe_w_gate, moe_w_up, moe_w_down):
    import concourse.bacc as bacc
    from concourse.bass_utils import run_bass_kernel_spmd

    a = {k: np.asarray(v) for k, v in locals().items() if hasattr(v, "shape")}
    feat = np.zeros((DEPTH, P, PC_END), np.float32)
    feat[:, :, PC_W:PC_B] = a["ml_conv_w"].reshape(DEPTH, CONV, 2 * ML_H, P).transpose(0, 3, 2, 1).reshape(DEPTH, P, -1)
    feat[:, :, PC_B:PC_I] = a["ml_conv_b"].reshape(DEPTH, 2 * ML_H, P).transpose(0, 2, 1)
    feat[:, 0:ML_H, PC_I] = a["ml_i_b"]
    feat[:, 0:ML_H, PC_F] = a["ml_f_b"]
    arrays = {
        "x": a["x"], "w_in": a["w_in"], "w_out": a["w_out"],
        "ffn_gate": a["ffn_w_gate"], "ffn_up": a["ffn_w_up"], "ffn_down": a["ffn_w_down"],
        "w_router": a["moe_w_router"], "b_router": a["moe_b_router"],
        "moe_gate": a["moe_w_gate"], "moe_up": a["moe_w_up"], "moe_down": a["moe_w_down"],
        "feat_params": feat,
        "row_params": np.concatenate([a["ml_norm_g"], a["idx_k_norm_g"], a["idx_k_norm_b"]], axis=1),
        "ln_params": np.stack([a["ln1_g"], a["ln1_b"], a["ln2_g"], a["ln2_b"]], axis=1),
        "consts": shape_constants(),
    }
    arrays = {k: np.ascontiguousarray(v) for k, v in arrays.items()}
    nc = bacc.Bacc("TRN2", target_bir_lowering=False, num_devices=1)
    aps = {k: nc.dram_tensor(k, v.shape, mybir.dt.from_np(v.dtype), kind="ExternalInput").ap()
           for k, v in arrays.items()}
    shape, dtype = _OUTS[0]
    out = nc.dram_tensor("out", shape, mybir.dt.from_np(np.dtype(dtype)), kind="ExternalOutput").ap()
    build_program(nc, **aps, out=out)
    r = run_bass_kernel_spmd(nc, [arrays], core_ids=[0])
    return r.results[0]["out"]
```

```python
from contextlib import ExitStack

import numpy as np

import concourse.bass as bass
from concourse import mybir

F32 = mybir.dt.float32
F32R = mybir.dt.float32r
I32 = mybir.dt.int32
U32 = mybir.dt.uint32
ALU = mybir.AluOpType
ACT = mybir.ActivationFunctionType
AX = mybir.AxisListType

P = 128
SEQ, D = 256, 1024
T = SEQ // P
KT = D // P
DEPTH = 2
ML_H, ML_D = 4, 128
ML_W = ML_H * ML_D
CONV = 4
AT_H, AT_KV, AT_D = 8, 2, 64
IDX_H = 4
TOPK = min(256, SEQ // 4)
FF_DENSE, FF_EXPERT, NEXP = 2816, 3584, 8
ALPHA = (2 * DEPTH) ** 0.25
LN_EPS = 1e-5
ROPE_THETA = 500000.0
ROT = AT_D // 4 // 2

C_MQ, C_MK, C_MV, C_MO = 0, ML_W, 2 * ML_W, 3 * ML_W
C_GATE = 4 * ML_W
C_END = C_GATE + 2 * ML_H + AT_H * AT_D + 2 * AT_KV * AT_D + (IDX_H + 1) * AT_D + IDX_H
AW = C_END - C_GATE
A_Q = 2 * ML_H
A_K = A_Q + AT_H * AT_D
A_V = A_K + AT_KV * AT_D
A_IQ = A_V + AT_KV * AT_D
A_IK = A_IQ + IDX_H * AT_D
A_IW = A_IK + AT_D

NSLOT = 6
SLOT = 2048
NSPLIT = 3
CH = 512
NEG = -1.0e30
TAKEN = -3.0e38

K_ID, K_CAUSAL, K_CAUSALT, K_IOTA, K_TRIU, K_ONES = 0, 128, 512, 896, 1024, 1152
K_SEL, K_COS, K_SIN, K_EPS = 1408, 1920, 1936, 1952
K_END = 1953


def shape_constants():
    t = np.zeros((P, K_END), np.float32)
    p = np.arange(P)[:, None]
    f = np.arange(P)[None, :]
    t[:, K_ID:K_ID + P] = p == f
    diag = np.where(f <= p, 0.0, NEG)
    t[:, K_CAUSAL:K_CAUSAL + P] = diag
    t[:, K_CAUSAL + 2 * P:K_CAUSAL + 3 * P] = diag
    t[:, K_CAUSALT:K_CAUSALT + P] = diag.T
    t[:, K_CAUSALT + 2 * P:K_CAUSALT + 3 * P] = diag.T
    t[:, K_IOTA:K_IOTA + P] = f
    t[:, K_TRIU:K_TRIU + P] = p < f
    t[:, K_ONES:K_ONES + SEQ] = 1.0
    for h in range(ML_H):
        t[h, K_SEL + h * P:K_SEL + (h + 1) * P] = 1.0
    inv = np.float32(ROPE_THETA) ** (-np.arange(ROT, dtype=np.float32) / np.float32(ROT))
    ang = np.arange(SEQ, dtype=np.float32)[:, None] * inv[None, :]
    t[:, K_COS:K_COS + T * ROT] = np.cos(ang).reshape(T, P, ROT).transpose(1, 0, 2).reshape(P, T * ROT)
    t[:, K_SIN:K_SIN + T * ROT] = np.sin(ang).reshape(T, P, ROT).transpose(1, 0, 2).reshape(P, T * ROT)
    t[:, K_EPS] = LN_EPS
    return t


PC_W, PC_B, PC_I, PC_F, PC_END = 0, 2 * ML_H * CONV, 2 * ML_H * CONV + 2 * ML_H, 2 * ML_H * CONV + 2 * ML_H + 1, 42
AR_NG, AR_IG, AR_IB, AR_END = 0, ML_W, ML_W + AT_D, ML_W + 2 * AT_D


def build_program(nc, x, w_in, w_out, ffn_gate, ffn_up, ffn_down, w_router, b_router, moe_gate, moe_up, moe_down,
                  feat_params, row_params, ln_params, consts, out):
    with ExitStack() as ctx:
        def sb(name, shape, dt=F32):
            return ctx.enter_context(nc.sbuf_tensor(name, shape, dt))

        def sem(name):
            return ctx.enter_context(nc.semaphore(name))

        def layer_sem(name):
            return [sem(f"{name}_{l}") for l in range(DEPTH)]

        x_tok = sb("x_tok", [P, T, D])
        xT = sb("xT", [P, KT, SEQ])
        cst = sb("cst", [P, K_END])
        feat = sb("feat", [P, DEPTH, PC_END])
        rows = sb("rows", [P, DEPTH, AR_END])
        ln = sb("ln", [P, 2, D])
        ring = sb("ring", [P, NSLOT, SLOT])
        split = sb("split", [P, NSPLIT, 2, SLOT], F32R)
        xs = sb("xs", [P, 2, KT, SEQ], F32R)
        hs = sb("hs", [P, T, 2, CH // P, P], F32R)
        WORK = 12352
        work = sb("work", [P, WORK])
        used = [0, 0]

        def carve(phase, size):
            a = used[phase]
            used[phase] += size
            assert used[phase] <= WORK, (phase, used[phase])
            return work[:, a:a + size]

        pre_mem = carve(0, 2 * ML_H * (SEQ + CONV - 1))
        pre = pre_mem.rearrange("p (f s) -> p f s", f=2 * ML_H)
        og = pre_mem[:, 0:T * ML_W].rearrange("p (t n) -> p t n", t=T)
        v_tok = pre_mem[:, T * ML_W:2 * T * ML_W].rearrange("p (t n) -> p t n", t=T)
        qk_mem = carve(0, 2 * ML_H * SEQ)
        qk = qk_mem.rearrange("p (f s) -> p f s", f=2 * ML_H)
        mix = qk_mem.rearrange("p (t n) -> p t n", t=T)
        iscore = qk_mem[:, ML_H * SEQ:ML_H * SEQ + 384]
        left = qk_mem[:, ML_H * SEQ + 384:ML_H * SEQ + 768]
        att = carve(0, T * AW).rearrange("p (t n) -> p t n", t=T)
        aqT = carve(0, 4 * SEQ).rearrange("p (f s) -> p f s", f=4)
        akT = carve(0, AT_KV * SEQ).rearrange("p (g s) -> p g s", g=AT_KV)
        idx_mem = carve(0, 2 * SEQ + SEQ + 2 * 384)
        iqT = idx_mem[:, 0:2 * SEQ].rearrange("p (f s) -> p f s", f=2)
        ikT = idx_mem[:, 2 * SEQ:3 * SEQ]
        relu = idx_mem[:, 3 * SEQ:].rearrange("p (b s) -> p b s", b=2)
        mld = idx_mem[:, 0:ML_H * 384].rearrange("p (h s) -> p h s", h=ML_H)
        shared = carve(0, 6 * 384)
        rope = [shared[:, i * T * 10 * ROT:(i + 1) * T * 10 * ROT].rearrange("p (t h r) -> p t h r", t=T, h=10)
                for i in range(4)]
        kdup = shared[:, 0:T * 2 * AT_KV * AT_D].rearrange("p (t g c n) -> p t g c n", t=T, g=AT_KV, c=2)
        ikdup = shared[:, 640:640 + T * 2 * AT_D].rearrange("p (t c n) -> p t c n", t=T, c=2)
        gate = shared[:, 3 * 384:3 * 384 + 4 * SEQ].rearrange("p (r s) -> p r s", r=4)
        probs = shared[:, 0:3 * 384].rearrange("p (b s) -> p b s", b=3)
        probsT = shared[:, 3 * 384:6 * 384].rearrange("p (b s) -> p b s", b=3)
        choice = carve(0, 384)
        top8 = carve(0, T * 8).rearrange("p (t n) -> p t n", t=T)
        gT = carve(0, T * ML_H).rearrange("p (t h) -> p t h", t=T)
        emT = carve(0, T * ML_H).rearrange("p (t h) -> p t h", t=T)
        rden = carve(0, T * ML_H).rearrange("p (t h) -> p t h", t=T)
        rden2 = carve(0, T * ML_H).rearrange("p (t h) -> p t h", t=T)
        rsum = carve(0, T * AT_H).rearrange("p (t h) -> p t h", t=T)
        rmax = carve(0, 3 * T).rearrange("p (b t) -> p b t", b=3)
        nmax = carve(0, 3 * T).rearrange("p (b t) -> p b t", b=3)
        y = carve(1, T * D).rearrange("p (t n) -> p t n", t=T)
        silu = carve(1, T * CH).rearrange("p (t n) -> p t n", t=T)
        hid = carve(1, T * CH).rearrange("p (t n) -> p t n", t=T)
        sel = carve(1, T * P).rearrange("p (t n) -> p t n", t=T)
        selc = carve(1, T * P).rearrange("p (t n) -> p t n", t=T)
        selT = carve(1, T * P).rearrange("p (t n) -> p t n", t=T)
        eo = carve(1, D)
        stats = sb("stats", [P, 8, 2, 6])
        mv = sb("mv", [P, 8, 2])
        var = sb("var", [P, 8])
        rs = sb("rs", [P, 8])
        nt = sb("nt", [P, 2, 8])
        wr = sb("wr", [P, KT, NEXP])
        br = sb("br", [P, NEXP])
        lg = sb("lg", [P, T, NEXP])
        m8 = sb("m8", [P, T, 8])
        i8 = sb("i8", [P, T, 8], U32)
        i8f = sb("i8f", [P, T, 2])
        oh = sb("oh", [P, T, 2, NEXP])
        g2 = sb("g2", [P, T, 3])
        comb = sb("comb", [P, T, NEXP])
        routed = sb("routed", [P, T, NEXP])
        rank = sb("rank", [P, T, NEXP])
        cnt = sb("cnt", [P, NEXP])
        cmax = sb("cmax", [P, 1])
        more = sb("more", [P, 1], I32)

        bank = [ctx.enter_context(nc.psum_tensor(f"bank{i}", [P, CH], F32)) for i in range(2)]
        hid_ps = ctx.enter_context(nc.psum_tensor("bank23", [P, T, CH], F32))
        bank += [hid_ps[:, t, :] for t in range(T)]
        bank += [ctx.enter_context(nc.psum_tensor(f"bank{i}", [P, CH], F32)) for i in range(4, 8)]

        ident = cst[:, K_ID:K_ID + P]
        causal = cst[:, K_CAUSAL:K_CAUSAL + 384]
        causalT = cst[:, K_CAUSALT:K_CAUSALT + 384]
        iota = cst[:, K_IOTA:K_IOTA + P]
        triu = cst[:, K_TRIU:K_TRIU + P]
        ones = cst[:, K_ONES:K_ONES + SEQ]
        eps = cst[:, K_EPS:K_EPS + 1]
        one = cst[:, K_ONES:K_ONES + 1]

        in_x = [sem(f"in_x{t}") for t in range(T)]
        in_ident, in_const, in_rows, in_ln = sem("in_ident"), sem("in_const"), sem("in_rows"), sem("in_ln")
        stored = sem("stored")
        tile0_mm = sem("tile0_mm")
        xs_hi, xs_lo = sem("xs_hi"), sem("xs_lo")
        slot_full = [sem(f"slot_full{i}") for i in range(NSLOT)]
        dstep = sem("dstep")
        xt_mm, xt_ready = sem("xt_mm"), sem("xt_ready")
        x_ready = sem("x_ready")
        proj_t0, proj_ev = layer_sem("proj_t0"), layer_sem("proj_ev")
        gate_mm, gate_ev = layer_sem("gate_mm"), layer_sem("gate_ev")
        qk_ev = layer_sem("qk_ev")
        conv_y, conv_ok = layer_sem("conv_y"), layer_sem("conv_ok")
        var_ok, ln_v, rs_ok = layer_sem("var_ok"), layer_sem("ln_v"), layer_sem("rs_ok")
        roped, dup_ok = layer_sem("roped"), layer_sem("dup_ok")
        itr_mm, itr_ev = layer_sem("itr_mm"), layer_sem("itr_ev")
        idx_mm, idx_ev, idx_used = layer_sem("idx_mm"), layer_sem("idx_ev"), layer_sem("idx_used")
        atr_mm, atr_ev = layer_sem("atr_mm"), layer_sem("atr_ev")
        gate_row, gtr_mm, gtr_ev = layer_sem("gate_row"), layer_sem("gtr_mm"), layer_sem("gtr_ev")
        vo_mm, v_ev, o_ev, og_ok = layer_sem("vo_mm"), layer_sem("v_ev"), layer_sem("o_ev"), layer_sem("og_ok")
        mrow_mm, mls_mm, ml_e, ml_d, ml_p, num_mm, mix_ml = (
            layer_sem(n) for n in ("mrow_mm", "mls_mm", "ml_e", "ml_d", "ml_p", "num_mm", "mix_ml"))
        sc_mm, sc_max, sc_exp, ptr_mm, pt_ok, pv_mm, mix_at = (
            layer_sem(n) for n in ("sc_mm", "sc_max", "sc_exp", "ptr_mm", "pt_ok", "pv_mm", "mix_at"))
        mtr_mm, op_mm = layer_sem("mtr_mm"), layer_sem("op_mm")
        half_read = layer_sem("half_read")
        hi_ok, lo_ok, w_read = sem("hi_ok"), sem("lo_ok"), sem("w_read")
        g_silu, h_ok, ht_mm, ht_hi, ht_lo = (sem(n) for n in ("g_silu", "h_ok", "ht_mm", "ht_hi", "ht_lo"))
        rt_mm, rt_diff, rt_exp, rt_mask, rk_mm, more_ok = (
            sem(n) for n in ("rt_mm", "rt_diff", "rt_exp", "rt_mask", "rk_mm", "more_ok"))
        rank_ok = sem("rank_ok")
        Y0, GA0, ST0 = T, 1, 1
        EARLY_SPLIT = (4, 6)
        MIX_TR = ((0, 0, 6), (1, 0, 6), (0, 1, 6), (1, 1, 7))
        ML_BANK, PT_BANK = (6, 7, 0, 1), (3, 7)
        BACK = (6, 7, 1, 3)
        sel_ok, ga_mm, ga_hi, ga_lo, st_mm, st_ev, eo_lo, eo_hi, back_mm, y_add = (
            sem(n) for n in ("sel_ok", "ga_mm", "ga_hi", "ga_lo", "st_mm", "st_ev", "eo_lo", "eo_hi", "back_mm", "y_add"))

        def by_k(m, r0, c0, c1, k):
            return m[r0:r0 + k * P, c0:c1].rearrange("(k p) n -> p k n", p=P), k, c1 - c0

        A_GROUPS = (0, 368, 736, AW)
        DENSE = [(c, min(CH, FF_DENSE - c)) for c in range(0, FF_DENSE, CH)]
        UNITS = FF_EXPERT // CH
        stream, FIRST_IN, FIRST_OUT, SPLIT_IN = [], [], [], []

        def add(chunk, read):
            stream.append((*chunk, read))

        n_split = 0
        for l in range(DEPTH):
            m = w_in[l]
            FIRST_IN.append(len(stream))
            SPLIT_IN.append(n_split)
            parts = [by_k(m, r0, C_GATE + a, C_GATE + b, 4)
                     for a, b in zip(A_GROUPS, A_GROUPS[1:]) for r0 in (0, CH)]
            parts += [by_k(m, 0, C_MQ + i * SEQ, C_MQ + (i + 1) * SEQ, KT) for i in range(4)]
            for chunk in parts:
                n_split += 1
                add(chunk, (lo_ok, n_split))
            for c in range(2):
                c0 = C_MV + c * CH
                add(by_k(m, 0, c0, c0 + CH, 4), (half_read[l], c + 1))
                add(by_k(m, CH, c0, c0 + CH, 4), (vo_mm[l], 2 * (c + 1)))
            FIRST_OUT.append(len(stream))
            for i in range(4):
                n_split += 1
                add(by_k(w_out[l], i * 2 * P, 0, D, 2), (lo_ok, n_split))
            if l == 0:
                FIRST_DENSE, SPLIT_DENSE = len(stream), n_split
                downs = []
                for c, w in DENSE:
                    for m in (ffn_gate[0], ffn_up[0]):
                        parts = [(0, 4), (CH, 4)] if w == CH else [(0, KT)]
                        for r0, k in parts:
                            n_split += 1
                            add(by_k(m, r0, c, c + w, k), (lo_ok, n_split))
                    for d in downs:
                        n_split += 1
                        add(d, (lo_ok, n_split))
                    v = ffn_down[0, c:c + w, :].rearrange("(p j) n -> p j n", p=P)
                    downs = [(v[:, j:j + 2, :], 2, D) for j in range(0, w // P, 2)]
                for d in downs:
                    n_split += 1
                    add(d, (lo_ok, n_split))
                N_DENSE = n_split - SPLIT_DENSE
        N_STREAM, N_SPLIT = len(stream), n_split

        def slot_view(s, k, n):
            return ring[:, s, 0:k * n].rearrange("p (k n) -> p k n", k=k)

        def chunk_view(n):
            return slot_view(n % NSLOT, stream[n][1], stream[n][2])

        def wait_chunk(eng, n):
            eng.wait_ge(slot_full[n % NSLOT], 16 * (n // NSLOT + 1))

        XS_IN, XS_MIX, XS_DENSE = (0, 12), (4, 16), 8

        TURN = 2
        TURNS = NEXP // TURN
        ORDER = []
        for j in range(TURN):
            for c in range(UNITS + 1):
                for part in ("gate", "up") if c < UNITS else ():
                    ORDER += [(j, c, part, 0), (j, c, part, 1)]
                if c:
                    ORDER += [(j, c - 1, "down", 0), (j, c - 1, "down", 1)]
        PER_TURN = len(ORDER)
        assert PER_TURN % NSLOT == 0 and PER_TURN % NSPLIT == 0
        FILLS = PER_TURN // NSLOT
        wg_v = moe_gate.rearrange("a e (k p) f -> p (a e) k f", p=P)
        wu_v = moe_up.rearrange("a e (k p) f -> p (a e) k f", p=P)
        wd_v = moe_down.rearrange("a e (c p j) n -> p (a e) c j n", p=P, j=CH // P)

        class Run:

            def __init__(self, first, split0, shapes, it=0):
                self.first, self.split0, self.shapes, self.it = first, split0, shapes, it

            def raw(self, i):
                return ring[:, (self.first + i) % NSLOT, :]

            def parts(self, i):
                k, n = self.shapes[i % len(self.shapes)]
                return [split[:, (self.split0 + i) % NSPLIT, h, 0:k * n].rearrange("p (k n) -> p k n", k=k)
                        for h in range(2)]

            def wait_full(self, eng, i):
                n = self.first + i
                eng.wait_ge(slot_full[n % NSLOT], self.it * (16 * FILLS) + 16 * (n // NSLOT + 1))

            def count(self, i):
                return self.it * PER_TURN + (self.split0 + i)

        N_IN = 10

        def in_run(l):
            first = FIRST_IN[l]
            return Run(first, SPLIT_IN[l], [c[1:3] for c in stream[first:first + N_IN]])

        def out_run(l):
            first = FIRST_OUT[l]
            return Run(first, SPLIT_IN[l] + N_IN, [c[1:3] for c in stream[first:first + 4]])

        def dense_run():
            return Run(FIRST_DENSE, SPLIT_DENSE, [stream[FIRST_DENSE + i][1:3] for i in range(N_DENSE)])

        def turn_run(it):
            return Run(N_STREAM, N_SPLIT, [(2, D) if o[2] == "down" else (4, CH) for o in ORDER], it)

        def dense_stops():
            i, stops = 0, []
            for c in range(len(DENSE) + 1):
                for part in ("gate", "up") if c < len(DENSE) else ():
                    n = 2 if DENSE[c][1] == CH else 1
                    stops.append((part, c, list(range(i, i + n))))
                    i += n
                if c:
                    n = 2 if DENSE[c - 1][1] == CH else 1
                    stops.append(("down", c - 1, list(range(i, i + n))))
                    i += n
            return stops

        def turn_stops(j):
            i, stops = j * PER_TURN // TURN, []
            for c in range(UNITS + 1):
                for part in ("gate", "up") if c < UNITS else ():
                    stops.append((part, c, [i, i + 1]))
                    i += 2
                if c:
                    stops.append(("down", c - 1, [i, i + 1]))
                    i += 2
            return stops

        block = ctx.enter_context(nc.Block())

        def hidden_banks(tiles, w):
            return hid_ps[:, 0:tiles, 0:w * P].rearrange("p t (j n) -> p t j n", j=w)

        def hidden_split(u, tiles):
            return hs if tiles == T else hs[:, u % 2:u % 2 + 1]

        @block.sync
        def _(sp):
            for t in range(T):
                sp.dma_start(x_tok[:, t], x[0, t * P:(t + 1) * P, :]).then_inc(in_x[t], 16)
            for n, (src, _, _, _) in enumerate(stream):
                if n >= NSLOT:
                    sp.wait_ge(*stream[n - NSLOT][3])
                sp.dma_start(chunk_view(n), src).then_inc(slot_full[n % NSLOT], 16)

            def turn(it, pair):
                for i, (j, c, part, half) in enumerate(ORDER):
                    e = bass.ds(pair * TURN + j, 1)
                    n = N_STREAM + i
                    if isinstance(it, int) and i < NSLOT:
                        sp.wait_ge(*stream[n - NSLOT][3])
                    else:
                        sp.wait_ge(lo_ok, it * PER_TURN + (N_SPLIT + i - NSLOT + 1))
                    if part == "down":
                        src, k, w = wd_v[:, e, c, 2 * half:2 * half + 2], 2, D
                    else:
                        m = wg_v if part == "gate" else wu_v
                        src, k, w = m[:, e, 4 * half:4 * half + 4, c * CH:(c + 1) * CH], 4, CH
                    sp.dma_start(slot_view(n % NSLOT, k, w), src.rearrange("p a k n -> p (a k) n")
                                 ).then_inc(slot_full[n % NSLOT], 16)

            turn(0, 0)
            with sp.Fori(1, TURNS) as i:
                turn(i, i)
            sp.wait_ge(more_ok, 1)
            again = sp.value_load(more[0:1, 0:1], min_val=0, max_val=1)
            with sp.If(again > 0):
                with sp.Fori(0, TURNS) as i:
                    turn(i + TURNS, i)
            for t in range(T):
                sp.wait_ge(x_ready, 3 * T + t + 1)
                sp.dma_start(out[0, t * P:(t + 1) * P, :], x_tok[:, t, :]).then_inc(stored, 16)
            sp.wait_ge(stored, 16 * T)

        @block.gpsimd
        def _(pool):
            pool.dma_start(ident, consts[:, K_ID:K_ID + P]).then_inc(in_ident, 16)
            pool.wait_ge(xt_ready, 2)
            pool.dma_start(cst[:, P:], consts[:, P:]).then_inc(in_const, 16)
            pool.dma_start(feat[:], feat_params.rearrange("l p n -> p l n")).then_inc(in_const, 16)
            pool.dma_start(rows[:], row_params.partition_broadcast(P)).then_inc(in_rows, 16)
            pool.dma_start(br[:], b_router.rearrange("a n -> (a n)").partition_broadcast(P)).then_inc(in_rows, 16)
            pool.dma_start(wr[:], w_router[0].rearrange("(k p) n -> p k n", p=P)).then_inc(in_rows, 16)
            for l in range(DEPTH):
                if l:
                    pool.wait_ge(x_ready, 2 * l * T)
                pool.dma_start(ln[:], ln_params[l, 0:2].partition_broadcast(P)).then_inc(in_ln, 16)
                pool.wait_ge(roped[l], 1)
                for t in range(T):
                    pool.tensor_copy(ikdup[:, t], att[:, t, A_IK:A_IW].unsqueeze(1).to_broadcast([P, 2, AT_D])
                                     ).then_inc(dup_ok[l], 1)
                pool.wait_ge(roped[l], 2)
                for t in range(T):
                    k = att[:, t, A_K:A_V].rearrange("p (g n) -> p g n", g=AT_KV)
                    pool.tensor_copy(kdup[:, t], k.unsqueeze(2).to_broadcast([P, AT_KV, 2, AT_D])
                                     ).then_inc(dup_ok[l], 1)
                pool.wait_ge(in_rows, 48)
                for t in range(T):
                    pool.wait_ge(o_ev[l], t + 1)
                    pool.tensor_tensor(og[:, t], og[:, t], rows[:, l, AR_NG:AR_IG], ALU.mult).then_inc(og_ok[l], 1)
                pool.wait_ge(x_ready, (2 * l + 1) * T)
                pool.dma_start(ln[:], ln_params[l, 2:4].partition_broadcast(P)).then_inc(in_ln, 16)

        @block.tensor
        def _(pe):
            mm = nc.tensor.matmul
            tr = nc.tensor.transpose

            def x_transposes(stage):
                for t in range(T):
                    if stage:
                        pe.wait_ge(x_ready, (stage - 1) * T + t + 1)
                    else:
                        pe.wait_ge(in_x[t], 16)
                        pe.wait_ge(in_ident, 16)
                    for h in range(2):
                        for j in range(4):
                            k = 4 * h + j
                            i = tr(bank[4 + 2 * t + h][:, j * P:(j + 1) * P], x_tok[:, t, k * P:(k + 1) * P], ident)
                        i.then_inc(xt_mm, 1)

            def token_halves(l, n, banks, done, halves=(0, 1)):
                for half in halves:
                    wait_chunk(pe, n + half)
                    w = chunk_view(n + half)
                    for t in range(T):
                        for j in range(4):
                            i = mm(banks[t][:, :], xT[:, 4 * half + j, t * P:(t + 1) * P], w[:, j, :],
                                   start=half == 0 and j == 0, stop=half == 1 and j == 3)
                        if half:
                            i.then_inc(done, 1)
                    if not half:
                        i.then_inc(half_read[l], 1)

            def product(o, run, i, a, k, cols, first, last):
                hi, lo = run.parts(i)
                for kk in range(k):
                    ah, al = a(kk)
                    mm(o, ah, hi[:, kk, cols], start=first and kk == 0, stop=False)
                    mm(o, ah, lo[:, kk, cols], start=False, stop=False)
                    r = mm(o, al, hi[:, kk, cols], start=False, stop=last and kk == k - 1)
                return r

            def split_columns(l, i, banks, first, last):
                run = in_run(l)
                k, w = run.shapes[i]
                k0 = 0 if first else KT - k
                pe.wait_ge(lo_ok, run.count(i + 1))
                for t in range(T):
                    if i < 2:
                        pe.wait_ge(xs_lo, XS_IN[l] + 2 * t + i + 1)
                    r = product(banks[t][:, 0:w], run, i,
                                lambda kk: [xs[:, m, k0 + kk, t * P:(t + 1) * P] for m in range(2)], k,
                                slice(0, w), first, last)
                    if last and t == 0:
                        r.then_inc(proj_t0[l], 1)
                r.then_inc(w_read, 1)

            def feature_pairs(l, first):
                run = in_run(l)
                for j in range(first, first + 2):
                    i = N_IN - 4 + j
                    pe.wait_ge(lo_ok, run.count(i + 1))
                    if j >= 2:
                        pe.wait_ge(qk_ev[l], j - 1)
                    hi, lo = run.parts(i)
                    for f in range(2):
                        o, cols = bank[5 + j % 2][:, f * SEQ:(f + 1) * SEQ], slice(f * P, (f + 1) * P)
                        for k in range(KT):
                            mm(o, hi[:, k, cols], xs[:, 0, k, :], start=k == 0, stop=False)
                            mm(o, hi[:, k, cols], xs[:, 1, k, :], start=False, stop=False)
                            r = mm(o, lo[:, k, cols], xs[:, 0, k, :], start=False, stop=k == KT - 1)
                    r.then_inc(w_read, 1)

            def attention(l):
                c0 = FIRST_IN[l]
                for i in range(4):
                    split_columns(l, i, bank[i // 2 * 2:i // 2 * 2 + 2], i % 2 == 0, i % 2 == 1)
                pe.wait_ge(proj_ev[l], T)
                pe.wait_ge(xt_ready, 4 * (l + 1))
                for m in range(2):
                    for t in range(T):
                        i = tr(bank[6][0:ML_H, m * SEQ + t * P:m * SEQ + (t + 1) * P],
                               att[:, t, m * ML_H:(m + 1) * ML_H], ident)
                i.then_inc(gate_mm[l], 1)
                for i in (4, 5):
                    split_columns(l, i, (bank[4], bank[7]), i == 4, i == 5)
                pe.wait_ge(gate_ev[l], 2)
                feature_pairs(l, 0)
                pe.wait_ge(proj_ev[l], 6)
                pe.wait_ge(roped[l], 1)
                for f in range(2):
                    for t in range(T):
                        i = tr(bank[0][:, f * SEQ + t * P:f * SEQ + (t + 1) * P],
                               att[:, t, A_IQ + f * P:A_IQ + (f + 1) * P], ident)
                i.then_inc(itr_mm[l], 1)
                pe.wait_ge(dup_ok[l], T)
                for t in range(T):
                    i = tr(bank[1][:, t * P:(t + 1) * P], ikdup[:, t].rearrange("p c n -> p (c n)"), ident)
                i.then_inc(itr_mm[l], 1)
                feature_pairs(l, 2)
                pe.wait_ge(itr_ev[l], 2)
                for h in range(IDX_H):
                    a = AT_D * (h % 2)
                    for t in range(T):
                        o = (0, P)[t]
                        i = mm(bank[h][:, o:o + (t + 1) * P], iqT[a:a + AT_D, h // 2, t * P:(t + 1) * P],
                               ikT[a:a + AT_D, 0:(t + 1) * P], start=True, stop=True)
                    i.then_inc(idx_mm[l], 1)
                pe.wait_ge(dup_ok[l], 2 * T)
                pe.wait_ge(qk_ev[l], 4)
                for f in range(4):
                    for t in range(T):
                        i = tr(bank[4 + f // 2][:, (f % 2) * SEQ + t * P:(f % 2) * SEQ + (t + 1) * P],
                               att[:, t, A_Q + f * P:A_Q + (f + 1) * P], ident)
                    if f % 2:
                        i.then_inc(atr_mm[l], 1)
                for g in range(AT_KV):
                    for t in range(T):
                        i = tr(bank[6][:, g * SEQ + t * P:g * SEQ + (t + 1) * P],
                               kdup[:, t, g].rearrange("p c n -> p (c n)"), ident)
                i.then_inc(atr_mm[l], 1)
                pe.wait_ge(gate_row[l], 1)
                for m, r in enumerate((0, 2)):
                    for t in range(T):
                        i = tr(bank[7][:, (2 * m + t) * ML_H:(2 * m + t + 1) * ML_H],
                               gate[0:ML_H, r, t * P:(t + 1) * P], cst[0:ML_H, K_ID:K_ID + ML_H])
                i.then_inc(gtr_mm[l], 1)
                pe.wait_ge(idx_ev[l], IDX_H)
                token_halves(l, c0 + N_IN, bank[0:2], vo_mm[l])
                pe.wait_ge(atr_ev[l], 3)
                for h in range(ML_H):
                    i = mm(bank[4 + h // 2][:, (h % 2) * SEQ:(h % 2 + 1) * SEQ],
                           cst[0:ML_H, K_SEL + h * P:K_SEL + (h + 1) * P], gate[0:ML_H, 1, :], start=True, stop=True)
                    if h % 2:
                        i.then_inc(mrow_mm[l], 1)
                token_halves(l, c0 + N_IN + 2, bank[2:4], vo_mm[l], halves=(0,))
                pe.wait_ge(conv_ok[l], 2)
                pe.wait_ge(gtr_ev[l], 2)
                pe.wait_ge(v_ev[l], T)
                for h in range(ML_H):
                    b = bank[ML_BANK[h]]
                    mm(b[:, 0:SEQ], qk[:, ML_H + h, 0:P], qk[:, h, :], start=True, stop=True)
                    mm(b[:, SEQ:SEQ + P], qk[:, ML_H + h, P:SEQ], qk[:, h, P:SEQ],
                       start=True, stop=True).then_inc(mls_mm[l], 1)
                for h in range(ML_H):
                    pe.wait_ge(ml_p[l], h + 1)
                    v = [v_tok[:, t, h * ML_D:(h + 1) * ML_D] for t in range(T)]
                    o = [bank[4 + t][:, h * ML_D:(h + 1) * ML_D] for t in range(T)]
                    d = [bank[6][:, t * ML_H + h:t * ML_H + h + 1] for t in range(T)]
                    mm(o[0], mld[:, h, 0:P], v[0], start=True, stop=True)
                    mm(d[0], mld[:, h, 0:P], one, start=True, stop=True)
                    mm(o[1], mld[:, h, P:2 * P], v[0], start=True, stop=False)
                    mm(o[1], mld[:, h, 2 * P:3 * P], v[1], start=False, stop=True)
                    mm(d[1], mld[:, h, P:2 * P], one, start=True, stop=False)
                    mm(d[1], mld[:, h, 2 * P:3 * P], one, start=False, stop=True).then_inc(num_mm[l], 1)

                def scores(h):
                    a = AT_D * (h % 2)
                    if h >= 3:
                        pe.wait_ge(sc_max[l], h - 2)
                    elif h == 2:
                        pe.wait_ge(o_ev[l], 1)
                    else:
                        pe.wait_ge(ml_p[l], h + 3)
                    for t in range(T):
                        o = (0, P)[t]
                        i = mm(bank[h % 3][:, o:o + (t + 1) * P], aqT[a:a + AT_D, h // 2, t * P:(t + 1) * P],
                               akT[a:a + AT_D, h // (AT_H // AT_KV), 0:(t + 1) * P], start=True, stop=True)
                    i.then_inc(sc_mm[l], 1)

                def prob_transposes(h):
                    pe.wait_ge(sc_exp[l], h + 1)
                    if h >= 2:
                        pe.wait_ge(pt_ok[l], h - 1)
                    elif h == 0:
                        pe.wait_ge(o_ev[l], 2)
                    for j in range(3):
                        i = tr(bank[PT_BANK[h % 2]][:, j * P:(j + 1) * P], probs[:, h % 3, j * P:(j + 1) * P], ident)
                    i.then_inc(ptr_mm[l], 1)

                def values(h):
                    if h == 0:
                        pe.wait_ge(mix_ml[l], 1)
                    pe.wait_ge(pt_ok[l], h + 1)
                    v = A_V + AT_D * (h // (AT_H // AT_KV))
                    o = slice(h * AT_D, (h + 1) * AT_D)
                    pT = probsT[:, h % 3]
                    mm(bank[4][:, o], pT[:, 0:P], att[:, 0, v:v + AT_D], start=True, stop=True)
                    mm(bank[5][:, o], pT[:, P:2 * P], att[:, 0, v:v + AT_D], start=True, stop=False)
                    mm(bank[5][:, o], pT[:, 2 * P:3 * P], att[:, 1, v:v + AT_D], start=False, stop=True
                       ).then_inc(pv_mm[l], 1)

                def mix_transposes(g):
                    t, half, b = MIX_TR[g]
                    for j in range(4):
                        k = 4 * half + j
                        i = tr(bank[b][:, j * P:(j + 1) * P], mix[:, t, k * P:(k + 1) * P], ident)
                    i.then_inc(mtr_mm[l], 1)

                for h in range(AT_H + 4):
                    if h == 2:
                        token_halves(l, c0 + N_IN + 2, bank[2:4], vo_mm[l], halves=(1,))
                    if h < AT_H:
                        scores(h)
                    if 2 <= h < AT_H + 2:
                        prob_transposes(h - 2)
                    if h >= 4:
                        values(h - 4)
                    if h == 5:
                        mix_transposes(0)
                    if h == 8:
                        pe.wait_ge(xs_lo, XS_MIX[l] + 1)
                        mix_transposes(1)
                pe.wait_ge(xs_lo, XS_MIX[l] + 2)
                run = out_run(l)
                for q in range(4):
                    if q == 2:
                        pe.wait_ge(xs_lo, XS_MIX[l] + 4)
                    pe.wait_ge(lo_ok, run.count(q + 1))
                    for g in range(4):
                        t, c = divmod(g, 2)
                        i = product(bank[g][:, :], run, q,
                                    lambda kk: [xs[:, m, 2 * q + kk, t * P:(t + 1) * P] for m in range(2)], 2,
                                    slice(c * CH, (c + 1) * CH), q == 0, q == 3)
                        if q == 3 and g < 3:
                            i.then_inc(op_mm[l], 1)
                    i.then_inc(w_read, 1)
                    if q == 0:
                        pe.wait_ge(mix_at[l], 1)
                        mix_transposes(2)
                        mix_transposes(3)
                x_transposes(2 * l + 1)

            def units(run, stops, base, n_units, tiles, x_of, width, first_gate=None, last_up=None):
                def transposes(u):
                    pe.wait_ge(h_ok, base + (u + 1))
                    w = width(u)
                    for t in range(tiles):
                        h = hid[:, t, 0:w].rearrange("p (f j) -> p j f", j=w // P)
                        for j in range(w // P):
                            i = tr(bank[2 + t][:, j * P:(j + 1) * P], h[:, j, :], ident)
                    i.then_inc(ht_mm, 1)

                for part, u, chunks in stops:
                    w = width(u)
                    if part == "down" and u == n_units - 1 and tiles == T:
                        transposes(u)
                    if part == "gate":
                        pe.wait_ge(g_silu, base + u)
                    elif part == "up":
                        if u:
                            pe.wait_ge(ht_lo, base + u)
                        else:
                            pe.wait_ge(h_ok, base + u)
                    else:
                        pe.wait_ge(ht_lo, base + (u + 1))
                    for n, i in enumerate(chunks):
                        pe.wait_ge(lo_ok, run.count(i + 1))
                        k = run.shapes[i][0]
                        for t in range(tiles):
                            if part == "down":
                                for half in range(2):
                                    r = product(bank[4 + 2 * t + half][:, :], run, i,
                                                lambda kk: [hidden_split(u, tiles)[:, t, m, 2 * n + kk, :] for m in range(2)],
                                                k,
                                                slice(half * CH, (half + 1) * CH), u == 0 and n == 0,
                                                u == n_units - 1 and n == len(chunks) - 1)
                                if tiles == T and t == 0 and u == n_units - 1 and n == len(chunks) - 1:
                                    r.then_inc(tile0_mm, 1)
                            else:
                                if tiles == T and part == "gate" and u == 0:
                                    pe.wait_ge(xs_lo, XS_DENSE + 2 * t + n + 1)
                                r = product(bank[(0 if part == "gate" else 2) + t][:, 0:w], run, i,
                                            lambda kk: x_of(t, 4 * n + kk), k, slice(0, w), n == 0,
                                            n == len(chunks) - 1)
                        r.then_inc(w_read, 1)
                        if part == "gate" and n == 0 and u:
                            transposes(u - 1)
                        if part == "down" and n == 0 and u == n_units - 2 and tiles == 1:
                            transposes(n_units - 1)
                    if part == "gate" and u == 0 and first_gate:
                        first_gate()
                    if part == "up" and u == n_units - 1 and last_up:
                        last_up()

            def dense():
                units(dense_run(), dense_stops(), 0, len(DENSE), T,
                      lambda t, k: [xs[:, m, k, t * P:(t + 1) * P] for m in range(2)], lambda u: DENSE[u][1])
                x_transposes(2)

            def router():
                pe.wait_ge(xt_ready, 12)
                pe.wait_ge(in_rows, 48)
                for t in range(T):
                    for k in range(KT):
                        i = mm(bank[0][:, t * NEXP:(t + 1) * NEXP], xT[:, k, t * P:(t + 1) * P], wr[:, k, :],
                               start=k == 0, stop=k == KT - 1)
                i.then_inc(rt_mm, 1)
                pe.wait_ge(rt_mask, 1)
                mm(bank[1][:, 0:8], triu, routed[:, 0, :], start=True, stop=True).then_inc(ga_mm, GA0)
                mm(bank[1][:, 8:16], ones[:, 0:P], routed[:, 0, :], start=True, stop=False)
                mm(bank[1][:, 8:16], triu, routed[:, 1, :], start=False, stop=True).then_inc(st_mm, ST0)
                mm(bank[1][:, 16:24], ones[:, 0:P], routed[:, 0, :], start=True, stop=False)
                mm(bank[1][:, 16:24], ones[:, 0:P], routed[:, 1, :], start=False, stop=True).then_inc(rk_mm, 1)

            def gather(E):
                pe.wait_ge(sel_ok, E * 2 + 1)
                for h in range(2):
                    for kk in range(4):
                        k = 4 * h + kk
                        for t in range(T):
                            i = mm(bank[6 + h][:, kk * P:(kk + 1) * P], x_tok[:, t, k * P:(k + 1) * P],
                                   sel[:, t, :], start=t == 0, stop=t == T - 1)
                    i.then_inc(ga_mm, 1)

            def experts(it, final=False):
                for j in range(TURN):
                    E = it * TURN + j
                    more_to_come = not (final and j == TURN - 1)

                    def choice_transposes():
                        pe.wait_ge(sel_ok, E * 2 + 2)
                        pe.wait_ge(y_add, E * 4 + Y0)
                        for t in range(T):
                            i = tr(bank[1][:, t * P:(t + 1) * P], selc[:, t, :], ident)
                        i.then_inc(st_mm, 1)

                    pe.wait_ge(ga_lo, E * 2 + 2)
                    units(turn_run(it), turn_stops(j), it * (TURN * UNITS) + (len(DENSE) + j * UNITS), UNITS, 1,
                          lambda t, k: [xs[:, m, k, 0:P] for m in range(2)], lambda u: CH,
                          choice_transposes, (lambda: gather(E + 1)) if more_to_come else None)
                    pe.wait_ge(st_ev, E + 1)
                    if more_to_come:
                        pe.wait_ge(ga_lo, E * 2 + 4)
                    for half in range(2):
                        pe.wait_ge((eo_lo, eo_hi)[half], E + 1)
                        for t in range(T):
                            mm(bank[BACK[2 * half + t]][:, :], selT[:, t, :], eo[:, half * CH:(half + 1) * CH],
                               start=True, stop=True).then_inc(back_mm, 1)

            def again():
                pe.wait_ge(more_ok, 1)
                return pe.value_load(more[0:1, 0:1], min_val=0, max_val=1)

            x_transposes(0)
            attention(0)
            dense()
            attention(1)
            router()
            gather(0)
            with pe.Fori(0, TURNS - 1) as i:
                experts(i)
            experts(TURNS - 1, final=True)
            with pe.If(again() > 0):
                pe.wait_ge(y_add, 4 * NEXP + Y0)
                gather(NEXP)
                with pe.Fori(TURNS, 2 * TURNS - 1) as i:
                    experts(i)
                experts(2 * TURNS - 1, final=True)

        @block.scalar
        def _(act):
            copy = nc.scalar.copy

            def fn(out_, in_, f, **kw):
                return nc.scalar.activation(out_, in_, f, **kw)

            def x_evacuate(stage, then=None):
                def evacuate(part, signal, lo_read=None):
                    for t in range(T):
                        for h in range(2):
                            if lo_read is not None:
                                act.wait_ge(xs_lo, lo_read + 2 * t + h + 1)
                            act.wait_ge(xt_mm, 4 * stage + 2 * t + h + 1)
                            copy(part[:, 4 * h:4 * h + 4, t * P:(t + 1) * P],
                                 bank[4 + 2 * t + h][:, :].rearrange("p (k n) -> p k n", k=4)).then_inc(signal, 1)
                        if then and part is not xT and t == 0:
                            then()

                if stage < 3:
                    evacuate(xs[:, 0], xs_hi)
                if stage != 1:
                    evacuate(xT, xt_ready, XS_IN[stage // 2] if stage < 3 else None)

            def rsqrt_start(l, step, v, r):
                act.wait_ge(var_ok[l], step + 1)
                fn(r, v, ACT.Ln, bias=eps).then_inc(ln_v[l], 1)
                act.wait_ge(ln_v[l], step + 1)
                fn(r, r, ACT.Exp, scale=-0.5).then_inc(rs_ok[l], 1)

            def norm_rsqrt(l, which):
                for t in range(T):
                    rsqrt_start(l, 2 + T * which + t, mv[:, t, 1:2], rs[:, t:t + 1])

            def split_hi(run, i):
                run.wait_full(act, i)
                if run.split0 + i >= NSPLIT:
                    act.wait_ge(w_read, run.count(i - NSPLIT + 1))
                k, n = run.shapes[i % len(run.shapes)]
                copy(run.parts(i)[0], run.raw(i)[:, 0:k * n].rearrange("p (k n) -> p k n", k=k)).then_inc(hi_ok, 1)

            def q_or_k(l, first):
                for j in range(first, first + 2):
                    act.wait_ge(w_read, in_run(l).count(N_IN - 3 + j))
                    copy(pre[:, 2 * j:2 * j + 2, CONV - 1:], bank[5 + j % 2][:, :].rearrange("p (f s) -> p f s", f=2)
                         ).then_inc(qk_ev[l], 1)
                    if j == 0:
                        split_hi(in_run(l), 9)

            def attention(l):
                run = in_run(l)
                for i in (2, 3):
                    split_hi(run, i)
                for g in range(6):
                    c, t = divmod(g, 2)
                    cols = slice(A_GROUPS[c], A_GROUPS[c + 1])
                    if t == 0:
                        act.wait_ge(proj_t0[l], c + 1)
                    else:
                        act.wait_ge(w_read, run.count(2 * c + 2))
                    copy(att[:, t, cols], bank[(0, 1, 2, 3, 4, 7)[g]][:, 0:cols.stop - cols.start]
                         ).then_inc(proj_ev[l], 1)
                    if g == 1:
                        split_hi(run, 4)
                        split_hi(run, 5)
                    if g == 3:
                        split_hi(run, 6)
                        act.wait_ge(gate_mm[l], 1)
                        act.wait_ge(in_const, 32)
                        fn(gate[0:ML_H, 0, :], bank[6][0:ML_H, 0:SEQ], ACT.Identity,
                           bias=feat[0:ML_H, l, PC_I:PC_I + 1]).then_inc(gate_ev[l], 1)
                        fn(gate[0:ML_H, 1, :], bank[6][0:ML_H, SEQ:2 * SEQ], ACT.Identity,
                           bias=feat[0:ML_H, l, PC_F:PC_F + 1]).then_inc(gate_ev[l], 1)
                        act.wait_ge(gate_ev[l], 2)
                        fn(gate[0:ML_H, 2, :], gate[0:ML_H, 1, :], ACT.Abs).then_inc(gate_ev[l], 1)
                        act.wait_ge(gate_ev[l], 3)
                        fn(gate[0:ML_H, 2, :], gate[0:ML_H, 2, :], ACT.Exp, scale=-1.0).then_inc(gate_ev[l], 1)
                        act.wait_ge(gate_ev[l], 4)
                        fn(gate[0:ML_H, 2, :], gate[0:ML_H, 2, :], ACT.Ln, bias=cst[0:ML_H, K_ONES:K_ONES + 1]
                           ).then_inc(gate_ev[l], 1)
                        split_hi(run, 7)
                rsqrt_start(l, 0, var[:, 0:T], rs[:, 0:T])
                split_hi(run, 8)
                q_or_k(l, 0)
                act.wait_ge(itr_mm[l], 1)
                copy(iqT, bank[0][:, :].rearrange("p (f s) -> p f s", f=2)).then_inc(itr_ev[l], 1)
                act.wait_ge(itr_mm[l], 2)
                copy(ikT, bank[1][:, 0:SEQ]).then_inc(itr_ev[l], 1)
                q_or_k(l, 2)
                for h in range(IDX_H):
                    act.wait_ge(idx_mm[l], h + 1)
                    if h >= 2:
                        act.wait_ge(idx_used[l], h - 1)
                    fn(relu[:, h % 2, :], bank[h][:, 0:384], ACT.Relu, scale=AT_D ** -0.5 * IDX_H ** -0.5
                       ).then_inc(idx_ev[l], 1)
                for b in range(3):
                    act.wait_ge(atr_mm[l], b + 1)
                    dst = aqT[:, 2 * b:2 * b + 2] if b < 2 else akT
                    copy(dst, bank[4 + b][:, :].rearrange("p (f s) -> p f s", f=2)).then_inc(atr_ev[l], 1)
                act.wait_ge(gtr_mm[l], 1)
                copy(gT, bank[7][:, 0:T * ML_H].rearrange("p (t h) -> p t h", t=T)).then_inc(gtr_ev[l], 1)
                fn(emT, bank[7][:, T * ML_H:2 * T * ML_H].rearrange("p (t h) -> p t h", t=T), ACT.Exp, scale=-1.0
                   ).then_inc(gtr_ev[l], 1)
                for half in range(2):
                    act.wait_ge(conv_y[l], half + 1)
                    fn(qk[:, half * ML_H:(half + 1) * ML_H, :], qk[:, half * ML_H:(half + 1) * ML_H, :], ACT.Silu
                       ).then_inc(conv_ok[l], 1)
                for t in range(T):
                    act.wait_ge(vo_mm[l], t + 1)
                    copy(v_tok[:, t], bank[t][:, :]).then_inc(v_ev[l], 1)
                for h in range(ML_H):
                    act.wait_ge(ml_e[l], h + 1)
                    fn(mld[:, h, :], mld[:, h, :], ACT.Exp).then_inc(ml_d[l], 1)
                split_hi(out_run(l), 0)

                def mix_hi(g):
                    t, half, b = MIX_TR[g]
                    act.wait_ge(mtr_mm[l], g + 1)
                    copy(xs[:, 0, 4 * half:4 * half + 4, t * P:(t + 1) * P],
                         bank[b][:, :].rearrange("p (k n) -> p k n", k=4)).then_inc(xs_hi, 1)

                for h in range(AT_H):
                    if h == 2:
                        rsqrt_start(l, 1, var[:, 0:T * ML_H], rs[:, 0:T * ML_H])
                        for t in range(T):
                            act.wait_ge(vo_mm[l], T + t + 1)
                            fn(og[:, t, :], bank[2 + t][:, :], ACT.Sigmoid).then_inc(o_ev[l], 1)
                    act.wait_ge(sc_max[l], h + 1)
                    for t in range(T):
                        o = slice(0, P) if t == 0 else slice(P, 3 * P)
                        i = fn(probs[:, h % 3, o], probs[:, h % 3, o], ACT.Exp, scale=AT_D ** -0.5,
                               bias=nmax[:, h % 3, t:t + 1], accum_out=rsum[:, t, h:h + 1])
                    i.then_inc(sc_exp[l], 1)
                    if h in EARLY_SPLIT:
                        split_hi(out_run(l), 1 + EARLY_SPLIT.index(h))
                    if h >= 6:
                        mix_hi(h - 6)
                for g in range(2, 4):
                    mix_hi(g)
                split_hi(out_run(l), 3)
                for i in range(2):
                    split_hi(turn_run(0) if l else dense_run(), i)
                norm_rsqrt(l, 0)
                x_evacuate(2 * l + 1)

            def units(run, stops, base, n_units, tiles, width, last, first_gate=None, last_up=None):
                def hidden(u):
                    act.wait_ge(ht_mm, base + (u + 1))
                    w = width(u) // P
                    copy(hidden_split(u, tiles)[:, :, 0, 0:w, :], hidden_banks(tiles, w)).then_inc(ht_hi, 1)

                for part, u, chunks in stops:
                    if part == "down" and u == n_units - 1 and tiles == T:
                        hidden(u)
                    for n, i in enumerate(chunks):
                        if i + 2 < last:
                            split_hi(run, i + 2)
                        if part == "gate" and n == 0 and u:
                            hidden(u - 1)
                        if part == "down" and n == 0 and u == n_units - 2 and tiles == 1:
                            hidden(n_units - 1)
                    if part == "gate":
                        act.wait_ge(w_read, run.count(chunks[-1] + 1))
                        w = width(u)
                        for t in range(tiles):
                            f = fn(silu[:, t, 0:w], bank[t][:, 0:w], ACT.Silu)
                        f.then_inc(g_silu, 1)
                    if part == "gate" and u == 0 and first_gate:
                        first_gate()
                    if part == "up" and u == n_units - 1 and last_up:
                        last_up()

            def dense():
                run = dense_run()
                units(run, dense_stops(), 0, len(DENSE), T, lambda u: DENSE[u][1], N_DENSE)
                for i in range(2):
                    split_hi(in_run(1), i)
                norm_rsqrt(0, 1)
                x_evacuate(2)

            def gathered_hi(E):
                for h in range(2):
                    act.wait_ge(ga_mm, E * 2 + (GA0 + h + 1))
                    copy(xs[:, 0, 4 * h:4 * h + 4, 0:P], bank[6 + h][:, :].rearrange("p (k n) -> p k n", k=4)
                         ).then_inc(ga_hi, 1)

            def experts(it, final=False):
                run = turn_run(it)
                for j in range(TURN):
                    E = it * TURN + j
                    more_to_come = not (final and j == TURN - 1)

                    def choice_transposed():
                        act.wait_ge(st_mm, E + (ST0 + 1))
                        copy(selT, bank[1][:, 0:SEQ].rearrange("p (t n) -> p t n", t=T)).then_inc(st_ev, 1)

                    units(run, turn_stops(j), it * (TURN * UNITS) + (len(DENSE) + j * UNITS), UNITS, 1,
                          lambda u: CH, PER_TURN if final else 2 * PER_TURN,
                          choice_transposed, (lambda: gathered_hi(E + 1)) if more_to_come else None)
                    act.wait_ge(w_read, run.count((j + 1) * PER_TURN // TURN))
                    copy(eo[:, 0:CH], bank[4][:, :]).then_inc(eo_lo, 1)

            x_evacuate(0, lambda: split_hi(in_run(0), 0))
            split_hi(in_run(0), 1)
            attention(0)
            dense()
            attention(1)
            act.wait_ge(rt_diff, 1)
            fn(g2[:, :, 0:1], g2[:, :, 0:1], ACT.Exp).then_inc(rt_exp, 1)
            gathered_hi(0)
            with act.Fori(0, TURNS - 1) as i:
                experts(i)
            experts(TURNS - 1, final=True)
            act.wait_ge(more_ok, 1)
            again = act.value_load(more[0:1, 0:1], min_val=0, max_val=1)
            with act.If(again > 0):
                for i in range(2):
                    split_hi(turn_run(TURNS), i)
                gathered_hi(NEXP)
                with act.Fori(TURNS, 2 * TURNS - 1) as i:
                    experts(i)
                experts(2 * TURNS - 1, final=True)
            norm_rsqrt(1, 1)

        @block.vector
        def _(dve):
            ts, tt, stt = nc.vector.tensor_scalar, nc.vector.tensor_tensor, nc.vector.scalar_tensor_tensor
            steps = [0]

            def step(i):
                i.then_inc(dstep, 1)
                steps[0] += 1
                return steps[0]

            def after(n):
                dve.wait_ge(dstep, n)

            def link(i):
                after(step(i))

            def rsqrt_finish(l, n_step, v, r, a, b):
                dve.wait_ge(rs_ok[l], n_step + 1)
                link(stt(a, v, eps, r, ALU.add, ALU.mult))
                link(stt(b, a, -0.5, r, ALU.mult, ALU.mult))
                link(stt(r, b, 1.5, r, ALU.add, ALU.mult))

            def layer_norm(l, which, src, sums=None):
                for t in range(T):
                    s = [step(sums(t, h)) if sums else None for h in range(2)]
                    for h in range(2):
                        if sums:
                            after(s[h])
                        s[h] = step(nc.vector.bn_stats(stats[:, t, h, :], src[:, t, h * CH:(h + 1) * CH]))
                    after(s[1])
                    nc.vector.bn_aggr(mv[:, t, :], stats[:, t]).then_inc(var_ok[l], 1)
                dve.wait_ge(in_ln, 16 * (2 * l + which + 1))
                for t in range(T):
                    c = slice(t, t + 1)
                    dve.wait_ge(var_ok[l], 3 + T * which + t)
                    rsqrt_finish(l, 2 + T * which + t, mv[:, t, 1:2], rs[:, c], nt[:, 0, c], nt[:, 1, c])
                    link(stt(x_tok[:, t], src[:, t], mv[:, t, 0:1], ln[:, 0], ALU.subtract, ALU.mult))
                    stt(x_tok[:, t], x_tok[:, t], rs[:, c], ln[:, 1], ALU.mult, ALU.add).then_inc(x_ready, 1)
                dve.wait_ge(x_ready, (2 * l + which + 1) * T)

            def split_lo(run, i):
                dve.wait_ge(hi_ok, run.count(i + 1))
                k, n = run.shapes[i % len(run.shapes)]
                hi, lo = run.parts(i)
                tt(lo, run.raw(i)[:, 0:k * n].rearrange("p (k n) -> p k n", k=k), hi.bitcast(F32), ALU.subtract
                   ).then_inc(lo_ok, 1)

            def x_lo(base, then=None):
                for g in range(4):
                    if g == 2 and then:
                        then()
                    t, h = divmod(g, 2)
                    dve.wait_ge(xs_hi, base + g + 1)
                    k, n = slice(4 * h, 4 * h + 4), slice(t * P, (t + 1) * P)
                    tt(xs[:, 1, k, n], bank[4 + g][:, :].rearrange("p (k n) -> p k n", k=4),
                       xs[:, 0, k, n].bitcast(F32), ALU.subtract).then_inc(xs_lo, 1)

            def mix_lo(l, g):
                t, half, b = MIX_TR[g]
                dve.wait_ge(xs_hi, XS_MIX[l] + g + 1)
                k, n = slice(4 * half, 4 * half + 4), slice(t * P, (t + 1) * P)
                tt(xs[:, 1, k, n], bank[b][:, :].rearrange("p (k n) -> p k n", k=4),
                   xs[:, 0, k, n].bitcast(F32), ALU.subtract).then_inc(xs_lo, 1)

            def rotate(l, h0, n):
                heads = att[:, :, A_Q:A_IW].rearrange("p t (h n) -> p t h n", n=AT_D)[:, :, h0:h0 + n]
                x1, x2 = heads[:, :, :, 0:ROT], heads[:, :, :, ROT:2 * ROT]
                table = [cst[:, a:a + T * ROT].rearrange("p (t r) -> p t r", t=T).unsqueeze(2)
                         .to_broadcast([P, T, n, ROT]) for a in (K_COS, K_SIN)]
                r = [b[:, :, 0:n, :] for b in rope]
                for i, (a, b) in enumerate(((x1, 0), (x2, 1), (x2, 0), (x1, 1))):
                    s = step(tt(r[i], a, table[b], ALU.mult))
                after(s)
                step(tt(x1, r[0], r[1], ALU.subtract))
                after(steps[0])
                tt(x2, r[2], r[3], ALU.add).then_inc(roped[l], 1)
                dve.wait_ge(roped[l], 1 if h0 else 2)

            def conv(l, half):
                dve.wait_ge(qk_ev[l], 2 * half + 2)
                f0 = half * ML_H
                for j in range(CONV):
                    for f in range(f0, f0 + ML_H):
                        w = feat[:, l, PC_W + f * CONV + j:PC_W + f * CONV + j + 1]
                        if j == 0:
                            s = step(ts(qk[:, f], pre[:, f, 0:SEQ], w, feat[:, l, PC_B + f:PC_B + f + 1],
                                        ALU.mult, ALU.add))
                        elif j < CONV - 1 or f < f0 + ML_H - 1:
                            after(s - ML_H + 1)
                            s = step(stt(qk[:, f], pre[:, f, j:j + SEQ], w, qk[:, f], ALU.mult, ALU.add))
                        else:
                            after(s)
                            stt(qk[:, f], pre[:, f, j:j + SEQ], w, qk[:, f], ALU.mult, ALU.add
                                ).then_inc(conv_y[l], 1)

            def index_norm(l):
                ik = [att[:, t, A_IK:A_IW] for t in range(T)]
                for t in range(T):
                    s = step(nc.vector.bn_stats(stats[:, t, 0, :], ik[t]))
                after(s)
                for t in range(T):
                    s = step(nc.vector.bn_aggr(mv[:, t, :], stats[:, t, 0]))
                after(s)
                nc.vector.tensor_copy(var[:, 0:T], mv[:, 0:T, 1]).then_inc(var_ok[l], 1)
                dve.wait_ge(var_ok[l], 1)
                rsqrt_finish(l, 0, var[:, 0:T], rs[:, 0:T], nt[:, 0, 0:T], nt[:, 1, 0:T])
                dve.wait_ge(in_rows, 48)
                for t in range(T):
                    link(ts(ik[t], ik[t], mv[:, t, 0:1], rs[:, t:t + 1], ALU.subtract, ALU.mult))
                    link(tt(ik[t], ik[t], rows[:, l, AR_IG:AR_IB], ALU.mult))
                    link(tt(ik[t], ik[t], rows[:, l, AR_IB:AR_END], ALU.add))

            def gates(l):
                r = [gate[0:ML_H, i, :] for i in range(4)]
                dve.wait_ge(gate_ev[l], 5)
                link(stt(r[2], r[1], 0.0, r[2], ALU.min, ALU.subtract))
                scan = nc.vector.tensor_tensor_scan
                link(scan(r[3], ones[0:ML_H], r[2], 0.0, ALU.mult, ALU.add))
                link(tt(r[0], r[0], r[3], ALU.subtract))
                link(scan(r[1], ones[0:ML_H], r[0], 0.0, ALU.mult, ALU.max))
                tt(r[2], r[3], r[1], ALU.add).then_inc(gate_row[l], 1)

            def choose(l):
                part = [slice(0, P), slice(P, 3 * P)]
                for h in range(IDX_H):
                    dve.wait_ge(idx_ev[l], h + 1)
                    for t in range(T):
                        w = att[:, t, A_IW + h:A_IW + h + 1]
                        o, r = iscore[:, part[t]], relu[:, h % 2, part[t]]
                        if h:
                            dve.wait_ge(idx_used[l], h)
                            i = stt(o, r, w, o, ALU.mult, ALU.add)
                        else:
                            i = ts(o, r, w, None, ALU.mult)
                    i.then_inc(idx_used[l], 1)
                dve.wait_ge(idx_used[l], IDX_H)
                link(tt(iscore, iscore, causal, ALU.add))
                for r in range(TOPK // 8):
                    src = iscore if r == 0 else left
                    for t in range(T):
                        if r:
                            after(steps[0] - 1)
                        step(nc.vector.max(top8[:, t], src[:, part[t]]))
                    for t in range(T):
                        after(steps[0] - 1)
                        step(nc.vector.match_replace(left[:, part[t]], top8[:, t], src[:, part[t]], TAKEN))
                after(steps[0])
                link(ts(choice, left, TAKEN, NEG, ALU.not_equal, ALU.mult))
                link(tt(choice, choice, causal, ALU.add))

            def mlstm(l):
                dve.wait_ge(gtr_ev[l], 2)
                for h in range(ML_H):
                    if h % 2 == 0:
                        dve.wait_ge(mrow_mm[l], h // 2 + 1)
                    m = bank[4 + h // 2][:, (h % 2) * SEQ:(h % 2 + 1) * SEQ]
                    stt(mld[:, h, 0:SEQ], causalT[:, 0:SEQ], gT[:, 0, h:h + 1], m, ALU.add, ALU.subtract)
                    stt(mld[:, h, SEQ:SEQ + P], causalT[:, SEQ:SEQ + P], gT[:, 1, h:h + 1], m[:, P:SEQ],
                        ALU.add, ALU.subtract).then_inc(ml_e[l], 1)
                for h in range(ML_H):
                    dve.wait_ge(mls_mm[l], h + 1)
                    dve.wait_ge(ml_d[l], h + 1)
                    stt(mld[:, h], bank[ML_BANK[h]][:, 0:384], float(ML_D) ** -0.5, mld[:, h], ALU.mult, ALU.mult
                        ).then_inc(ml_p[l], 1)

            def numerators(l):
                return [[bank[4 + t][:, h * ML_D:(h + 1) * ML_D] for h in range(ML_H)] for t in range(T)]

            def mlstm_norm_start(l):
                dve.wait_ge(num_mm[l], ML_H)
                num = numerators(l)
                den = bank[6][:, 0:T * ML_H].rearrange("p (t h) -> p t h", t=T)
                s = step(ts(rden2, den, -1.0, None, ALU.mult))
                for i in range(T * ML_H):
                    s2 = step(nc.vector.bn_stats(stats[:, i, 0, :], num[i // ML_H][i % ML_H]))
                after(s)
                s = step(tt(rden, den, rden2, ALU.max))
                after(s2)
                for i in range(T * ML_H):
                    s2 = step(nc.vector.bn_aggr(mv[:, i, :], stats[:, i, 0]))
                after(s)
                link(tt(rden, rden, emT, ALU.max))
                link(nc.vector.reciprocal(rden, rden))
                link(tt(rden2, rden, rden, ALU.mult))
                tt(var[:, 0:T * ML_H], mv[:, :, 1], rden2.rearrange("p t h -> p (t h)"), ALU.mult
                   ).then_inc(var_ok[l], 1)

            def mlstm_norm_end(l):
                num = numerators(l)
                dve.wait_ge(var_ok[l], 2)
                rsqrt_finish(l, 1, var[:, :], rs[:, :], nt[:, 0, :], nt[:, 1, :])
                link(tt(rs[:, :], rs[:, :], rden.rearrange("p t h -> p (t h)"), ALU.mult))
                for t in range(T):
                    for h in range(ML_H):
                        i = t * ML_H + h
                        s = step(ts(mix[:, t, h * ML_D:(h + 1) * ML_D], num[t][h], mv[:, i, 0:1], rs[:, i:i + 1],
                                    ALU.subtract, ALU.mult))
                dve.wait_ge(og_ok[l], T)
                after(s)
                step(tt(mix[:, 0, 0:ML_W], mix[:, 0, 0:ML_W], og[:, 0], ALU.mult))
                tt(mix[:, 1, 0:ML_W], mix[:, 1, 0:ML_W], og[:, 1], ALU.mult).then_inc(mix_ml[l], 1)

            def attention(l):
                run = in_run(l)
                x_lo(XS_IN[l], None if l else lambda: split_lo(run, 0))
                for i in range(1, 8):
                    split_lo(run, i)
                link(nc.vector.memset(pre[:, :, 0:CONV - 1], 0.0))
                dve.wait_ge(proj_ev[l], 6)
                index_norm(l)
                rotate(l, (A_IQ - A_Q) // AT_D, IDX_H + 1)
                split_lo(run, 8)
                gates(l)
                split_lo(run, 9)
                rotate(l, 0, AT_H + AT_KV)
                conv(l, 0)
                choose(l)
                conv(l, 1)
                mlstm(l)

                def masked(h):
                    b = h % 3
                    dve.wait_ge(sc_mm[l], h + 1)
                    if h >= 3:
                        dve.wait_ge(ptr_mm[l], h - 2)
                    for t in range(T):
                        o = slice(0, P) if t == 0 else slice(P, 3 * P)
                        s = step(nc.vector.tensor_tensor_reduce(
                            out=probs[:, b, o], in0=bank[h % 3][:, o], in1=choice[:, o], scale=1.0, scalar=TAKEN,
                            op0=ALU.add, op1=ALU.max, accum_out=rmax[:, b, t:t + 1]))
                    after(s)
                    ts(nmax[:, b], rmax[:, b], -(AT_D ** -0.5), None, ALU.mult).then_inc(sc_max[l], 1)

                def transposed(h):
                    dve.wait_ge(ptr_mm[l], h + 1)
                    if h >= 3:
                        dve.wait_ge(pv_mm[l], h - 2)
                    nc.vector.tensor_copy(probsT[:, h % 3], bank[PT_BANK[h % 2]][:, 0:384]).then_inc(pt_ok[l], 1)

                split_lo(out_run(l), 0)
                for h in range(AT_H + 2):
                    if h == 2:
                        mlstm_norm_start(l)
                        mlstm_norm_end(l)
                    if h < AT_H:
                        masked(h)
                    if h >= 2:
                        transposed(h - 2)
                    if h in EARLY_SPLIT:
                        split_lo(out_run(l), 1 + EARLY_SPLIT.index(h))
                    if h in (6, 8):
                        mix_lo(l, (h - 6) // 2)
                dve.wait_ge(pv_mm[l], AT_H)
                dve.wait_ge(sc_exp[l], AT_H)
                link(nc.vector.reciprocal(rsum, rsum))
                for t in range(T):
                    i = tt(mix[:, t, ML_W:].rearrange("p (h n) -> p h n", h=AT_H),
                           bank[4 + t][:, :].rearrange("p (h n) -> p h n", h=AT_H),
                           rsum[:, t].unsqueeze(2).to_broadcast([P, AT_H, AT_D]), ALU.mult)
                    if t == 0:
                        step(i)
                i.then_inc(mix_at[l], 1)
                for g in range(2, 4):
                    mix_lo(l, g)
                split_lo(out_run(l), 3)
                split_lo(turn_run(0) if l else dense_run(), 0)

                def residual(t, c):
                    g = 2 * t + c
                    if g < 3:
                        dve.wait_ge(op_mm[l], g + 1)
                    else:
                        dve.wait_ge(w_read, out_run(l).count(4))
                    half = x_tok[:, t, c * CH:(c + 1) * CH]
                    return stt(half, half, ALPHA, bank[g][:, :], ALU.mult, ALU.add)

                layer_norm(l, 0, x_tok, residual)
                if l:
                    split_lo(turn_run(0), 1)

            def units(run, stops, base, n_units, tiles, width, last, second_gate=None, last_up=None):
                def hidden(u):
                    dve.wait_ge(ht_hi, base + (u + 1))
                    w = width(u) // P
                    h = hidden_split(u, tiles)
                    tt(h[:, :, 1, 0:w, :], hidden_banks(tiles, w), h[:, :, 0, 0:w, :].bitcast(F32), ALU.subtract
                       ).then_inc(ht_lo, 1)

                for part, u, chunks in stops:
                    if part == "down" and u == n_units - 1 and tiles == T:
                        hidden(u)
                    for n, i in enumerate(chunks):
                        if i + 2 < last:
                            split_lo(run, i + 2)
                        if part == "gate" and n == 0 and u:
                            hidden(u - 1)
                        if part == "down" and n == 0 and u == n_units - 2 and tiles == 1:
                            hidden(n_units - 1)
                    if part == "up":
                        dve.wait_ge(g_silu, base + (u + 1))
                        dve.wait_ge(w_read, run.count(chunks[-1] + 1))
                        w = width(u)
                        for t in range(tiles):
                            i = tt(hid[:, t, 0:w], silu[:, t, 0:w], bank[2 + t][:, 0:w], ALU.mult)
                        i.then_inc(h_ok, 1)
                    if part == "gate" and u == 1 and second_gate:
                        second_gate()
                    if part == "up" and u == n_units - 1 and last_up:
                        last_up()

            def dense():
                x_lo(XS_DENSE)
                run = dense_run()
                split_lo(run, 1)
                units(run, dense_stops(), 0, len(DENSE), T, lambda u: DENSE[u][1], N_DENSE)
                split_lo(in_run(1), 0)

                def residual(t, c):
                    if c == 0:
                        dve.wait_ge(*((tile0_mm, 1), (w_read, run.count(N_DENSE)))[t])
                    half = x_tok[:, t, c * CH:(c + 1) * CH]
                    return stt(half, half, ALPHA, bank[4 + 2 * t + c][:, :], ALU.mult, ALU.add)

                layer_norm(0, 1, x_tok, residual)

            def route():
                dve.wait_ge(rt_mm, 1)
                for t in range(T):
                    s = step(tt(lg[:, t], bank[0][:, t * NEXP:(t + 1) * NEXP], br[:], ALU.add))
                after(s)
                for t in range(T):
                    s = step(nc.vector.max(m8[:, t], lg[:, t]))
                after(s)
                tt(g2[:, :, 0:1], m8[:, :, 1:2], m8[:, :, 0:1], ALU.subtract).then_inc(rt_diff, 1)
                for t in range(T):
                    s = step(nc.vector.max_index(i8[:, t], m8[:, t], lg[:, t]))
                after(s)
                link(nc.vector.tensor_copy(i8f[:, :, :], i8[:, :, 0:2]))
                for t in range(T):
                    for j in range(2):
                        s = step(ts(oh[:, t, j], iota[:, 0:NEXP], i8f[:, t, j:j + 1], None, ALU.is_equal))
                after(s)
                tt(routed[:, :, :], oh[:, :, 0], oh[:, :, 1], ALU.add).then_inc(rt_mask, 1)
                dve.wait_ge(rt_exp, 1)
                link(ts(g2[:, :, 1:2], g2[:, :, 0:1], 1.0, None, ALU.add))
                link(nc.vector.reciprocal(g2[:, :, 1:2], g2[:, :, 1:2]))
                link(tt(g2[:, :, 2:3], g2[:, :, 0:1], g2[:, :, 1:2], ALU.mult))
                for t in range(T):
                    s = step(ts(comb[:, t], oh[:, t, 0], g2[:, t, 1:2], None, ALU.mult))
                after(s)
                for t in range(T):
                    s = step(stt(comb[:, t], oh[:, t, 1], g2[:, t, 2:3], comb[:, t], ALU.mult, ALU.add))
                dve.wait_ge(rk_mm, 1)
                after(s)
                r = rank[:, :, :]
                link(stt(r, bank[1][:, 0:16].rearrange("p (t e) -> p t e", t=T), 1.0, routed[:, :, :],
                         ALU.add, ALU.mult))
                link(ts(r, r, -1.0, None, ALU.add))
                link(nc.vector.reduce_max(cmax[:], bank[1][:, 16:24], axis=AX.X))
                ts(more[:], cmax[:], float(P), None, ALU.is_gt).then_inc(more_ok, 1)

            def slots_of(E, e):
                dve.wait_ge(ga_mm, E * 2 + GA0)
                for t in range(T):
                    i = ts(sel[:, t], iota, rank[:, t, e], None, ALU.is_equal)
                i.then_inc(sel_ok, 1)
                dve.wait_ge(st_mm, E + ST0)
                for t in range(T):
                    i = ts(selc[:, t], iota, rank[:, t, e], comb[:, t, e], ALU.is_equal, ALU.mult)
                i.then_inc(sel_ok, 1)

            def gathered_lo(E):
                for h in range(2):
                    dve.wait_ge(ga_hi, E * 2 + (h + 1))
                    k = slice(4 * h, 4 * h + 4)
                    tt(xs[:, 1, k, 0:P], bank[6 + h][:, :].rearrange("p (k n) -> p k n", k=4),
                       xs[:, 0, k, 0:P].bitcast(F32), ALU.subtract).then_inc(ga_lo, 1)

            def experts(it, pair, final=False):
                run = turn_run(it)
                for j in range(TURN):
                    E = it * TURN + j
                    more_to_come = not (final and j == TURN - 1)
                    units(run, turn_stops(j), it * (TURN * UNITS) + (len(DENSE) + j * UNITS), UNITS, 1,
                          lambda u: CH, PER_TURN if final else 2 * PER_TURN,
                          (lambda: slots_of(E + 1, bass.ds(pair * TURN + (j + 1), 1))) if more_to_come else None,
                          (lambda: gathered_lo(E + 1)) if more_to_come else None)
                    dve.wait_ge(w_read, run.count((j + 1) * PER_TURN // TURN))
                    nc.vector.tensor_copy(eo[:, CH:D], bank[5][:, :]).then_inc(eo_hi, 1)
                    dve.wait_ge(y_add, E * 4 + Y0)
                    for half in range(2):
                        for t in range(T):
                            g = 2 * half + t
                            dve.wait_ge(back_mm, E * 4 + (g + 1))
                            part = y[:, t, half * CH:(half + 1) * CH]
                            tt(part, part, bank[BACK[g]][:, :], ALU.add).then_inc(y_add, 1)

            attention(0)
            dense()
            attention(1)
            route()
            slots_of(0, slice(0, 1))
            for t in range(T):
                ts(y[:, t], x_tok[:, t], ALPHA, None, ALU.mult).then_inc(y_add, 1)
            gathered_lo(0)
            with dve.Fori(0, TURNS - 1) as i:
                experts(i, i)
            experts(TURNS - 1, TURNS - 1, final=True)
            dve.wait_ge(y_add, 4 * NEXP + Y0)
            again = dve.value_load(more[0:1, 0:1], min_val=0, max_val=1)
            with dve.If(again > 0):
                ts(rank[:, :, :], rank[:, :, :], -float(P), None, ALU.add).then_inc(rank_ok, 1)
                dve.wait_ge(rank_ok, 1)
                slots_of(NEXP, slice(0, 1))
                for i in range(2):
                    split_lo(turn_run(TURNS), i)
                gathered_lo(NEXP)
                with dve.Fori(0, TURNS - 1) as i:
                    experts(i + TURNS, i)
                experts(2 * TURNS - 1, TURNS - 1, final=True)
                dve.wait_ge(y_add, 8 * NEXP + Y0)
            layer_norm(1, 1, y)


_OUTS = [((1, SEQ, D), "float32")]


def kernel(x, w_in, ml_conv_w, ml_conv_b, ml_i_b, ml_f_b, ml_norm_g, idx_k_norm_g, idx_k_norm_b, w_out,
           ln1_g, ln1_b, ln2_g, ln2_b, ffn_w_gate, ffn_w_up, ffn_w_down,
           moe_w_router, moe_b_router, moe_w_gate, moe_w_up, moe_w_down):
    import concourse.bacc as bacc
    from concourse.bass_utils import run_bass_kernel_spmd

    a = {k: np.asarray(v) for k, v in locals().items() if hasattr(v, "shape")}
    feat = np.zeros((DEPTH, P, PC_END), np.float32)
    feat[:, :, PC_W:PC_B] = a["ml_conv_w"].reshape(DEPTH, CONV, 2 * ML_H, P).transpose(0, 3, 2, 1).reshape(DEPTH, P, -1)
    feat[:, :, PC_B:PC_I] = a["ml_conv_b"].reshape(DEPTH, 2 * ML_H, P).transpose(0, 2, 1)
    feat[:, 0:ML_H, PC_I] = a["ml_i_b"]
    feat[:, 0:ML_H, PC_F] = a["ml_f_b"]
    arrays = {
        "x": a["x"], "w_in": a["w_in"], "w_out": a["w_out"],
        "ffn_gate": a["ffn_w_gate"], "ffn_up": a["ffn_w_up"], "ffn_down": a["ffn_w_down"],
        "w_router": a["moe_w_router"], "b_router": a["moe_b_router"],
        "moe_gate": a["moe_w_gate"], "moe_up": a["moe_w_up"], "moe_down": a["moe_w_down"],
        "feat_params": feat,
        "row_params": np.concatenate([a["ml_norm_g"], a["idx_k_norm_g"], a["idx_k_norm_b"]], axis=1),
        "ln_params": np.stack([a["ln1_g"], a["ln1_b"], a["ln2_g"], a["ln2_b"]], axis=1),
        "consts": shape_constants(),
    }
    arrays = {k: np.ascontiguousarray(v) for k, v in arrays.items()}
    nc = bacc.Bacc("TRN2", target_bir_lowering=False, num_devices=1)
    aps = {k: nc.dram_tensor(k, v.shape, mybir.dt.from_np(v.dtype), kind="ExternalInput").ap()
           for k, v in arrays.items()}
    shape, dtype = _OUTS[0]
    out = nc.dram_tensor("out", shape, mybir.dt.from_np(np.dtype(dtype)), kind="ExternalOutput").ap()
    build_program(nc, **aps, out=out)
    r = run_bass_kernel_spmd(nc, [arrays], core_ids=[0])
    return r.results[0]["out"]
```
